# Optimizing a Trainium2 kernel written in Bass

```python
import math
import jax, jax.numpy as jnp
from jax import lax
import numpy as np

D_MODEL = 1024
BATCH = 1
SEQ = 256
DEPTH = 1

HEAD_DIM = 64
A_GROUPS = 4
A_WIDTH = A_GROUPS * HEAD_DIM
CHUNK = 128
B_HEADS = 6
B_WIDTH = B_HEADS * HEAD_DIM
DIL_PAIRS = ((128, 1), (512, 4), (2048, 16))
C_HEADS_PER_GROUP = 2
C_GROUPS = len(DIL_PAIRS)
C_HEADS = C_GROUPS * C_HEADS_PER_GROUP
C_WIDTH = C_HEADS * HEAD_DIM
C_DILATIONS = tuple(d for (w, d) in DIL_PAIRS for _ in range(C_HEADS_PER_GROUP))
N_OFFSETS = DIL_PAIRS[0][0] // DIL_PAIRS[0][1] + 1
MIX_WIDTH = A_WIDTH + B_WIDTH + C_WIDTH
IN_WIDTH = 2 * A_WIDTH + 3 * B_WIDTH + 3 * C_WIDTH
Q_BLOCK = 128
D_FF = 2816
CONV_WIDTH = 3
ROPE_THETA = 10000.0
EPS = 1e-6
N_MOD = 6


def _rmsnorm(x, g):
    x32 = x.astype(jnp.float32)
    y = x32 * lax.rsqrt(jnp.mean(x32 * x32, axis=-1, keepdims=True) + EPS)
    return (y * g.astype(jnp.float32)).astype(x.dtype)

def _rope_tables(positions):
    inv_freq = ROPE_THETA ** (-jnp.arange(0, HEAD_DIM, 2, dtype=jnp.float32) / HEAD_DIM)
    ang = positions.astype(jnp.float32)[..., None] * inv_freq
    return jnp.cos(ang)[:, :, None, :], jnp.sin(ang)[:, :, None, :]

def _rope(x, cos, sin):
    x32 = x.astype(jnp.float32)
    x1, x2 = jnp.split(x32, 2, axis=-1)
    return jnp.concatenate([x1 * cos - x2 * sin, x2 * cos + x1 * sin], axis=-1).astype(x.dtype)

def _spatial_gating(u, v, g_sgu, w_sp, b_sp):
    bsz, seq, _ = u.shape
    n_chunks = seq // CHUNK
    u = jax.nn.gelu(u)
    v = jax.nn.gelu(v).reshape(bsz, n_chunks, CHUNK, A_GROUPS, HEAD_DIM)
    v = _rmsnorm(v, g_sgu.reshape(A_GROUPS, HEAD_DIM))
    causal = jnp.tril(jnp.ones((CHUNK, CHUNK), dtype=bool))
    w_causal = jnp.where(causal[None], w_sp, 0.0).astype(v.dtype)
    mixed = jnp.einsum('gts,bnsgc->bntgc', w_causal, v) + b_sp.T[:, :, None].astype(v.dtype)
    return u * mixed.reshape(bsz, seq, A_WIDTH)

def _stick_breaking(q, k, v):
    bsz, seq, n_heads, dh = q.shape
    n_blocks = seq // Q_BLOCK
    scale = dh ** -0.5
    k_pos = jnp.arange(seq)
    q_blocks = q.reshape(bsz, n_blocks, Q_BLOCK, n_heads, dh).transpose(1, 0, 2, 3, 4)

    def one_block(args):
        q_blk, blk = args
        q_pos = blk * Q_BLOCK + jnp.arange(Q_BLOCK)
        before = (k_pos[None, :] < q_pos[:, None])[None, None]
        z = jnp.einsum('bqhd,bkhd->bhqk', q_blk, k).astype(jnp.float32) * scale
        log_beta = jax.nn.log_sigmoid(z)
        log_stay = jnp.where(before, jax.nn.log_sigmoid(-z), 0.0)
        tail = lax.cumsum(log_stay, axis=3, reverse=True) - log_stay
        weight = jnp.where(before, jnp.exp(log_beta + tail), 0.0)
        return jnp.einsum('bhqk,bkhd->bqhd', weight.astype(v.dtype), v)

    out = lax.map(one_block, (q_blocks, jnp.arange(n_blocks)))
    return out.transpose(1, 0, 2, 3, 4).reshape(bsz, seq, n_heads * dh)

def _dilated_window(q, k, v):
    bsz, seq, n_heads, dh = q.shape
    n_blocks = seq // Q_BLOCK
    scale = dh ** -0.5
    dil = jnp.array(C_DILATIONS, dtype=jnp.int32)
    offsets = jnp.arange(N_OFFSETS, dtype=jnp.int32)
    head_idx = jnp.arange(n_heads)[None, None, :]
    q_blocks = q.reshape(bsz, n_blocks, Q_BLOCK, n_heads, dh).transpose(1, 0, 2, 3, 4)

    def one_block(args):
        q_blk, blk = args
        q_pos = blk * Q_BLOCK + jnp.arange(Q_BLOCK, dtype=jnp.int32)
        idx = q_pos[:, None, None] - offsets[None, :, None] * dil[None, None, :]
        valid = idx >= 0
        idx = jnp.maximum(idx, 0)
        k_g = k[:, idx, head_idx, :]
        v_g = v[:, idx, head_idx, :]
        z = jnp.einsum('bqhd,bqmhd->bqhm', q_blk, k_g).astype(jnp.float32) * scale
        z = jnp.where(valid.transpose(0, 2, 1)[None], z, -jnp.inf)
        z_max = jnp.max(z, axis=-1, keepdims=True)
        p = jnp.exp(z - z_max)
        denom = jnp.sum(p, axis=-1)
        o = jnp.einsum('bqhm,bqmhd->bqhd', p.astype(v.dtype), v_g) / denom[..., None]
        return o.astype(q.dtype), z_max[..., 0] + jnp.log(denom)

    o, lse = lax.map(one_block, (q_blocks, jnp.arange(n_blocks)))
    o = o.transpose(1, 0, 2, 3, 4).reshape(bsz, seq, C_GROUPS, C_HEADS_PER_GROUP, dh)
    lse = lse.transpose(1, 0, 2, 3).reshape(bsz, seq, C_GROUPS, C_HEADS_PER_GROUP)
    alpha = jax.nn.softmax(lse, axis=2)
    return (o * alpha[..., None].astype(o.dtype)).reshape(bsz, seq, n_heads * dh)

def _causal_dwconv(h, w, b):
    seq = h.shape[1]
    hp = jnp.pad(h, ((0, 0), (CONV_WIDTH - 1, 0), (0, 0)))
    out = b.astype(h.dtype)
    for i in range(CONV_WIDTH):
        out = out + w[i].astype(h.dtype) * hp[:, i:i + seq]
    return out

def first_inputs(seed: int = 0) -> dict:
    key = jax.random.key(seed)
    ks = jax.random.split(key, 17)
    f32 = jnp.float32

    def nrm(k, shape, s):
        return jax.random.normal(k, shape, f32) * s

    x = nrm(ks[0], (BATCH, SEQ, D_MODEL), 1.0)
    c = nrm(ks[1], (BATCH, D_MODEL), 1.0)
    offset = jax.random.randint(ks[2], (BATCH, 1), 0, 1024, dtype=jnp.int32)
    positions = jnp.arange(SEQ, dtype=jnp.int32)[None, :] + offset
    w_ada = nrm(ks[3], (DEPTH, D_MODEL, N_MOD * D_MODEL), 0.2 * D_MODEL ** -0.5)
    b_ada = nrm(ks[4], (DEPTH, N_MOD * D_MODEL), 0.02)
    g_mix = 1.0 + nrm(ks[5], (DEPTH, D_MODEL), 0.05)
    w_in = nrm(ks[6], (DEPTH, D_MODEL, IN_WIDTH), D_MODEL ** -0.5)
    g_sgu = 1.0 + nrm(ks[7], (DEPTH, A_WIDTH), 0.05)
    w_sp = nrm(ks[8], (DEPTH, A_GROUPS, CHUNK, CHUNK), CHUNK ** -0.5)
    b_sp = 1.0 + nrm(ks[9], (DEPTH, A_GROUPS, CHUNK), 0.1)
    w_out = nrm(ks[10], (DEPTH, MIX_WIDTH, D_MODEL), MIX_WIDTH ** -0.5)
    g_ffn = 1.0 + nrm(ks[11], (DEPTH, D_MODEL), 0.05)
    w_up = nrm(ks[12], (DEPTH, D_MODEL, 2 * D_FF), D_MODEL ** -0.5)
    conv_w = nrm(ks[13], (DEPTH, CONV_WIDTH, 2 * D_FF), CONV_WIDTH ** -0.5)
    conv_b = nrm(ks[14], (DEPTH, 2 * D_FF), 0.02)
    w_down = nrm(ks[15], (DEPTH, D_FF, D_MODEL), D_FF ** -0.5)
    g_final = 1.0 + nrm(ks[16], (D_MODEL,), 0.05)
    return {'x': x, 'c': c, 'positions': positions, 'w_ada': w_ada, 'b_ada': b_ada,
            'g_mix': g_mix, 'w_in': w_in, 'g_sgu': g_sgu, 'w_sp': w_sp, 'b_sp': b_sp,
            'w_out': w_out, 'g_ffn': g_ffn, 'w_up': w_up, 'conv_w': conv_w,
            'conv_b': conv_b, 'w_down': w_down, 'g_final': g_final}

def first_block(x, c, positions, w_ada, b_ada, g_mix, w_in, g_sgu, w_sp, b_sp, w_out,
              g_ffn, w_up, conv_w, conv_b, w_down, g_final):
    bsz, seq, _ = x.shape
    cos, sin = _rope_tables(positions)
    splits = np.cumsum([A_WIDTH, A_WIDTH, B_WIDTH, B_WIDTH, B_WIDTH, C_WIDTH, C_WIDTH]).tolist()
    c_act = jax.nn.silu(c)
    for l in range(DEPTH):
        mod = (c_act @ w_ada[l] + b_ada[l])[:, None, :]
        shift1, scale1, gate1, shift2, scale2, gate2 = jnp.split(mod, N_MOD, axis=-1)
        h = _rmsnorm(x, g_mix[l]) * (1.0 + scale1) + shift1
        proj = h @ w_in[l]
        a_u, a_v, b_q, b_k, b_v, c_q, c_k, c_v = jnp.split(proj, splits, axis=-1)
        y_a = _spatial_gating(a_u, a_v, g_sgu[l], w_sp[l], b_sp[l])
        y_b = _stick_breaking(b_q.reshape(bsz, seq, B_HEADS, HEAD_DIM),
                              b_k.reshape(bsz, seq, B_HEADS, HEAD_DIM),
                              b_v.reshape(bsz, seq, B_HEADS, HEAD_DIM))
        y_c = _dilated_window(_rope(c_q.reshape(bsz, seq, C_HEADS, HEAD_DIM), cos, sin),
                              _rope(c_k.reshape(bsz, seq, C_HEADS, HEAD_DIM), cos, sin),
                              c_v.reshape(bsz, seq, C_HEADS, HEAD_DIM))
        y = jnp.concatenate([y_a, y_b, y_c], axis=-1) @ w_out[l]
        x = x + (1.0 + gate1) * y
        h = _rmsnorm(x, g_ffn[l]) * (1.0 + scale2) + shift2
        up = _causal_dwconv(h @ w_up[l], conv_w[l], conv_b[l])
        gate, val = jnp.split(up, 2, axis=-1)
        x = x + (1.0 + gate2) * ((jax.nn.silu(gate) * val) @ w_down[l])
    return _rmsnorm(x, g_final)


DEPTH_2 = 2

GRID_W = 64
N_HEADS = 16
N_KV_HEADS = 4
HEAD_DIM_2 = D_MODEL // N_HEADS
GROUP = N_HEADS // N_KV_HEADS
ATTN_QKV = N_HEADS * HEAD_DIM_2 + 2 * N_KV_HEADS * HEAD_DIM_2
GLA_HEADS = 4
GLA_DK = D_MODEL // 2 // GLA_HEADS
GLA_DV = D_MODEL // GLA_HEADS
GLA_QK = GLA_HEADS * GLA_DK
GLA_V = GLA_HEADS * GLA_DV
GATE_RANK = 16
GATE_TAU = 16.0
GLA_CHUNK = 64
GLA_IN = 2 * GLA_QK + 2 * GLA_V + 2 * GATE_RANK
D_FF_2 = 4 * D_MODEL
N_MIXERS = 2
N_ATTN = (DEPTH_2 + 1) // 2
N_GLA = DEPTH_2 // 2


def rmsnorm(x, g):
    x32 = x.astype(jnp.float32)
    y = x32 * lax.rsqrt(jnp.mean(x32 * x32, axis=-1, keepdims=True) + EPS)
    return (y * g.astype(jnp.float32)).astype(x.dtype)

def rope_angles(pos, dim):
    inv = ROPE_THETA ** (-jnp.arange(0, dim, 2, dtype=jnp.float32) / dim)
    ang = pos.astype(jnp.float32)[:, None] * inv[None, :]
    return jnp.cos(ang), jnp.sin(ang)

def apply_rot(x, cos, sin):
    half = x.shape[-1] // 2
    x32 = x.astype(jnp.float32)
    x1, x2 = x32[..., :half], x32[..., half:]
    c = cos[None, :, None, :]
    s = sin[None, :, None, :]
    return jnp.concatenate([x1 * c - x2 * s, x2 * c + x1 * s], axis=-1).astype(x.dtype)

def axial_rope(x, rope):
    cr, sr, cc, sc = rope
    half = HEAD_DIM_2 // 2
    return jnp.concatenate([apply_rot(x[..., :half], cr, sr), apply_rot(x[..., half:], cc, sc)], axis=-1)

def attention_mixer(h, w_qkv, q_g, k_g, w_o, rope):
    B, S, _ = h.shape
    qkv = h @ w_qkv
    q, k, v = jnp.split(qkv, [N_HEADS * HEAD_DIM_2, (N_HEADS + N_KV_HEADS) * HEAD_DIM_2], axis=-1)
    q = rmsnorm(q.reshape(B, S, N_HEADS, HEAD_DIM_2), q_g)
    k = rmsnorm(k.reshape(B, S, N_KV_HEADS, HEAD_DIM_2), k_g)
    v = v.reshape(B, S, N_KV_HEADS, HEAD_DIM_2)
    q = axial_rope(q, rope)
    k = axial_rope(k, rope)
    n_blk = S // Q_BLOCK
    qb = jnp.moveaxis(q.reshape(B, n_blk, Q_BLOCK, N_KV_HEADS, GROUP, HEAD_DIM_2), 1, 0)
    scale = 1.0 / math.sqrt(HEAD_DIM_2)

    def block(qblk):
        s = jnp.einsum('bqhgd,bkhd->bhgqk', qblk, k, preferred_element_type=jnp.float32) * scale
        p = jax.nn.softmax(s, axis=-1).astype(v.dtype)
        return jnp.einsum('bhgqk,bkhd->bqhgd', p, v)

    o = lax.map(block, qb)
    o = jnp.moveaxis(o, 0, 1).reshape(B, S, N_HEADS * HEAD_DIM_2)
    return o @ w_o

def gla_chunked(q, k, v, logg):
    B, S, H, DK = q.shape
    DV = v.shape[-1]
    N = S // GLA_CHUNK
    to_c = lambda t: t.reshape(B, N, GLA_CHUNK, H, t.shape[-1]).transpose(0, 3, 1, 2, 4)
    q, k, v, logg = to_c(q), to_c(k), to_c(v), to_c(logg)
    b = jnp.cumsum(logg, axis=3)
    qe = q * jnp.exp(b)
    ke = k * jnp.exp(-b)
    mask = jnp.tril(jnp.ones((GLA_CHUNK, GLA_CHUNK), dtype=bool))
    a = jnp.einsum('bhncd,bhnjd->bhncj', qe, ke)
    a = jnp.where(mask, a, 0.0)
    o_intra = jnp.einsum('bhncj,bhnjv->bhncv', a, v)
    b_last = b[..., -1:, :]
    kd = k * jnp.exp(b_last - b)
    chunk_kv = jnp.einsum('bhncd,bhncv->bhndv', kd, v)
    decay = jnp.exp(b_last[..., 0, :])

    def step(state, inp):
        dec, ckv = inp
        return dec[..., None] * state + ckv, state

    init = jnp.zeros((B, H, DK, DV), jnp.float32)
    _, s_before = lax.scan(step, init, (jnp.moveaxis(decay, 2, 0), jnp.moveaxis(chunk_kv, 2, 0)))
    s_before = jnp.moveaxis(s_before, 0, 2)
    o = o_intra + jnp.einsum('bhncd,bhndv->bhncv', qe, s_before)
    return o.transpose(0, 2, 3, 1, 4).reshape(B, S, H, DV)

def gla_mixer(h, w_in, w_gate_up, b_gate, out_g, w_o):
    B, S, _ = h.shape
    f32 = jnp.float32
    proj = h @ w_in
    q, k, v, r, z = jnp.split(proj, [GLA_QK, 2 * GLA_QK, 2 * GLA_QK + GLA_V, 2 * GLA_QK + 2 * GLA_V], axis=-1)
    q = q.astype(f32).reshape(B, S, GLA_HEADS, GLA_DK) * (GLA_DK ** -0.5)
    k = k.astype(f32).reshape(B, S, GLA_HEADS, GLA_DK)
    v = v.astype(f32).reshape(B, S, GLA_HEADS, GLA_DV)
    z = z.astype(f32).reshape(B, S, 2, GATE_RANK)
    logit = jnp.einsum('bsir,ire->bsie', z, w_gate_up.astype(f32)) + b_gate.astype(f32)
    logg = (jax.nn.log_sigmoid(logit) / GATE_TAU).reshape(B, S, 2, GLA_HEADS, GLA_DK)
    o_f = gla_chunked(q, k, v, logg[:, :, 0])
    flip = lambda t: jnp.flip(t, axis=1)
    o_b = flip(gla_chunked(flip(q), flip(k), flip(v), flip(logg[:, :, 1])))
    o = rmsnorm(o_f + o_b, out_g).reshape(B, S, GLA_V)
    o = o * jax.nn.silu(r.astype(f32))
    return o.astype(h.dtype) @ w_o

def sq_relu_mlp(h, w_in, w_out):
    return jnp.square(jax.nn.relu(h @ w_in)) @ w_out

def second_inputs(seed: int = 0) -> dict:
    key = jax.random.key(seed)
    ks = jax.random.split(key, 16)
    nrm = lambda k, shape, fan_in: jax.random.normal(k, shape, jnp.float32) * (fan_in ** -0.5)
    gain = lambda k, shape: 1.0 + 0.05 * jax.random.normal(k, shape, jnp.float32)
    return {
        'x': jax.random.normal(ks[0], (BATCH, SEQ, D_MODEL), jnp.float32),
        'norm_mix': gain(ks[1], (DEPTH_2, D_MODEL)),
        'norm_mlp': gain(ks[2], (DEPTH_2, D_MODEL)),
        'attn_w_qkv': nrm(ks[3], (N_ATTN, D_MODEL, ATTN_QKV), D_MODEL),
        'attn_q_norm': gain(ks[4], (N_ATTN, HEAD_DIM_2)),
        'attn_k_norm': gain(ks[5], (N_ATTN, HEAD_DIM_2)),
        'attn_w_o': nrm(ks[6], (N_ATTN, N_HEADS * HEAD_DIM_2, D_MODEL), N_HEADS * HEAD_DIM_2),
        'gla_w_in': nrm(ks[7], (N_GLA, D_MODEL, GLA_IN), D_MODEL),
        'gla_w_gate_up': nrm(ks[8], (N_GLA, 2, GATE_RANK, GLA_QK), GATE_RANK),
        'gla_b_gate': 0.1 * jax.random.normal(ks[9], (N_GLA, 2, GLA_QK), jnp.float32),
        'gla_out_norm': gain(ks[10], (N_GLA, GLA_DV)),
        'gla_w_o': nrm(ks[11], (N_GLA, GLA_V, D_MODEL), GLA_V),
        'mlp_w_in': nrm(ks[12], (DEPTH_2, D_MODEL, D_FF_2), D_MODEL),
        'mlp_w_out': nrm(ks[13], (DEPTH_2, D_FF_2, D_MODEL), D_FF_2),
        'final_norm': gain(ks[14], (D_MODEL,)),
    }

def second_block(x, norm_mix, norm_mlp, attn_w_qkv, attn_q_norm, attn_k_norm, attn_w_o,
              gla_w_in, gla_w_gate_up, gla_b_gate, gla_out_norm, gla_w_o,
              mlp_w_in, mlp_w_out, final_norm):
    S = x.shape[1]
    rows = S // GRID_W
    row = jnp.repeat(jnp.arange(rows, dtype=jnp.int32), GRID_W)
    col = jnp.tile(jnp.arange(GRID_W, dtype=jnp.int32), rows)
    cr, sr = rope_angles(row, HEAD_DIM_2 // 2)
    cc, sc = rope_angles(col, HEAD_DIM_2 // 2)
    rope = (cr, sr, cc, sc)
    h = x
    for i in range(DEPTH_2):
        j = i // N_MIXERS
        hn = rmsnorm(h, norm_mix[i])
        if i % N_MIXERS == 0:
            h = h + attention_mixer(hn, attn_w_qkv[j], attn_q_norm[j], attn_k_norm[j], attn_w_o[j], rope)
        else:
            h = h + gla_mixer(hn, gla_w_in[j], gla_w_gate_up[j], gla_b_gate[j], gla_out_norm[j], gla_w_o[j])
        h = h + sq_relu_mlp(rmsnorm(h, norm_mlp[i]), mlp_w_in[i], mlp_w_out[i])
    return rmsnorm(h, final_norm)


def setup_inputs(seed=0):
    out = dict(first_inputs(seed))
    for name, value in second_inputs(seed + 1).items():
        if name != "x":
            out[name + "_2"] = value
    return out


def reference(
    x, c, positions, w_ada, b_ada, g_mix, w_in, g_sgu, w_sp, b_sp, w_out, g_ffn, w_up, conv_w,
    conv_b, w_down, g_final, norm_mix_2, norm_mlp_2, attn_w_qkv_2, attn_q_norm_2, attn_k_norm_2,
    attn_w_o_2, gla_w_in_2, gla_w_gate_up_2, gla_b_gate_2, gla_out_norm_2, gla_w_o_2,
    mlp_w_in_2, mlp_w_out_2, final_norm_2,
):
    x = first_block(
        x, c, positions, w_ada, b_ada, g_mix, w_in, g_sgu, w_sp, b_sp, w_out, g_ffn, w_up,
        conv_w, conv_b, w_down, g_final,
    )
    return second_block(
        x, norm_mix_2, norm_mlp_2, attn_w_qkv_2, attn_q_norm_2, attn_k_norm_2, attn_w_o_2,
        gla_w_in_2, gla_w_gate_up_2, gla_b_gate_2, gla_out_norm_2, gla_w_o_2, mlp_w_in_2,
        mlp_w_out_2, final_norm_2,
    )


_drawn_inputs = setup_inputs


def setup_inputs(seed=0):
    import zlib

    import numpy as np

    out = dict(_drawn_inputs(seed))
    spreads = {}
    factors = {'g_sgu': 3.627,
     'conv_b': 2.971,
     'attn_q_norm_2': 8.0,
     'attn_k_norm_2': 6.744,
     'gla_b_gate_2': 3.091,
     'gla_out_norm_2': 3.114}
    for name, (base, spread) in spreads.items():
        noise = np.random.default_rng([zlib.crc32(name.encode()), seed]).standard_normal(out[name].shape)
        drawn = base * np.exp(spread * noise) if base else spread * noise
        out[name] = __import__('jax').numpy.asarray(drawn.astype(out[name].dtype))
    for name, factor in factors.items():
        out[name] = (out[name] * factor).astype(out[name].dtype)
    return out
```

```python
from contextlib import ExitStack

import numpy as np

import concourse.bass as bass
from concourse import mybir

ALU = mybir.AluOpType
ACT = mybir.ActivationFunctionType
AX = mybir.AxisListType
F32 = mybir.dt.float32
F32R = mybir.dt.float32r

P = 128
D = 1024
S = 256
KT = D // P
TT = S // P
HD = 64
EPS = 1e-6
D_FF = 2816
FF_STEPS = D_FF // S
MLP_STEPS = 4 * D // S
GLA_IN = 3104
GLA_CHUNK = 64
NCH = S // GLA_CHUNK
CHUNK = KT * S
RAW_SLOTS = 4
SPLIT_SLOTS = 3
SP3 = 3 * P
MAGIC = 12582912.0
TWO_PI = (6.28125, 0.0019350051879882812, 3.0199159819e-07)
PI_BELOW = 3.1415925

IN_COLS = [1664, 1920, 2176, 0, 256, 512, 768, 1024, 1280, (1536, 2432), 2560]
QKV = [4, 5, 0, 1, 2, 3]
GLA = [12, 0, 1, 2, 3, 4, 5, 6, 7, 8, 9, 10, 11]

CONST_W = {
    "ident": P, "ones": P, "tail": P, "tail_all": P, "before": P, "window": 3 * SP3, "upto": P,
    "rope_swap": P, "axial_swap": P, "axial_cos": S, "axial_sin": S, "head_mean": P,
    "chunk_fwd": P, "chunk_bwd": P, "scan_fwd": S, "scan_bwd": S, "inv_freq": 1, "eps": 1, "one": 1,
}
CONST_AT, CONST_COLS = {}, 0
for _name, _w in CONST_W.items():
    CONST_AT[_name] = (CONST_COLS, _w)
    CONST_COLS += _w

ROWS = [
    {"c": 8, "b_ada": 48, "g_mix": 8, "g_ffn": 8, "g_final": 8, "g_sgu": 2},
    {"norm_mix": 16, "norm_mlp": 16, "final_norm": 8, "b_gate": 8, "out_norm": 2, "q_norm": 1, "k_norm": 1},
    {"conv_w0": 22 * 2, "conv_w1": 22 * 2},
    {"conv_w2": 22 * 2, "conv_b": 22 * 2},
]
COL_AT, N_COLS = {}, 0
for _rows in ROWS:
    for _name, _n in _rows.items():
        COL_AT[_name] = N_COLS
        N_COLS += _n


def constants():
    f = np.float32
    r = np.arange(P)
    k, q = r[:, None], r[None, :]
    t = np.arange(S)
    out = {}
    out["ident"] = (k == q)
    out["ones"] = np.ones((P, P))
    out["tail"] = -(k >= q).astype(f)
    out["tail_all"] = -np.ones((P, P))
    out["before"] = (k < q)
    win = []
    for dil in (1, 4, 16):
        for qb, width in ((0, P), (1, S)):
            back = (qb * P + r)[:, None] - np.arange(width)[None, :]
            ok = (back >= 0) & (back % dil == 0) & (back <= 128 * dil)
            win.append(np.where(ok, 0.0, -1e30))
    out["window"] = np.concatenate(win, 1)
    out["upto"] = (k <= q)
    for name, w in (("rope_swap", 32), ("axial_swap", 16)):
        low = (q % (2 * w)) < w
        out[name] = np.where(low & (k == q + w), -1.0, 0.0) + np.where(~low & (k == q - w), 1.0, 0.0)
    inv = (f(10000.0) ** (-np.arange(0, 32, 2, dtype=f) / f(32))).astype(f)
    pos = np.where((r % 64 < 32)[:, None], (t // 64)[None, :], (t % 64)[None, :]).astype(f)
    ang = pos * inv[r % 16][:, None]
    out["axial_cos"], out["axial_sin"] = np.cos(ang), np.sin(ang)
    out["head_mean"] = (k // HD == q // HD) / HD
    same = k // GLA_CHUNK == q // GLA_CHUNK
    out["chunk_fwd"], out["chunk_bwd"] = same & (k <= q), same & (k >= q)
    out["scan_fwd"] = np.broadcast_to(t % GLA_CHUNK != 0, (P, S))
    out["scan_bwd"] = np.broadcast_to(t % GLA_CHUNK != GLA_CHUNK - 1, (P, S))
    inv = (f(10000.0) ** (-np.arange(0, HD, 2, dtype=f) / f(HD))).astype(f)
    out["inv_freq"] = inv[r % 32][:, None]
    out["eps"] = np.full((P, 1), EPS)
    out["one"] = np.ones((P, 1))
    return np.ascontiguousarray(np.concatenate([np.asarray(out[n], f) for n in CONST_W], 1))


def weight_stream():
    ada = [("ada", p, q) for p in range(2, 6) for q in range(4)]
    s = [("ada", p, q) for p in range(2) for q in range(4)]
    for n in range(11):
        s.append(("in", n))
        if n >= 3:
            s.append(ada.pop(0))
    s += [("out", 0), ("out", 1)] + ada + [("out", 2), ("out", 3)]
    for i in range(FF_STEPS + 1):
        s += [("gate", i), ("val", i)] if i < FF_STEPS else []
        s += [("down", i - 1)] if i > 0 else []
    s += [("qkv", n) for n in range(6)]
    s += [("wo", n) for n in range(4)]
    for layer in range(2):
        if layer == 1:
            s += [("gla", n) for n in range(13)]
            s += [("gla_out", n) for n in range(4)]
        for i in range(MLP_STEPS + 1):
            s += [("mlp_in", layer, i)] if i < MLP_STEPS else []
            s += [("mlp_out", layer, i - 1)] if i > 0 else []
    return s


STREAM = weight_stream()
LOAD_OF = {key: n for n, key in enumerate(STREAM)}
SPLITS = [key for key in STREAM if key[0] != "ada"]
SPLIT_OF = {key: n for n, key in enumerate(SPLITS)}


def schedule():
    ada = [("ada", p, q) for p in range(2, 6) for q in range(4)]
    s = [("setup",)] + [("ada", p, q) for p in range(2) for q in range(4)] + [("gains", 0)]
    s += [("root", 0), ("scaled", 0)]
    extra = {1: [("rope", 0)], 2: [("rope", 1), ("rope", 2)], 3: [("rope", 3), ("rope", 4)],
             4: [("rope", 5), ("v_norm",)], 8: [("gate_mix",), ("stick_a", 0)], 9: [("win_a", 0), ("stick_a", 1)]}
    for n in range(11):
        s.append(("in", n))
        s += extra.get(n, [])
        if n >= 3:
            s.append(ada.pop(0))
    s += [("stick_b", 0), ("win_a", 1), ("stick_a", 2), ("stick_b", 1), ada.pop(0), ("win_a", 2), ("stick_c", 0),
          ("stick_a", 3), ("stick_b", 2), ada.pop(0), ("win_a", 3), ("stick_a", 4), ("stick_b", 3), ada.pop(0),
          ("stick_c", 1), ("win_a", 4), ("stick_a", 5), ("stick_b", 4), ada.pop(0), ("win_a", 5), ("stick_b", 5),
          ("win_b",), ada.pop(0), ("stick_c", 2)]
    for m in range(3):
        s += [("win_c", 2 * m), ("win_c", 2 * m + 1), ada.pop(0), ("win_d", m)]
    s += [("gains", 1), ("split", 1)]
    s += [("project", "out", n) for n in range(4)]
    s += [("root", 1), ("scaled", 1)]
    for i in range(FF_STEPS + 1):
        s += [("ff_up", i)] if i < FF_STEPS else []
        s += [("down", "down", i - 1)] if i > 0 else []
    s += [("add_down", "down")]
    s += [("root", 2), ("scaled", 2), ("root", 3), ("scaled", 3)]
    for n in range(6):
        s += [("qkv", n)]
        if n == 2:
            s += [("qk_a", 0), ("qk_a", 1), ("qk_b", 0)]
        if n >= 2:
            t = 2 * (n - 1)
            s += [("qk_a", t), ("qk_b", t - 1), ("qk_a", t + 1), ("qk_b", t)]
    s += [("qk_b", 9), ("att_a", 0)]
    for h in range(16):
        s += [("att_a", h + 1)] if h < 15 else []
        s += [("att_b", h)] + ([("att_o", h - 1)] if h else [])
        s += [("att_c", h // 2 - 1)] if h >= 2 and h % 2 == 0 else []
    s += [("att_o", 15), ("att_c", 7)]
    s += [("split", 4)]
    s += [("project", "wo", n) for n in range(4)]
    for layer in range(2):
        if layer == 1:
            s += [("root", 5), ("scaled", 5)]
            s += [("gla", n) for n in range(13)]
            for h in range(4):
                s += [("gla_a", h), ("gla_b", h)]
            s += [("split", 7)]
            s += [("project", "gla_out", n) for n in range(4)]
        s += [("root", 4 + 2 * layer), ("scaled", 4 + 2 * layer)]
        for i in range(MLP_STEPS + 1):
            s += [("mlp_up", layer, i)] if i < MLP_STEPS else []
            s += [("down", "mlp_out", layer, i - 1)] if i > 0 else []
        s += [("add_down", "mlp_out", layer)]
    s += [("root", 7), ("scaled", 7), ("finish",)]
    return s


NEXT_NORM = {"out": 1, "down": 2, "wo": 4, "gla_out": 6}
SET_OF_NORM = {0: 0, 1: 2, 3: 3, 4: 5, 5: 6, 6: 8}
QK_CHUNK = [0, 0, 2, 2, 3, 3, 4, 4, 5, 5]
LAST_USE = {0: ("in", 10), 1: ("out", 3), 2: ("val", FF_STEPS - 1), 3: ("qkv", 5), 4: ("wo", 3),
            5: ("mlp_in", 0, MLP_STEPS - 1), 6: ("gla", 12), 7: ("gla_out", 3), 8: ("mlp_in", 1, MLP_STEPS - 1)}
USES = {"in": 0, "out": 1, "gate": 2, "val": 2, "qkv": 3, "wo": 4, "gla": 6, "gla_out": 7}


def build(nc, a, out, known):
    marks, banks, counts, sems = {}, {}, {}, {}
    ctx = ExitStack()
    with ctx:
        def sb(name, shape, dt=F32):
            return ctx.enter_context(nc.sbuf_tensor(name, shape, dt))

        def sem(name):
            if name not in sems:
                sems[name] = ctx.enter_context(nc.semaphore(name))
            return sems[name]

        def mark(name, *event, by=1):
            counts[name] = counts.get(name, 0) + by
            assert (name, *event) not in marks, (name, event)
            marks[(name, *event)] = (name, counts[name])
            return sem(name), by

        def same(event, as_event):
            assert event not in marks, event
            marks[event] = marks[as_event]

        def at(*event):
            name, value = (event[0], 1) if known is None else known[0][event]
            return sem(name), value

        raw = sb("raw", [P, RAW_SLOTS, CHUNK])
        w_hi = sb("w_hi", [P, SPLIT_SLOTS, CHUNK], F32R)
        w_lo = sb("w_lo", [P, SPLIT_SLOTS, CHUNK], F32R)
        const = sb("const", [P, CONST_COLS])
        rows = sb("rows", [P, len(ROWS), P])
        cols = sb("cols", [P, N_COLS])
        mod = sb("mod", [P, 48])
        gain = sb("gain", [P, 4, KT])
        c_act = sb("c_act", [P, KT])
        ada = sb("ada", [P, 2, D])
        x_t = sb("x_t", [P, KT, S])
        h_hi = sb("h_hi", [P, KT, S], F32R)
        h_lo = sb("h_lo", [P, KT, S], F32R)
        y_t = sb("y_t", [P, KT, S])
        rstd = sb("rstd", [P, S])
        a_hi = sb("a_hi", [P, 4, S], F32R)
        a_lo = sb("a_lo", [P, 4, S], F32R)
        work = sb("work", [P, 8, S])
        arena = sb("arena", [P, 48 * S])
        pos_i = sb("pos_i", [P, S], mybir.dt.int32)
        small = sb("small", [P, P])
        psum = [ctx.enter_context(nc.psum_tensor(f"psum{b}", [P, 512], F32)) for b in range(8)]

        def cst(name):
            o, w = CONST_AT[name]
            return const[:, o:o + w]

        def col(name, i=0, n=1):
            return cols[:, COL_AT[name] + i:COL_AT[name] + i + n]

        def area(first, n):
            return arena[:, first * S:(first + n) * S].rearrange("p (n s) -> p n s", s=S)

        def blocks3(ap):
            return ap.rearrange("p (n c) -> p n c", c=P)

        ring = {"n": 0, "last": {}, "set": range(8)}

        def evacuated(*job):
            name = "act_read" if known is not None and ("act_read", *job) in known[0] else "dve_read"
            return at(name, *job)

        def take(pe, *job):
            b = ring["set"][ring["n"] % len(ring["set"])]
            ring["n"] += 1
            if b in ring["last"]:
                pe.wait_ge(*evacuated(*ring["last"][b]))
            ring["last"][b] = job
            banks[job] = b
            return psum[b]

        def bank(*job):
            return psum[0 if known is None else known[1][job]]

        u_t, v_tok, v_nrm = area(0, 2), area(2, 2), area(4, 2)
        bqz, bk_t = area(6, 6), area(12, 3)
        vals = arena[:, 15 * S:21 * S].rearrange("p (t c) -> p t c", t=TT)
        cqk, cqz, ck_t = area(21, 6), area(27, 6), area(33, 3)
        w_sp_r = arena[:, 21 * S:23 * S].rearrange("p (g s) -> p g s", g=4)
        w_sp_t = arena[:, 36 * S:38 * S].rearrange("p (g s) -> p g s", g=4)
        angle = area(38, 6)
        b_sp_b = arena[:, 45 * S:46 * S].rearrange("p (m s) -> p m s", m=2)

        def stick(h):
            return arena[:, 21 * S + (h % 4) * SP3:21 * S + (h % 4 + 1) * SP3]

        def win_p(h):
            return arena[:, 36 * S + h * SP3:36 * S + (h + 1) * SP3]

        def win_pt(h):
            o = h * SP3 if h < 4 else 27 * S + (h - 4) * SP3
            return arena[:, o:o + SP3]

        ff_g, ff_v, ff_s = area(0, 2), area(2, 2), area(4, 2)
        aqz, ak_dup, ak_r, v2 = area(0, 16), area(16, 4), area(20, 2), area(22, 2)
        att_p = area(24, 4).rearrange("p (b q) s -> p b q s", b=2)
        att_pt = area(28, 4).rearrange("p (b q) s -> p b q s", b=2)
        qn = area(32, 4)
        gq, gk, gr, z_t = area(0, 4), area(4, 4), area(16, 8), area(24, 1)
        gv = arena[:, 8 * S:16 * S].rearrange("p (t c) -> p t c", t=TT)
        qe, ke = area(25, 4), area(29, 4)
        kd = area(33, 2)
        kd_tok = area(35, 2).rearrange("p n (t d) -> p n t d", t=TT)
        state = area(37, 6).rearrange("p (n c) s -> p n c s", n=2)
        a_sum = area(43, 1).rearrange("p n (t c) -> p n t c", t=TT)
        a_tmp = area(44, 1).rearrange("p n (t c) -> p n t c", t=TT)
        gla_sq = area(45, 2)
        w_gate = ada[96:128, 0, :].rearrange("p (n e) -> p n e", n=2)
        x_rows = work[:, :, :].rearrange("p n s -> p (n s)").rearrange("p (t c) -> p t c", t=TT)
        y_rows = raw[:, 0:2, 0:D]

        def wview(buf, slot, kt):
            return buf[:, slot, :].rearrange("p (k c) -> p k c", k=kt)

        def halved(buf, slot, key):
            return wview(buf, slot, KT)[:, :, 0:P] if key == ("gla", 0) else buf[:, slot, :]

        def landed(n):
            return at(f"raw_landed{n % RAW_SLOTS}", n)

        block = ctx.enter_context(nc.Block())

        @block.sync
        def _(sp):
            def column_chunk(w, c0, n=S):
                return w[:, c0:c0 + n].rearrange("(k p) c -> p k c", p=P)

            def row_chunk(w, r0):
                return w[r0:r0 + S, :].rearrange("(k p) c -> p k c", p=P)

            def sources(key):
                kind, n = key[0], key[-1]
                if kind == "ada":
                    return [(0, row_chunk(a["w_ada"][0][:, key[1] * D:(key[1] + 1) * D], n * S))], 2
                if kind == "in":
                    c0 = IN_COLS[n]
                    if isinstance(c0, tuple):
                        return [(j * P, column_chunk(a["w_in"][0], c, P)) for j, c in enumerate(c0)], KT
                    return [(0, column_chunk(a["w_in"][0], c0))], KT
                if kind == "gla" and n == 0:
                    return [(0, column_chunk(a["gla_w_in_2"][0], GLA_IN - P, P))], KT
                if kind == "down":
                    return [(0, row_chunk(a["w_down"][0], n * S))], 2
                if kind == "mlp_out":
                    return [(0, row_chunk(a["mlp_w_out_2"][key[1]], n * S))], 2
                w, c0 = {
                    "out": lambda: (a["w_out"][0], n * S), "gate": lambda: (a["w_up"][0], n * S),
                    "val": lambda: (a["w_up"][0], D_FF + n * S), "qkv": lambda: (a["attn_w_qkv_2"][0], QKV[n] * S),
                    "wo": lambda: (a["attn_w_o_2"][0], n * S), "gla": lambda: (a["gla_w_in_2"][0], GLA[n] * S),
                    "gla_out": lambda: (a["gla_w_o_2"][0], n * S),
                    "mlp_in": lambda: (a["mlp_w_in_2"][key[1]], n * S),
                }[kind]()
                return [(0, column_chunk(w, c0))], KT

            for n, key in enumerate(STREAM):
                if n >= RAW_SLOTS:
                    old = STREAM[n - RAW_SLOTS]
                    if old[0] == "ada":
                        sp.wait_ge(*at("ada_added", *old[1:]))
                    else:
                        sp.wait_ge(*at("w_lo", SPLIT_OF[old]))
                parts, kt = sources(key)
                slot = n % RAW_SLOTS
                for j, (c0, src) in enumerate(parts):
                    dst = wview(raw, slot, kt)[:, :, c0:c0 + src.shape[2]]
                    event = (n,) if j == len(parts) - 1 else (n, "first part")
                    sp.dma_start(dst, src).then_inc(*mark(f"raw_landed{slot}", *event, by=16))
            for t in range(TT):
                sp.wait_ge(*at("y_rows", 2 * t))
                sp.wait_ge(*at("y_half", 2 * t + 1))
                sp.dma_start(out[0, t * P:(t + 1) * P, :], y_rows[:, t, :]).then_inc(*mark("out_landed", t, by=16))
            sp.wait_ge(*at("out_landed", TT - 1))

        @block.gpsimd
        def _(pool):
            pool.memset(bqz, 0.0).then_inc(*mark("zeroed", 0))
            pool.memset(cqz, 0.0).then_inc(*mark("zeroed", 1))
            for n, key in enumerate(SPLITS):
                r = LOAD_OF[key]
                pool.wait_ge(*landed(r))
                pool.wait_ge(*at("w_hi", n))
                pool.tensor_tensor(halved(w_lo, n % SPLIT_SLOTS, key), halved(raw, r % RAW_SLOTS, key),
                                   halved(w_hi, n % SPLIT_SLOTS, key).bitcast(F32), ALU.subtract)\
                    .then_inc(*mark("w_lo", n))

        @block.scalar
        def _(act):
            done = {"hi": 0}

            def weights_upto(n):
                while done["hi"] <= min(n, len(SPLITS) - 1):
                    m = done["hi"]
                    r = LOAD_OF[SPLITS[m]]
                    act.wait_ge(*landed(r))
                    if m >= SPLIT_SLOTS:
                        act.wait_ge(*at("chunk_used", m - SPLIT_SLOTS))
                    act.activation(halved(w_hi, m % SPLIT_SLOTS, SPLITS[m]), halved(raw, r % RAW_SLOTS, SPLITS[m]),
                                   ACT.Copy).then_inc(*mark("w_hi", m))
                    done["hi"] += 1

            def ahead(key):
                weights_upto(SPLIT_OF[key] + SPLIT_SLOTS - 1)

            def high(idx):
                for k in range(KT):
                    act.wait_ge(*at("full", idx, k))
                    if k == 0 and idx > 0:
                        act.wait_ge(*at("chunk_used", SPLIT_OF[LAST_USE[idx - 1]]))
                    act.activation(h_hi[:, k, :], y_t[:, k, :], ACT.Copy).then_inc(*mark("high", idx, k))

            def copy(job, dst, func=ACT.Copy, **kw):
                act.wait_ge(*at("job", *job))
                act.activation(dst, bank(*job)[:, 0:S], func, **kw).then_inc(*mark("act_read", *job))

            def setup():
                act.dma_start(const[:, :], a["const"]).then_inc(*mark("const_landed", 0, by=16))
                at_row = 0
                src = {"c": a["c"].rearrange("o (n p) -> (o n) p", p=P),
                       "b_ada": a["b_ada"].rearrange("o (n p) -> (o n) p", p=P),
                       "g_mix": a["g_mix"].rearrange("o (n p) -> (o n) p", p=P),
                       "g_ffn": a["g_ffn"].rearrange("o (n p) -> (o n) p", p=P),
                       "g_final": a["g_final"].rearrange("(n p) -> n p", p=P),
                       "g_sgu": a["g_sgu"].rearrange("o (n p) -> (o n) p", p=P),
                       "norm_mix": a["norm_mix_2"].rearrange("o (n p) -> (o n) p", p=P),
                       "norm_mlp": a["norm_mlp_2"].rearrange("o (n p) -> (o n) p", p=P),
                       "final_norm": a["final_norm_2"].rearrange("(n p) -> n p", p=P),
                       "b_gate": a["gla_b_gate_2"][0].rearrange("o (n p) -> (o n) p", p=P),
                       "out_norm": a["gla_out_norm_2"].rearrange("o (n p) -> (o n) p", p=P),
                       "conv_w0": a["conv_w"][0, 0:1].rearrange("o (n p) -> (o n) p", p=P),
                       "conv_w1": a["conv_w"][0, 1:2].rearrange("o (n p) -> (o n) p", p=P),
                       "conv_w2": a["conv_w"][0, 2:3].rearrange("o (n p) -> (o n) p", p=P),
                       "conv_b": a["conv_b"].rearrange("o (n p) -> (o n) p", p=P)}
                for j, names in enumerate(ROWS):
                    at_row = 0
                    for name, n in names.items():
                        if name in ("q_norm", "k_norm"):
                            g = a[f"attn_{name}_2"]
                            act.dma_start(rows[at_row:at_row + 1, j, 0:HD], g).then_inc(*mark("rows_landed", name, 0, by=16))
                            act.dma_start(rows[at_row:at_row + 1, j, HD:P], g).then_inc(*mark("rows_landed", name, 1, by=16))
                        else:
                            act.dma_start(rows[at_row:at_row + n, j, :], src[name])\
                                .then_inc(*mark("rows_landed", name, by=16))
                        at_row += n
                    if j == 0:
                        act.dma_start(x_rows, a["x"][0].rearrange("(t p) c -> p t c", p=P))\
                            .then_inc(*mark("x_landed", 0, by=16))
                act.dma_start(w_sp_r, a["w_sp"][0].rearrange("g t s -> t g s")).then_inc(*mark("w_sp_landed", 0, by=16))
                act.dma_start(pos_i[:, :], a["positions"].broadcast_to([P, S])).then_inc(*mark("pos_landed", 0, by=16))
                for g in range(4):
                    act.dma_start(b_sp_b[64 * (g % 2):64 * (g % 2) + 64, g // 2, :],
                                  a["b_sp"][0, g:g + 1, :].broadcast_to([64, P])).then_inc(*mark("b_sp_landed", g, by=16))
                act.wait_ge(*at("cols", 0))
                act.activation(c_act[:, :], col("c", 0, KT), ACT.Silu).then_inc(*mark("c_act", 0))
                for j in range(2):
                    act.wait_ge(*at("angle", j))
                    act.activation(angle[:, j, :], angle[:, 2 + j, :], ACT.Sin).then_inc(*mark("sine", j))
                act.wait_ge(*at("x_new", 0, KT - 1))
                weights_upto(2)

            def root(i):
                for k in range(KT):
                    act.wait_ge(*at("x_new", i, k))
                    act.activation(work[:, k, :], x_t[:, k, :], ACT.Square).then_inc(*mark("square", i, k))
                copy(("sum", i), rstd[:, :], ACT.Sqrt, scale=1.0 / D, bias=cst("eps"))

            def scaled(i):
                if i in SET_OF_NORM:
                    high(SET_OF_NORM[i])

            def take_in(n):
                ahead(("in", n))
                for m in range(2):
                    job = ("in", n, m)
                    t = 2 * n + m
                    if n < 3:
                        copy(job, cqk[:, t, :], scale=0.125 if t < 3 else 1.0)
                    elif n == 3:
                        copy(job, u_t[:, m, :], ACT.Gelu_apprx_tanh)
                    elif n == 4:
                        copy(job, v_tok[:, m, :], ACT.Gelu_apprx_tanh)
                    elif n < 8 and t - 10 < 3:
                        act.wait_ge(*at("job", *job))
                        act.wait_ge(*at("zeroed", 0))
                        act.activation(bqz[0:64, 2 * (t - 10), :], bank(*job)[0:64, 0:S], ACT.Copy, scale=0.125)\
                            .then_inc(*mark("b_q", t - 10))
                        act.activation(bqz[64:128, 2 * (t - 10) + 1, :], bank(*job)[64:128, 0:S], ACT.Copy,
                                       scale=0.125).then_inc(*mark("act_read", *job))
                    elif n < 8:
                        copy(job, bk_t[:, t - 13, :])
                    else:
                        copy(job, vals[:, m, (n - 8) * S:(n - 7) * S])

            def v_norm():
                act.wait_ge(*at("v_sum", 0))
                act.activation(small[:, 8:16], small[:, 0:8], ACT.Sqrt, scale=1.0 / HD, bias=cst("eps"))\
                    .then_inc(*mark("v_root", 0))

            def stick_a(h):
                act.wait_ge(*at("job", "stick", h))
                if h >= 4:
                    act.wait_ge(*at("job", "stick_o", (h - 4) // 2))
                act.activation(stick(h), bank("stick", h)[:, 0:SP3], ACT.Abs).then_inc(*mark("stick_act", h, 0))
                act.wait_ge(*at("stick_act", h, 0))
                act.activation(stick(h), stick(h), ACT.Exp, scale=-1.0).then_inc(*mark("stick_act", h, 1))
                act.wait_ge(*at("stick_act", h, 1))
                act.activation(stick(h), stick(h), ACT.Ln, bias=cst("one")).then_inc(*mark("stick_act", h, 2))

            def stick_b(h):
                act.wait_ge(*at("stick_tail", h))
                act.activation(stick(h), bank("stick", h)[:, 0:SP3], ACT.Exp).then_inc(*mark("act_read", "stick", h))

            def win_a(h):
                act.wait_ge(*at("win_max", h))
                for q in range(TT):
                    pr = win_p(h)[:, 0:P] if q == 0 else win_p(h)[:, P:SP3]
                    act.activation(pr, pr, ACT.Exp, bias=small[:, 32 + 2 * h + q:33 + 2 * h + q],
                                   accum_out=small[:, 48 + 2 * h + q:49 + 2 * h + q]).then_inc(*mark("win_exp", h, q))

            def win_b():
                act.wait_ge(*at("win_rel", 0))
                act.activation(small[:, 64:76], small[:, 64:76], ACT.Exp).then_inc(*mark("win_factor", 0))

            def win_c(h):
                act.wait_ge(*at("job", "win_t", h))
                act.activation(win_pt(h), bank("win_t", h)[:, 0:SP3], ACT.Copy).then_inc(*mark("act_read", "win_t", h))

            def project(kind, n):
                ahead((kind, n))

            def ff_up(i):
                ahead(("gate", i))
                for f in range(2):
                    act.wait_ge(*at("job", "gate", i, f))
                    if i > 0:
                        act.wait_ge(*at("ff_product", i - 1, f))
                    act.activation(ff_g[:, f, :], bank("gate", i, f)[:, 0:S], ACT.Identity,
                                   scale=col("conv_w2", 2 * i + f), bias=col("conv_b", 2 * i + f))\
                        .then_inc(*mark("ff_newest", "gate", i, f))
                ahead(("val", i))
                for f in range(2):
                    act.wait_ge(*at("job", "val", i, f))
                    if i > 0:
                        act.wait_ge(*at("hidden_lo", "down", i - 1, f))
                    act.activation(ff_v[:, f, :], bank("val", i, f)[:, 0:S], ACT.Identity,
                                   scale=col("conv_w2", 22 + 2 * i + f), bias=col("conv_b", 22 + 2 * i + f))\
                        .then_inc(*mark("ff_newest", "val", i, f))
                    act.wait_ge(*at("dve_read", "gate", i, f))
                    act.activation(ff_s[:, f, :], ff_g[:, f, :], ACT.Silu).then_inc(*mark("ff_silu", i, f))
                for f in range(2):
                    act.wait_ge(*at("ff_product", i, f))
                    if i >= 2 and f == 0:
                        act.wait_ge(*at("chunk_used", SPLIT_OF[("down", i - 2)]))
                    act.activation(a_hi[:, 2 * (i % 2) + f, :], ff_v[:, f, :], ACT.Copy)\
                        .then_inc(*mark("hidden_hi", "down", i, f))

            def down(*key):
                ahead(key)

            def qkv(n):
                ahead(("qkv", n))
                if n == 1:
                    for m in range(2):
                        copy(("qkv", n, m), v2[:, m, :])

            def qk_a(t):
                job = ("qkv", QK_CHUNK[t], t % 2)
                act.wait_ge(*at("job", *job))
                if t >= 2:
                    act.wait_ge(*at("job", "qk_mean", t - 2))
                act.activation(work[:, t % 2, :], bank(*job)[:, 0:S], ACT.Square).then_inc(*mark("qk_square", t))
                act.wait_ge(*at("job", "qk_mean", t))
                if t >= 2:
                    act.wait_ge(*at("qk_normed", t - 2))
                act.activation(work[:, 2 + t % 2, :], bank("qk_mean", t)[:, 0:S], ACT.Sqrt, bias=cst("eps"))\
                    .then_inc(*mark("act_read", "qk_mean", t))

            def qk_b(t):
                if t < 2:
                    for n in range(2):
                        act.wait_ge(*at("turn", t, 1 + n))
                        act.dma_start(ak_dup[64 * (1 - n):64 * (1 - n) + 64, 2 * t + n, :],
                                      ak_dup[64 * n:64 * n + 64, 2 * t + n, :])\
                            .then_inc(*mark(f"k_doubled{2 * t + n}", 0, by=16))

            def att_a(h):
                act.wait_ge(*at("att_max", h))
                if h >= 2:
                    act.wait_ge(*at("job", "att_t", h - 2))
                for q in range(TT):
                    c = 4 * (h % 2) + q
                    act.activation(att_p[:, h % 2, q, :], bank("att", h)[:, q * S:(q + 1) * S], ACT.Exp,
                                   bias=small[:, 8 + c:9 + c], accum_out=small[:, 16 + c:17 + c])\
                        .then_inc(*(mark("act_read", "att", h) if q else mark("att_exp", h)))

            def att_b(h):
                act.wait_ge(*at("job", "att_t", h))
                if h >= 2:
                    act.wait_ge(*at("att_pv", h - 2))
                act.activation(att_pt[:, h % 2, :, :], bank("att_t", h)[:, :].rearrange("p (k s) -> p k s", k=TT),
                               ACT.Copy).then_inc(*mark("act_read", "att_t", h))

            def mlp_up(layer, i):
                ahead(("mlp_in", layer, i))
                for f in range(2):
                    job = ("mlp_in", layer, i, f)
                    act.wait_ge(*at("job", *job))
                    if i > 0:
                        act.wait_ge(*at("relu_squared", layer, i - 1, f))
                    act.activation(ff_g[:, f, :], bank(*job)[:, 0:S], ACT.Relu).then_inc(*mark("act_read", *job))
                for f in range(2):
                    act.wait_ge(*at("relu_squared", layer, i, f))
                    if i >= 2 and f == 0:
                        act.wait_ge(*at("chunk_used", SPLIT_OF[("mlp_out", layer, i - 2)]))
                    act.activation(a_hi[:, 2 * (i % 2) + f, :], ff_s[:, f, :], ACT.Copy)\
                        .then_inc(*mark("hidden_hi", "mlp_out", layer, i, f))

            def gla(n):
                if n == 0:
                    act.wait_ge(*at("w_gate_zero", 0))
                    for j in range(2):
                        act.dma_start(w_gate[16 * j:16 * j + 16, j, :], a["gla_w_gate_up_2"][0, j])\
                            .then_inc(*mark("w_gate_landed", j, by=16))
                ahead(("gla", n))
                for m in range(1 if n == 0 else 2):
                    job = ("gla", n, m)
                    if n == 0:
                        act.wait_ge(*at("job", *job))
                        act.activation(z_t[96:128, 0, :], bank(*job)[96:128, 0:S], ACT.Copy)\
                            .then_inc(*mark("act_read", *job))
                    elif n < 3:
                        copy(job, gq[:, 2 * (n - 1) + m, :], scale=float(P) ** -0.5)
                    elif n < 5:
                        copy(job, gk[:, 2 * (n - 3) + m, :])
                    elif n < 9:
                        copy(job, gv[:, m, (n - 5) * S:(n - 4) * S])
                    else:
                        copy(job, gr[:, 2 * (n - 9) + m, :], ACT.Silu)

            def gla_a(h):
                for n in range(2):
                    j = 2 * h + n
                    o = 4 * n
                    act.wait_ge(*at("job", "logit", j))
                    if h > 0:
                        act.wait_ge(*at("gated", j - 2))
                    act.activation(work[:, o, :], bank("logit", j)[:, 0:S], ACT.Abs, bias=col("b_gate", 4 * n + h))\
                        .then_inc(*mark("gate_act", j, 0))
                    act.wait_ge(*at("gate_act", j, 0))
                    act.activation(work[:, o, :], work[:, o, :], ACT.Exp, scale=-1.0).then_inc(*mark("gate_act", j, 1))
                    act.wait_ge(*at("gate_act", j, 1))
                    act.activation(work[:, o, :], work[:, o, :], ACT.Ln, bias=cst("one"))\
                        .then_inc(*mark("gate_act", j, 2))
                for n in range(2):
                    j = 2 * h + n
                    o = 4 * n
                    act.wait_ge(*at("gate_sum", j))
                    act.activation(work[:, o + 2, :], work[:, o, :], ACT.Exp, scale=1.0 / 16)\
                        .then_inc(*mark("gate_exp", j, 0))
                    act.activation(work[:, o + 3, :], work[:, o, :], ACT.Exp, scale=-1.0 / 16)\
                        .then_inc(*mark("gate_exp", j, 1))
                    act.wait_ge(*at("job", "kd_t", j))
                    if h > 0:
                        act.wait_ge(*at("job", "gla_kv", j - 2, 2))
                    act.activation(kd_tok[:, n, :, :], blocks3(bank("kd_t", j)[:, 0:S]), ACT.Copy)\
                        .then_inc(*mark("act_read", "kd_t", j))

            def gla_b(h):
                for m in range(2):
                    act.wait_ge(*at("job", "gla_o", h, m))
                    if h > 0:
                        act.wait_ge(*at("job", "gla_sum", h - 1))
                    act.activation(gla_sq[:, m, :], bank("gla_o", h, m)[:, 0:S], ACT.Square)\
                        .then_inc(*mark("gla_square", h, m))
                copy(("gla_sum", h), rstd[:, :], ACT.Sqrt, scale=1.0 / S, bias=cst("eps"))

            def finish():
                act.wait_ge(*at("w_lo", len(SPLITS) - 1))
                for j in (1, 3):
                    act.wait_ge(*at("job", "turned", j))
                    act.activation(y_rows[:, j // 2, 512:1024], bank("turned", j)[:, :], ACT.Copy)\
                        .then_inc(*mark("y_half", j))

            steps = {"setup": setup, "root": root, "scaled": scaled, "split": high, "in": take_in, "v_norm": v_norm,
                     "stick_a": stick_a, "stick_b": stick_b, "win_a": win_a, "win_b": win_b, "win_c": win_c,
                     "project": project, "ff_up": ff_up, "down": down, "qkv": qkv, "qk_a": qk_a, "qk_b": qk_b, "att_a": att_a,
                     "att_b": att_b, "mlp_up": mlp_up, "gla": gla, "gla_a": gla_a, "gla_b": gla_b, "finish": finish}
            for step in schedule():
                if step[0] in steps:
                    steps[step[0]](*step[1:])

        @block.vector
        def _(dve):
            def low(idx):
                for k in range(KT):
                    dve.wait_ge(*at("high", idx, k))
                    dve.tensor_tensor(h_lo[:, k, :], y_t[:, k, :], h_hi[:, k, :].bitcast(F32), ALU.subtract)\
                        .then_inc(*mark("low", idx, k))

            def setup():
                for j in range(len(ROWS)):
                    dve.wait_ge(*at("job", "rows", j))
                    o = COL_AT[next(iter(ROWS[j]))]
                    n = sum(ROWS[j].values())
                    dve.tensor_copy(cols[:, o:o + n], bank("rows", j)[:, 0:n]).then_inc(*mark("dve_read", "rows", j))
                    same(("cols", j), ("dve_read", "rows", j))
                for j in range(4):
                    dve.wait_ge(*at("job", "x", j))
                    dve.tensor_copy(x_t[:, 2 * j:2 * j + 2, :], bank("x", j)[:, :].rearrange("p (k s) -> p k s", k=2))\
                        .then_inc(*mark("dve_read", "x", j))
                    for k in (2 * j, 2 * j + 1):
                        same(("x_new", 0, k), ("dve_read", "x", j))
                dve.wait_ge(*at("pos_landed", 0))
                dve.wait_ge(*at("const_landed", 0))
                dve.tensor_copy(angle[:, 0, :], pos_i[:, :]).then_inc(*mark("reduce", 0))
                dve.wait_ge(*at("reduce", 0))
                dve.tensor_scalar(angle[:, 4, :], angle[:, 0, :], cst("inv_freq"), None, ALU.mult)\
                    .then_inc(*mark("reduce", 1))
                dve.wait_ge(*at("reduce", 1))
                dve.tensor_scalar(angle[:, 5, :], angle[:, 4, :], float(1 / (2 * np.pi)), MAGIC, ALU.mult, ALU.add)\
                    .then_inc(*mark("reduce", 2))
                dve.wait_ge(*at("reduce", 2))
                dve.tensor_scalar(angle[:, 5, :], angle[:, 5, :], -MAGIC, None, ALU.add).then_inc(*mark("reduce", 3))
                for j, part in enumerate(TWO_PI):
                    dve.wait_ge(*at("reduce", 3 + j))
                    dve.scalar_tensor_tensor(out=angle[:, 4, :], in0=angle[:, 5, :], scalar=-part,
                                             in1=angle[:, 4, :], op0=ALU.mult, op1=ALU.add)\
                        .then_inc(*mark("reduce", 4 + j))
                dve.wait_ge(*at("reduce", 6))
                dve.tensor_scalar(angle[:, 2, :], angle[:, 4, :], PI_BELOW, -PI_BELOW, ALU.min, ALU.max)\
                    .then_inc(*mark("angle", 0))
                dve.scalar_tensor_tensor(out=angle[:, 3, :], in0=angle[:, 4, :], scalar=-1.0, in1=angle[:, 4, :],
                                         op0=ALU.mult, op1=ALU.max).then_inc(*mark("reduce", 7))
                dve.wait_ge(*at("reduce", 7))
                dve.tensor_scalar(angle[:, 3, :], angle[:, 3, :], -1.0, float(np.pi / 2), ALU.mult, ALU.add)\
                    .then_inc(*mark("angle", 1))
                for g in range(4):
                    dve.wait_ge(*at("job", "w_sp", 0))
                    dve.tensor_tensor(w_sp_t[:, g, :], bank("w_sp", 0)[:, g * P:(g + 1) * P], cst("upto"), ALU.mult)\
                        .then_inc(*(mark("dve_read", "w_sp", 0) if g == 3 else mark("w_sp_masked", g)))

            def ada_step(p, q):
                r = LOAD_OF[("ada", p, q)]
                dve.wait_ge(*landed(r))
                if q == 0:
                    dve.wait_ge(*at("c_act", 0))
                    if p >= 2:
                        dve.wait_ge(*at("job", "mod", p - 2))
                for kk in range(2):
                    k = 2 * q + kk
                    src = wview(raw, r % RAW_SLOTS, 2)[:, kk, :]
                    if k == 0:
                        ins = dve.tensor_scalar(ada[:, p % 2, :], src, c_act[:, 0:1], None, ALU.mult)
                    else:
                        dve.wait_ge(*(at("ada_added", p, q - 1) if kk == 0 else at("ada_half", p, q)))
                        ins = dve.scalar_tensor_tensor(out=ada[:, p % 2, :], in0=src, scalar=c_act[:, k:k + 1],
                                                       in1=ada[:, p % 2, :], op0=ALU.mult, op1=ALU.add)
                    ins.then_inc(*(mark("ada_added", p, q) if kk else mark("ada_half", p, q)))
                if q == 3:
                    dve.wait_ge(*at("job", "mod", p))
                    dve.tensor_tensor(mod[:, KT * p:KT * p + KT], bank("mod", p)[:, 0:KT], col("b_ada", KT * p, KT),
                                      ALU.add).then_inc(*mark("dve_read", "mod", p))

            def gains(n):
                if n == 0:
                    dve.wait_ge(*at("dve_read", "mod", 1))
                    dve.scalar_tensor_tensor(out=gain[:, 0, :], in0=mod[:, 8:16], scalar=1.0, in1=col("g_mix", 0, KT),
                                             op0=ALU.add, op1=ALU.mult).then_inc(*mark("gains", 0))
                else:
                    dve.wait_ge(*at("dve_read", "mod", 5))
                    dve.scalar_tensor_tensor(out=gain[:, 1, :], in0=mod[:, 32:40], scalar=1.0,
                                             in1=col("g_ffn", 0, KT), op0=ALU.add, op1=ALU.mult)\
                        .then_inc(*mark("gains", 1))
                    dve.tensor_scalar(gain[:, 2, :], mod[:, 16:24], 1.0, None, ALU.add).then_inc(*mark("gains", 2))
                    dve.tensor_scalar(gain[:, 3, :], mod[:, 40:48], 1.0, None, ALU.add).then_inc(*mark("gains", 3))

            def root(i):
                dve.wait_ge(*at("act_read", "sum", i))
                dve.reciprocal(rstd[:, :], rstd[:, :]).then_inc(*mark("rstd", i))

            def scaled(i):
                dve.wait_ge(*at("rstd", i))
                g = {0: gain[:, 0, :], 1: gain[:, 1, :], 2: col("g_final", 0, KT), 3: col("norm_mix", 0, KT),
                     4: col("norm_mlp", 0, KT), 5: col("norm_mix", KT, KT), 6: col("norm_mlp", KT, KT),
                     7: col("final_norm", 0, KT)}[i]
                if i in (0, 1):
                    dve.wait_ge(*at("gains", i))
                dst = x_t if i == 2 else y_t
                for k in range(KT):
                    ins = dve.scalar_tensor_tensor(out=dst[:, k, :], in0=x_t[:, k, :], scalar=g[:, k:k + 1],
                                                   in1=rstd[:, :], op0=ALU.mult, op1=ALU.mult)
                    if i == 2:
                        ins.then_inc(*mark("x_new", 3, k))
                    elif i == 7:
                        ins.then_inc(*mark("y_normed", k))
                    elif i in (0, 1):
                        ins.then_inc(*mark("normed", i, k))
                        dve.wait_ge(*at("normed", i, k))
                        dve.tensor_scalar(y_t[:, k, :], y_t[:, k, :], mod[:, 24 * i + k:24 * i + k + 1], None, ALU.add)\
                            .then_inc(*mark("full", SET_OF_NORM[i], k))
                    else:
                        ins.then_inc(*mark("full", SET_OF_NORM[i], k))
                if i in SET_OF_NORM:
                    low(SET_OF_NORM[i])

            def rope(t):
                dve.wait_ge(*at("job", "rope", t))
                dve.wait_ge(*at("sine", 1))
                if t == 0:
                    dve.wait_ge(*at("square", 0, KT - 1))
                    dve.wait_ge(*at("job", "sum", 0))
                else:
                    dve.wait_ge(*at("roped", t - 1, 2))
                dve.tensor_tensor(work[:, 0, :], cqk[:, t, :], angle[:, 1, :], ALU.mult).then_inc(*mark("roped", t, 0))
                dve.tensor_tensor(work[:, 1, :], bank("rope", t)[:, 0:S], angle[:, 0, :], ALU.mult)\
                    .then_inc(*mark("dve_read", "rope", t))
                dve.wait_ge(*at("dve_read", "rope", t))
                if t < 3:
                    dve.wait_ge(*at("zeroed", 1))
                    dve.tensor_tensor(cqz[0:64, 2 * t, :], work[0:64, 0, :], work[0:64, 1, :], ALU.add)\
                        .then_inc(*mark("roped", t, 1))
                    dve.tensor_tensor(cqz[64:128, 2 * t + 1, :], work[64:128, 0, :], work[64:128, 1, :], ALU.add)\
                        .then_inc(*mark("roped", t, 2))
                else:
                    dve.tensor_tensor(ck_t[:, t - 3, :], work[:, 0, :], work[:, 1, :], ALU.add)\
                        .then_inc(*mark("roped", t, 2))

            def v_norm():
                dve.wait_ge(*at("act_read", "in", 4, 1))
                sq = work[:, 2:4, :]
                dve.tensor_tensor(sq, v_tok, v_tok, ALU.mult).then_inc(*mark("v_square", 0))
                dve.wait_ge(*at("v_square", 0))
                dve.tensor_reduce(small[:, 0:8], sq.rearrange("p t (g c) -> p (t g) c", c=HD), AX.X, ALU.add)\
                    .then_inc(*mark("v_sum", 0))
                dve.wait_ge(*at("v_root", 0))
                dve.reciprocal(small[:, 8:16], small[:, 8:16]).then_inc(*mark("v_rstd", 0))
                dve.wait_ge(*at("v_rstd", 0))
                dve.tensor_tensor(v_nrm.rearrange("p t (g c) -> p (t g) c", c=HD),
                                  v_tok.rearrange("p t (g c) -> p (t g) c", c=HD),
                                  small[:, 8:16].rearrange("p (n o) -> p n o", o=1).broadcast_to([P, 8, HD]), ALU.mult)\
                    .then_inc(*mark("v_normed", 0))

            def gate_mix():
                dve.wait_ge(*at("b_sp_landed", 3))
                for m in range(2):
                    dve.wait_ge(*at("job", "gated", m))
                    if m == 0:
                        dve.wait_ge(*at("low", 0, KT - 1))
                        dve.wait_ge(*at("act_read", "in", 3, 1))
                    dve.scalar_tensor_tensor(out=blocks3(work[:, 4 + m, :]), in0=blocks3(bank("gated", m)[:, 0:S]),
                                             scalar=col("g_sgu", m),
                                             in1=b_sp_b[:, m:m + 1, :].broadcast_to([P, TT, P]),
                                             op0=ALU.mult, op1=ALU.add).then_inc(*mark("dve_read", "gated", m))
                    dve.wait_ge(*at("dve_read", "gated", m))
                    dve.tensor_tensor(y_t[:, m, :], work[:, 4 + m, :], u_t[:, m, :], ALU.mult)\
                        .then_inc(*mark("full", 1, m))

            def diag(ap):
                return blocks3(ap)[:, 0:3:2, :]

            def before():
                return cst("before").rearrange("p (o c) -> p o c", o=1).broadcast_to([P, 2, P])

            def stick_a(h):
                dve.wait_ge(*at("stick_act", h, 2))
                dve.scalar_tensor_tensor(out=stick(h), in0=bank("stick", h)[:, 0:SP3], scalar=0.0, in1=stick(h),
                                         op0=ALU.max, op1=ALU.add).then_inc(*mark("stick_soft", h))
                dve.wait_ge(*at("stick_soft", h))
                dve.tensor_tensor(diag(stick(h)), diag(stick(h)), before(), ALU.mult).then_inc(*mark("stick_masked", h))

            def stick_b(h):
                dve.wait_ge(*at("act_read", "stick", h))
                dve.scalar_tensor_tensor(out=diag(stick(h)), in0=diag(stick(h)), scalar=1.0, in1=before(),
                                         op0=ALU.min, op1=ALU.mult).then_inc(*mark("stick_weight", h))

            def stick_c(m):
                dve.wait_ge(*at("job", "stick_o", m))
                dve.tensor_copy(y_t[:, 2 + m, :], bank("stick_o", m)[:, 0:S]).then_inc(*mark("dve_read", "stick_o", m))
                same(("full", 1, 2 + m), ("dve_read", "stick_o", m))

            def win_a(h):
                dve.wait_ge(*at("job", "win", h))
                o = CONST_AT["window"][0] + (h // 2) * SP3
                dve.tensor_tensor(win_p(h), bank("win", h)[:, 0:SP3], const[:, o:o + SP3], ALU.add)\
                    .then_inc(*mark("dve_read", "win", h))
                dve.wait_ge(*at("dve_read", "win", h))
                dve.tensor_reduce(small[:, 16 + 2 * h:17 + 2 * h], win_p(h)[:, 0:P], AX.X, ALU.max)\
                    .then_inc(*mark("win_red", h, 0))
                dve.tensor_reduce(small[:, 17 + 2 * h:18 + 2 * h], win_p(h)[:, P:SP3], AX.X, ALU.max)\
                    .then_inc(*mark("win_red", h, 1))
                dve.wait_ge(*at("win_red", h, 1))
                dve.tensor_scalar(small[:, 32 + 2 * h:34 + 2 * h], small[:, 16 + 2 * h:18 + 2 * h], -1.0, None,
                                  ALU.mult).then_inc(*mark("win_max", h))

            def win_b():
                mx, den, rel, top, tmp, tot, fac = (small[:, 16:28], small[:, 48:60], small[:, 64:76],
                                                    small[:, 80:84], small[:, 88:100], small[:, 84:88],
                                                    small[:, 100:112])
                groups = lambda ap: ap.rearrange("p (g x) -> p g x", g=3)
                spread = lambda ap: ap.rearrange("p (o x) -> p o x", o=1).broadcast_to([P, 3, 4])
                dve.tensor_reduce(top, mx.rearrange("p (g x) -> p x g", g=3), AX.X, ALU.max)\
                    .then_inc(*mark("win_mix", 0))
                dve.wait_ge(*at("win_mix", 0))
                dve.tensor_tensor(groups(rel), groups(mx), spread(top), ALU.subtract).then_inc(*mark("win_rel", 0))
                dve.wait_ge(*at("win_factor", 0))
                dve.tensor_tensor(tmp, rel, den, ALU.mult).then_inc(*mark("win_mix", 1))
                dve.wait_ge(*at("win_mix", 1))
                dve.tensor_reduce(tot, tmp.rearrange("p (g x) -> p x g", g=3), AX.X, ALU.add)\
                    .then_inc(*mark("win_mix", 2))
                dve.wait_ge(*at("win_mix", 2))
                dve.reciprocal(tot, tot).then_inc(*mark("win_mix", 3))
                dve.wait_ge(*at("win_mix", 3))
                dve.tensor_tensor(groups(fac), groups(rel), spread(tot), ALU.mult).then_inc(*mark("win_mix", 4))
                dve.wait_ge(*at("win_mix", 4))
                for h in range(6):
                    for q in range(TT):
                        pr = win_p(h)[:, 0:P] if q == 0 else win_p(h)[:, P:SP3]
                        dve.tensor_scalar(pr, pr, small[:, 100 + 2 * h + q:101 + 2 * h + q], None, ALU.mult)\
                            .then_inc(*mark("win_scaled", h, q))

            def win_d(m):
                dve.wait_ge(*at("job", "win_o", m))
                dve.tensor_copy(y_t[:, 5 + m, :], bank("win_o", m)[:, 0:S]).then_inc(*mark("dve_read", "win_o", m))
                same(("full", 1, 5 + m), ("dve_read", "win_o", m))

            def split(idx):
                low(idx)

            def project(kind, n):
                i = NEXT_NORM[kind]
                for m in range(2):
                    k = 2 * n + m
                    dve.wait_ge(*at("job", kind, n, m))
                    if kind == "out":
                        if k == 0:
                            dve.wait_ge(*at("gains", 2))
                        ins = dve.scalar_tensor_tensor(out=x_t[:, k, :], in0=bank(kind, n, m)[:, 0:S],
                                                       scalar=gain[:, 2, k:k + 1], in1=x_t[:, k, :],
                                                       op0=ALU.mult, op1=ALU.add)
                    else:
                        ins = dve.tensor_tensor(x_t[:, k, :], bank(kind, n, m)[:, 0:S], x_t[:, k, :], ALU.add)
                    ins.then_inc(*mark("dve_read", kind, n, m))
                    same(("x_new", i, k), ("dve_read", kind, n, m))

            def ff_up(i):
                for kind, buf, first in (("gate", ff_g, 0), ("val", ff_v, 22)):
                    for f in range(2):
                        c = bank(kind, i, f)
                        t = first + 2 * i + f
                        dve.wait_ge(*at("ff_newest", kind, i, f))
                        dve.scalar_tensor_tensor(out=buf[:, f, 1:S], in0=c[:, 0:S - 1], scalar=col("conv_w1", t),
                                                 in1=buf[:, f, 1:S], op0=ALU.mult, op1=ALU.add)\
                            .then_inc(*mark("ff_middle", kind, i, f))
                        dve.wait_ge(*at("ff_middle", kind, i, f))
                        dve.scalar_tensor_tensor(out=buf[:, f, 2:S], in0=c[:, 0:S - 2], scalar=col("conv_w0", t),
                                                 in1=buf[:, f, 2:S], op0=ALU.mult, op1=ALU.add)\
                            .then_inc(*mark("dve_read", kind, i, f))
                        if kind == "val":
                            dve.wait_ge(*at("dve_read", "val", i, f))
                            dve.wait_ge(*at("ff_silu", i, f))
                            dve.tensor_tensor(ff_v[:, f, :], ff_v[:, f, :], ff_s[:, f, :], ALU.mult)\
                                .then_inc(*mark("ff_product", i, f))
                for f in range(2):
                    hidden_low(ff_v[:, f, :], i, f, "down", i)

            def hidden_low(full, i, f, *key):
                dve.wait_ge(*at("hidden_hi", *key, f))
                b = 2 * (i % 2) + f
                dve.tensor_tensor(a_lo[:, b, :], full, a_hi[:, b, :].bitcast(F32), ALU.subtract)\
                    .then_inc(*mark("hidden_lo", *key, f))

            def mlp_up(layer, i):
                for f in range(2):
                    dve.wait_ge(*at("act_read", "mlp_in", layer, i, f))
                    if i > 0:
                        dve.wait_ge(*at("hidden_lo", "mlp_out", layer, i - 1, f))
                    dve.tensor_tensor(ff_s[:, f, :], ff_g[:, f, :], ff_g[:, f, :], ALU.mult)\
                        .then_inc(*mark("relu_squared", layer, i, f))
                for f in range(2):
                    hidden_low(ff_s[:, f, :], i, f, "mlp_out", layer, i)

            def add_down(*key):
                i = 2 if key[0] == "down" else 5 + 2 * key[1]
                for k in range(KT):
                    acc = psum[4 + k // 2][:, (k % 2) * S:(k % 2 + 1) * S]
                    dve.wait_ge(*at("summed", *key, k | 1))
                    if key[0] == "down":
                        ins = dve.scalar_tensor_tensor(out=x_t[:, k, :], in0=acc, scalar=gain[:, 3, k:k + 1],
                                                       in1=x_t[:, k, :], op0=ALU.mult, op1=ALU.add)
                    else:
                        ins = dve.tensor_tensor(x_t[:, k, :], acc, x_t[:, k, :], ALU.add)
                    ins.then_inc(*mark("x_new", i, k))
                    if k % 2:
                        same(("dve_read", "acc", *key, 4 + k // 2), ("x_new", i, k))

            def qkv(n):
                if n == 0:
                    dve.memset(aqz, 0.0).then_inc(*mark("aqz_zero", 0))
                    dve.tensor_scalar(small[:, 0:1], col("q_norm"), 0.125, None, ALU.mult).then_inc(*mark("q_gain", 0))

            def qk_a(t):
                job = ("qkv", QK_CHUNK[t], t % 2)
                b = t % 2
                dve.wait_ge(*at("act_read", "qk_mean", t))
                dve.reciprocal(work[:, 2 + b, :], work[:, 2 + b, :]).then_inc(*mark("qk_rstd", t))
                dve.wait_ge(*at("qk_rstd", t))
                dve.wait_ge(*at("q_gain", 0))
                if t >= 2:
                    dve.wait_ge(*at("job", "axial", t - 2))
                dve.scalar_tensor_tensor(out=qn[:, b, :], in0=bank(*job)[:, 0:S],
                                         scalar=col("k_norm") if t < 2 else small[:, 0:1],
                                         in1=work[:, 2 + b, :], op0=ALU.mult, op1=ALU.mult)\
                    .then_inc(*mark("dve_read", *job))
                same(("qk_normed", t), ("dve_read", *job))

            def qk_b(t):
                b = t % 2
                dve.wait_ge(*at("job", "axial", t))
                if t > 0:
                    dve.wait_ge(*at("turn", t - 1, 2))
                dve.tensor_tensor(work[:, 4, :], qn[:, b, :], cst("axial_cos"), ALU.mult).then_inc(*mark("turn", t, 0))
                dve.tensor_tensor(work[:, 5, :], bank("axial", t)[:, 0:S], cst("axial_sin"), ALU.mult)\
                    .then_inc(*mark("dve_read", "axial", t))
                dve.wait_ge(*at("dve_read", "axial", t))
                if t < 2:
                    for n in range(2):
                        r = slice(64 * n, 64 * n + 64)
                        dve.tensor_tensor(ak_dup[r, 2 * t + n, :], work[r, 4, :], work[r, 5, :], ALU.add)\
                            .then_inc(*mark("turn", t, 1 + n))
                else:
                    dve.wait_ge(*at("aqz_zero", 0))
                    for n in range(2):
                        r = slice(64 * n, 64 * n + 64)
                        dve.tensor_tensor(aqz[r, 2 * (t - 2) + n, :], work[r, 4, :], work[r, 5, :], ALU.add)\
                            .then_inc(*mark("turn", t, 1 + n))

            def att_a(h):
                o = 4 * (h % 2)
                dve.wait_ge(*at("job", "att", h))
                if h >= 2:
                    dve.wait_ge(*at("act_read", "att", h - 2))
                dve.tensor_reduce(small[:, 4 + 20 + o:6 + 20 + o], bank("att", h)[:, :]
                                  .rearrange("p (q s) -> p q s", q=TT), AX.X, ALU.max).then_inc(*mark("att_red", h))
                dve.wait_ge(*at("att_red", h))
                dve.tensor_scalar(small[:, 8 + o:10 + o], small[:, 24 + o:26 + o], -1.0, None, ALU.mult)\
                    .then_inc(*mark("att_max", h))

            def att_b(h):
                o = 4 * (h % 2)
                dve.wait_ge(*at("act_read", "att", h))
                dve.reciprocal(small[:, 32 + o:34 + o], small[:, 16 + o:18 + o]).then_inc(*mark("att_rden", h))
                dve.wait_ge(*at("att_rden", h))
                for q in range(TT):
                    pr = att_p[:, h % 2, q, :]
                    dve.tensor_scalar(pr, pr, small[:, 32 + o + q:33 + o + q], None, ALU.mult)\
                        .then_inc(*mark("att_scaled", h, q))

            def att_c(m):
                dve.wait_ge(*at("job", "att_o", m))
                dve.tensor_copy(y_t[:, m, :], bank("att_o", m)[:, 0:S]).then_inc(*mark("dve_read", "att_o", m))
                same(("full", 4, m), ("dve_read", "att_o", m))

            def gla(n):
                if n == 0:
                    dve.wait_ge(*at("full", 6, KT - 1))
                    dve.memset(ada[96:128, 0, :], 0.0).then_inc(*mark("w_gate_zero", 0))

            def gla_a(h):
                b = 2 * (h % 2)
                for n in range(2):
                    j, o = 2 * h + n, 4 * n
                    dve.wait_ge(*at("gate_act", j, 0))
                    if h > 0:
                        dve.wait_ge(*at("gate_exp", j - 2, 1))
                    dve.tensor_scalar(work[:, o + 1, :], bank("logit", j)[:, 0:S], col("b_gate", 4 * n + h), 0.0,
                                      ALU.add, ALU.min).then_inc(*mark("gate_min", j))
                    dve.wait_ge(*at("gate_min", j))
                    dve.wait_ge(*at("gate_act", j, 2))
                    dve.tensor_tensor(work[:, o + 1, :], work[:, o + 1, :], work[:, o, :], ALU.subtract)\
                        .then_inc(*mark("dve_read", "logit", j))
                    dve.wait_ge(*at("dve_read", "logit", j))
                    if n == 0:
                        ins = dve.tensor_tensor_scan(work[:, o, :], cst("scan_fwd"), work[:, o + 1, :], 0.0,
                                                     ALU.mult, ALU.add)
                    else:
                        ins = dve.tensor_tensor_scan(work[:, o, ::-1], cst("scan_bwd")[:, ::-1],
                                                     work[:, o + 1, ::-1], 0.0, ALU.mult, ALU.add)
                    ins.then_inc(*mark("gate_sum", j))
                for n in range(2):
                    j, o = 2 * h + n, 4 * n
                    dve.wait_ge(*at("gate_exp", j, 1))
                    dve.wait_ge(*at("act_read", "gla", 4, 1))
                    if h >= 2:
                        dve.wait_ge(*at("job", "gla_o", h - 2, 1))
                    dve.tensor_tensor(qe[:, b + n, :], gq[:, h, :], work[:, o + 2, :], ALU.mult)\
                        .then_inc(*mark("gla_qe", j))
                    dve.tensor_tensor(ke[:, b + n, :], gk[:, h, :], work[:, o + 3, :], ALU.mult)\
                        .then_inc(*mark("gla_ke", j))
                    dve.wait_ge(*at("gla_ke", j))
                    if h > 0:
                        dve.wait_ge(*at("job", "kd_t", j - 2))
                    last = GLA_CHUNK - 1 if n == 0 else 0
                    e = work[:, o + 2, :].rearrange("p (c t) -> p c t", c=NCH)[:, :, last:last + 1]
                    dve.tensor_tensor(kd[:, n, :].rearrange("p (c t) -> p c t", c=NCH),
                                      ke[:, b + n, :].rearrange("p (c t) -> p c t", c=NCH),
                                      e.broadcast_to([P, NCH, GLA_CHUNK]), ALU.mult).then_inc(*mark("gla_kd", j))
                for n in range(2):
                    j = 2 * h + n
                    dve.wait_ge(*at("job", "gla_a", j))
                    if n == 0 and h > 0:
                        dve.wait_ge(*at("job", "gla_o", h - 1, 1))
                        dve.wait_ge(*at("gla_masked", h - 1))
                    mask = cst(("chunk_fwd", "chunk_bwd")[n]).rearrange("p (o c) -> p o c", o=1)\
                        .broadcast_to([P, TT, P])
                    dst = (a_sum, a_tmp)[n]
                    dve.tensor_tensor(dst[:, 0, :, :], blocks3(bank("gla_a", j)[:, 0:S]), mask, ALU.mult)\
                        .then_inc(*mark("dve_read", "gla_a", j))
                dve.wait_ge(*at("dve_read", "gla_a", 2 * h + 1))
                dve.tensor_tensor(a_sum[:, 0, :, :], a_sum[:, 0, :, :], a_tmp[:, 0, :, :], ALU.add)\
                    .then_inc(*mark("gla_masked", h))
                for c in range(NCH - 1):
                    for n in range(2):
                        j, o = 2 * h + n, 4 * n
                        dve.wait_ge(*at("job", "gla_kv", j, c))
                        kv = bank("gla_kv", j, c)[:, 0:S]
                        if c == 0:
                            ins = dve.tensor_copy(state[:, n, 0, :], kv)
                        else:
                            t = c * GLA_CHUNK + GLA_CHUNK - 1 if n == 0 else (NCH - 1 - c) * GLA_CHUNK
                            dve.wait_ge(*at("dve_read", "gla_kv", j, c - 1))
                            ins = dve.scalar_tensor_tensor(out=state[:, n, c, :], in0=state[:, n, c - 1, :],
                                                           scalar=work[:, o + 2, t:t + 1], in1=kv,
                                                           op0=ALU.mult, op1=ALU.add)
                        ins.then_inc(*mark("dve_read", "gla_kv", j, c))
                for n in range(2):
                    same(("gated", 2 * h + n), ("dve_read", "gla_kv", 2 * h + 1, NCH - 2))

            def gla_b(h):
                dve.wait_ge(*at("act_read", "gla_sum", h))
                dve.reciprocal(rstd[:, :], rstd[:, :]).then_inc(*mark("gla_rstd", h))
                dve.wait_ge(*at("gla_rstd", h))
                for m in range(2):
                    dve.scalar_tensor_tensor(out=y_t[:, 2 * h + m, :], in0=bank("gla_o", h, m)[:, 0:S],
                                             scalar=col("out_norm", m), in1=rstd[:, :], op0=ALU.mult, op1=ALU.mult)\
                        .then_inc(*mark("dve_read", "gla_o", h, m))
                    dve.wait_ge(*at("dve_read", "gla_o", h, m))
                    dve.tensor_tensor(y_t[:, 2 * h + m, :], y_t[:, 2 * h + m, :], gr[:, 2 * h + m, :], ALU.mult)\
                        .then_inc(*mark("full", 7, 2 * h + m))

            def finish():
                dve.wait_ge(*at("w_lo", len(SPLITS) - 1))
                for j in (0, 2):
                    dve.wait_ge(*at("job", "turned", j))
                    dve.tensor_copy(y_rows[:, j // 2, 0:512], bank("turned", j)[:, :]).then_inc(*mark("y_rows", j))

            steps = {"setup": setup, "ada": ada_step, "gains": gains, "root": root, "scaled": scaled, "rope": rope,
                     "v_norm": v_norm, "gate_mix": gate_mix, "stick_a": stick_a, "stick_b": stick_b,
                     "stick_c": stick_c, "win_a": win_a, "win_b": win_b, "win_d": win_d, "split": split,
                     "project": project, "ff_up": ff_up, "mlp_up": mlp_up, "add_down": add_down, "qkv": qkv,
                     "qk_a": qk_a, "qk_b": qk_b, "att_a": att_a, "att_b": att_b, "att_c": att_c, "gla": gla,
                     "gla_a": gla_a, "gla_b": gla_b, "finish": finish}
            for step in schedule():
                if step[0] in steps:
                    steps[step[0]](*step[1:])

        @block.tensor
        def _(pe):
            seen = set()

            def operand(idx, k):
                if (idx, k) not in seen:
                    seen.add((idx, k))
                    pe.wait_ge(*at("low", idx, k))

            def weights(key):
                n = SPLIT_OF[key]
                pe.wait_ge(*at("w_lo", n))
                return n % SPLIT_SLOTS

            def used(key, event):
                same(("chunk_used", SPLIT_OF[key]), event)

            def three(dst, lhs, rhs, start, stop):
                pe.matmul(dst, lhs[0], rhs[0], start=start, stop=False, skip_group_check=True)
                pe.matmul(dst, lhs[0], rhs[1], start=False, stop=False, skip_group_check=True)
                return pe.matmul(dst, lhs[1], rhs[0], start=False, stop=stop, skip_group_check=True)

            def feature_tile(idx, key, m, width=S):
                slot = weights(key)
                dst = take(pe, *key, m)[:, 0:S]
                for k in range(KT):
                    operand(idx, k)
                    w = [wview(b, slot, KT)[:, k, m * P:m * P + P] for b in (w_hi, w_lo)]
                    ins = three(dst, w, (h_hi[:, k, :], h_lo[:, k, :]), k == 0, k == KT - 1)
                ins.then_inc(*mark("job", *key, m))

            def token_tile(idx, key, t):
                slot = weights(key)
                dst = take(pe, *key, t)[:, 0:S]
                for k in range(KT):
                    operand(idx, k)
                    h = [b[:, k, t * P:t * P + P] for b in (h_hi, h_lo)]
                    w = [wview(b, slot, KT)[:, k, :] for b in (w_hi, w_lo)]
                    ins = three(dst, h, w, k == 0, k == KT - 1)
                ins.then_inc(*mark("job", *key, t))

            def project_chunk(idx, key, tile=feature_tile, n=2):
                for m in range(n):
                    tile(idx, key, m)
                used(key, ("job", *key, n - 1))

            def setup():
                pe.wait_ge(*at("const_landed", 0))
                ident = cst("ident")
                for j in range(len(ROWS)):
                    n = sum(ROWS[j].values())
                    if j == 0:
                        pe.wait_ge(*at("rows_landed", "conv_b"))
                    pe.transpose(take(pe, "rows", j)[:, 0:n], rows[0:n, j, :], ident[0:n, 0:n])\
                        .then_inc(*mark("job", "rows", j))
                pe.wait_ge(*at("x_landed", 0))
                for j in range(4):
                    dst = take(pe, "x", j)
                    for kk in range(2):
                        for t in range(TT):
                            k = 2 * j + kk
                            ins = pe.transpose(dst[:, kk * S + t * P:kk * S + t * P + P],
                                               x_rows[:, t, k * P:k * P + P], ident)
                    ins.then_inc(*mark("job", "x", j))
                pe.wait_ge(*at("w_sp_landed", 0))
                dst = take(pe, "w_sp", 0)
                for g in range(4):
                    ins = pe.transpose(dst[:, g * P:(g + 1) * P], w_sp_r[:, g, :], ident)
                ins.then_inc(*mark("job", "w_sp", 0))

            def ada_step(p, q):
                if q == 3:
                    pe.wait_ge(*at("ada_added", p, 3))
                    dst = take(pe, "mod", p)
                    for k in range(KT):
                        ins = pe.matmul(dst[:, k:k + 1], ada[:, p % 2, k * P:(k + 1) * P], cst("ones")[:, 0:1],
                                        start=True, stop=True)
                    ins.then_inc(*mark("job", "mod", p))

            def root(i):
                dst = take(pe, "sum", i)[:, 0:S]
                for k in range(KT):
                    pe.wait_ge(*at("square", i, k))
                    ins = pe.matmul(dst, cst("ones"), work[:, k, :], start=(k == 0), stop=(k == KT - 1))
                ins.then_inc(*mark("job", "sum", i))

            def take_in(n):
                project_chunk(0, ("in", n), token_tile if n == 4 or n >= 8 else feature_tile)

            def rope(t):
                pe.wait_ge(*at("act_read", "in", t // 2, t % 2))
                pe.matmul(take(pe, "rope", t)[:, 0:S], cst("rope_swap"), cqk[:, t, :], start=True, stop=True)\
                    .then_inc(*mark("job", "rope", t))

            def gate_mix():
                pe.wait_ge(*at("v_normed", 0))
                pe.wait_ge(*at("dve_read", "w_sp", 0))
                for m in range(2):
                    dst = take(pe, "gated", m)
                    for g in range(2):
                        for t in range(TT):
                            f = (2 * m + g) * HD
                            ins = pe.matmul(dst[64 * g:64 * g + 64, t * P:t * P + P], v_nrm[:, t, f:f + HD],
                                            w_sp_t[:, 2 * m + g, :], start=True, stop=True, skip_group_check=True)
                    ins.then_inc(*mark("job", "gated", m))

            def stick_a(h):
                pe.wait_ge(*at("act_read", "in", 7, 1))
                dst = take(pe, "stick", h)
                k = bk_t[:, h // 2, :]
                pe.matmul(dst[:, 0:S], k[:, 0:P], bqz[:, h, :], start=True, stop=False, skip_group_check=True)
                pe.matmul(dst[:, S:SP3], k[:, P:S], bqz[:, h, P:S], start=False, stop=False, skip_group_check=True)\
                    .then_inc(*mark("job", "stick", h))

            def stick_b(h):
                pe.wait_ge(*at("stick_masked", h))
                s, dst = stick(h), bank("stick", h)
                pe.matmul(dst[:, 0:S], cst("tail"), s[:, 0:S], start=False, stop=False, skip_group_check=True)
                pe.matmul(dst[:, P:S], cst("tail_all"), s[:, S:SP3], start=False, stop=False, skip_group_check=True)
                pe.matmul(dst[:, S:SP3], cst("tail"), s[:, S:SP3], start=False, stop=True, skip_group_check=True)\
                    .then_inc(*mark("stick_tail", h))

            def values_out(dst, h, column, prob):
                o = 64 * (h % 2)
                pe.matmul(dst[o:o + 64, 0:S], vals[:, 0, column:column + HD], prob[:, 0:S], start=True, stop=False,
                          skip_group_check=True)
                return pe.matmul(dst[o:o + 64, P:S], vals[:, 1, column:column + HD], prob[:, S:SP3], start=False,
                                 stop=True, skip_group_check=True)

            def stick_c(m):
                dst = take(pe, "stick_o", m)
                for h in (2 * m, 2 * m + 1):
                    pe.wait_ge(*at("stick_weight", h))
                    pe.wait_ge(*at("act_read", "in", 10, 1))
                    ins = values_out(dst, h, h * HD, stick(h))
                ins.then_inc(*mark("job", "stick_o", m))

            def win_a(h):
                if h == 0:
                    pe.wait_ge(*at("roped", 5, 2))
                dst = take(pe, "win", h)
                pe.matmul(dst[:, 0:P], cqz[:, h, 0:P], ck_t[:, h // 2, 0:P], start=True, stop=True,
                          skip_group_check=True)
                pe.matmul(dst[:, P:SP3], cqz[:, h, P:S], ck_t[:, h // 2, :], start=True, stop=True,
                          skip_group_check=True).then_inc(*mark("job", "win", h))

            def win_c(h):
                pe.wait_ge(*at("win_scaled", h, 1))
                dst = take(pe, "win_t", h)
                for n in range(3):
                    ins = pe.transpose(dst[:, n * P:(n + 1) * P], win_p(h)[:, n * P:(n + 1) * P], cst("ident"))
                ins.then_inc(*mark("job", "win_t", h))

            def win_d(m):
                dst = take(pe, "win_o", m)
                for h in (2 * m, 2 * m + 1):
                    pe.wait_ge(*at("act_read", "win_t", h))
                    ins = values_out(dst, h, 6 * HD + h * HD, win_pt(h))
                ins.then_inc(*mark("job", "win_o", m))

            def project(kind, n):
                project_chunk(USES[kind], (kind, n))

            def ff_up(i):
                if i == 0:
                    ring["set"] = range(4)
                project_chunk(2, ("gate", i))
                project_chunk(2, ("val", i))

            def mlp_up(layer, i):
                if i == 0:
                    ring["set"] = range(4)
                project_chunk(5 + 3 * layer, ("mlp_in", layer, i))

            def down(*key):
                i = key[-1]
                last = i == (FF_STEPS if key[0] == "down" else MLP_STEPS) - 1
                slot = weights(key)
                for f in range(2):
                    pe.wait_ge(*at("hidden_lo", *key, f))
                for k in range(KT):
                    b = 4 + k // 2
                    if i == 0 and k % 2 == 0 and b in ring["last"]:
                        pe.wait_ge(*evacuated(*ring["last"][b]))
                    dst = psum[b][:, (k % 2) * S:(k % 2 + 1) * S]
                    for f in range(2):
                        w = [wview(x, slot, 2)[:, f, k * P:k * P + P] for x in (w_hi, w_lo)]
                        n = 2 * (i % 2) + f
                        ins = three(dst, w, (a_hi[:, n, :], a_lo[:, n, :]), i == 0 and k % 2 == 0 and f == 0,
                                    last and f == 1)
                    if last:
                        ins.then_inc(*mark("summed", *key[:-1], k))
                    elif k == KT - 1:
                        ins.then_inc(*mark("added", *key))
                used(key, ("summed", *key[:-1], KT - 1) if last else ("added", *key))

            def add_down(*key):
                for b in range(4, 8):
                    ring["last"][b] = ("acc", *key, b)
                ring["set"] = range(8)

            def qkv(n):
                project_chunk(3, ("qkv", n), token_tile if n == 1 else feature_tile)

            def qk_a(t):
                pe.wait_ge(*at("qk_square", t))
                pe.matmul(take(pe, "qk_mean", t)[:, 0:S], cst("head_mean"), work[:, t % 2, :], start=True, stop=True)\
                    .then_inc(*mark("job", "qk_mean", t))

            def qk_b(t):
                pe.wait_ge(*at("qk_normed", t))
                pe.matmul(take(pe, "axial", t)[:, 0:S], cst("axial_swap"), qn[:, t % 2, :], start=True, stop=True)\
                    .then_inc(*mark("job", "axial", t))

            def att_a(h):
                if h == 0:
                    pe.wait_ge(*at("turn", 9, 2))
                    for g in range(4):
                        pe.wait_ge(*at(f"k_doubled{g}", 0))
                dst = take(pe, "att", h)
                for q in range(TT):
                    ins = pe.matmul(dst[:, q * S:(q + 1) * S], aqz[:, h, q * P:q * P + P], ak_dup[:, h // 4, :],
                                    start=True, stop=True, skip_group_check=True)
                ins.then_inc(*mark("job", "att", h))

            def att_b(h):
                pe.wait_ge(*at("att_scaled", h, 1))
                dst = take(pe, "att_t", h)
                for q in range(TT):
                    for k in range(TT):
                        ins = pe.transpose(dst[:, k * S + q * P:k * S + q * P + P],
                                           att_p[:, h % 2, q, k * P:k * P + P], cst("ident"))
                ins.then_inc(*mark("job", "att_t", h))

            def att_o(h):
                pe.wait_ge(*at("act_read", "att_t", h))
                m = h // 2
                dst = take(pe, "att_o", m) if h % 2 == 0 else psum[banks[("att_o", m)]]
                o = 64 * (h % 2)
                g = h // 4
                for k in range(TT):
                    ins = pe.matmul(dst[o:o + 64, 0:S], v2[:, k, g * HD:g * HD + HD], att_pt[:, h % 2, k, :],
                                    start=(k == 0), stop=(k == TT - 1), skip_group_check=True)
                if h % 2:
                    ins.then_inc(*mark("job", "att_o", m))
                    same(("att_pv", h), ("job", "att_o", m))
                else:
                    ins.then_inc(*mark("att_pv", h))

            def gla(n):
                if n == 0:
                    project_chunk(6, ("gla", 0), n=1)
                else:
                    project_chunk(6, ("gla", n), token_tile if 5 <= n < 9 else feature_tile)

            def gla_a(h):
                for n in range(2):
                    j = 2 * h + n
                    if j == 0:
                        pe.wait_ge(*at("w_gate_landed", 1))
                        pe.wait_ge(*at("act_read", "gla", 0, 0))
                    pe.matmul(take(pe, "logit", j)[:, 0:S], w_gate[:, n, h * P:h * P + P], z_t[96:128, 0, :],
                              start=True, stop=True).then_inc(*mark("job", "logit", j))
                b = 2 * (h % 2)
                for n in range(2):
                    j = 2 * h + n
                    pe.wait_ge(*at("gla_ke", j))
                    dst = take(pe, "gla_a", j)
                    for t in range(TT):
                        ins = pe.matmul(dst[:, t * P:t * P + P], ke[:, b + n, t * P:t * P + P],
                                        qe[:, b + n, t * P:t * P + P], start=True, stop=True, skip_group_check=True)
                    ins.then_inc(*mark("job", "gla_a", j))
                    pe.wait_ge(*at("gla_kd", j))
                    dst = take(pe, "kd_t", j)
                    for t in range(TT):
                        ins = pe.transpose(dst[:, t * P:t * P + P], kd[:, n, t * P:t * P + P], cst("ident"))
                    ins.then_inc(*mark("job", "kd_t", j))
                for c in range(NCH - 1):
                    for n in range(2):
                        j = 2 * h + n
                        at_c = c if n == 0 else NCH - 1 - c
                        t, o = at_c // 2, 64 * (at_c % 2)
                        pe.wait_ge(*at("act_read", "kd_t", j))
                        pe.wait_ge(*at("act_read", "gla", 8, 1))
                        pe.matmul(take(pe, "gla_kv", j, c)[:, 0:S], kd_tok[o:o + 64, n, t, :],
                                  gv[o:o + 64, t, h * S:(h + 1) * S], start=True, stop=True)\
                            .then_inc(*mark("job", "gla_kv", j, c))

            def gla_b(h):
                b = 2 * (h % 2)
                pe.wait_ge(*at("gla_masked", h))
                pe.wait_ge(*at("gated", 2 * h + 1))
                for m in range(2):
                    dst = take(pe, "gla_o", h, m)
                    for t in range(TT):
                        pe.matmul(dst[:, t * P:t * P + P], gv[:, t, h * S + m * P:h * S + m * P + P],
                                  a_sum[:, 0, t, :], start=(t == 0), stop=False, skip_group_check=True)
                    for c in range(NCH - 1):
                        for n in range(2):
                            o = GLA_CHUNK * (c + 1 if n == 0 else NCH - 2 - c)
                            ins = pe.matmul(dst[:, o:o + GLA_CHUNK], state[:, n, c, m * P:m * P + P],
                                            qe[:, b + n, o:o + GLA_CHUNK], start=False,
                                            stop=(c == NCH - 2 and n == 1), skip_group_check=True)
                    ins.then_inc(*mark("job", "gla_o", h, m))
                dst = take(pe, "gla_sum", h)[:, 0:S]
                for m in range(2):
                    pe.wait_ge(*at("gla_square", h, m))
                    ins = pe.matmul(dst, cst("ones"), gla_sq[:, m, :], start=(m == 0), stop=(m == 1))
                ins.then_inc(*mark("job", "gla_sum", h))

            def finish():
                for j in range(4):
                    dst = take(pe, "turned", j)
                    for n in range(4):
                        k = 4 * (j % 2) + n
                        pe.wait_ge(*at("y_normed", k))
                        ins = pe.transpose(dst[:, n * P:n * P + P], y_t[:, k, (j // 2) * P:(j // 2) * P + P],
                                           cst("ident"))
                    ins.then_inc(*mark("job", "turned", j))

            steps = {"setup": setup, "ada": ada_step, "root": root, "in": take_in, "rope": rope,
                     "gate_mix": gate_mix, "stick_a": stick_a, "stick_b": stick_b, "stick_c": stick_c,
                     "win_a": win_a, "win_c": win_c, "win_d": win_d, "project": project, "ff_up": ff_up,
                     "mlp_up": mlp_up, "down": down, "add_down": add_down, "qkv": qkv, "qk_a": qk_a, "qk_b": qk_b,
                     "att_a": att_a, "att_b": att_b, "att_o": att_o, "gla": gla, "gla_a": gla_a, "gla_b": gla_b,
                     "finish": finish}
            for step in schedule():
                if step[0] in steps:
                    steps[step[0]](*step[1:])
    return marks, banks


_INS = ['x', 'c', 'positions', 'w_ada', 'b_ada', 'g_mix', 'w_in', 'g_sgu', 'w_sp', 'b_sp', 'w_out', 'g_ffn', 'w_up',
        'conv_w', 'conv_b', 'w_down', 'g_final', 'norm_mix_2', 'norm_mlp_2', 'attn_w_qkv_2', 'attn_q_norm_2',
        'attn_k_norm_2', 'attn_w_o_2', 'gla_w_in_2', 'gla_w_gate_up_2', 'gla_b_gate_2', 'gla_out_norm_2',
        'gla_w_o_2', 'mlp_w_in_2', 'mlp_w_out_2', 'final_norm_2']


def kernel(**inputs):
    import concourse.bacc as _bacc
    from concourse.bass_utils import run_bass_kernel_spmd as _run

    arrays = {f"in_{name}_dram": np.ascontiguousarray(inputs[name]) for name in _INS}
    arrays["in_const_dram"] = constants()
    known = None
    for _ in range(2):
        nc = _bacc.Bacc("TRN2", target_bir_lowering=False, num_devices=1)
        a = {name[3:-5]: nc.dram_tensor(name, v.shape, mybir.dt.from_np(v.dtype), kind="ExternalInput").ap()
             for name, v in arrays.items()}
        out = nc.dram_tensor("out_0_dram", (1, S, D), F32, kind="ExternalOutput").ap()
        known = build(nc, a, out, known)
    r = _run(nc, [arrays], core_ids=[0])
    return r.results[0]["out_0_dram"]
```

```python
from contextlib import ExitStack

import numpy as np

import concourse.bass as bass
from concourse import mybir

ALU = mybir.AluOpType
ACT = mybir.ActivationFunctionType
AX = mybir.AxisListType
F32 = mybir.dt.float32
F32R = mybir.dt.float32r

P = 128
D = 1024
S = 256
KT = D // P
TT = S // P
HD = 64
EPS = 1e-6
D_FF = 2816
FF_STEPS = D_FF // S
MLP_STEPS = 4 * D // S
GLA_IN = 3104
CHUNK = KT * S
RAW_SLOTS = 4
SPLIT_SLOTS = 3
SP3 = 3 * P
MAGIC = 12582912.0
TWO_PI = (6.28125, 0.0019350051879882812, 3.0199159819e-07)
PI_BELOW = 3.1415925

IN_COLS = [1664, 1920, 2176, 0, 256, 512, 768, 1024, 1280, (1536, 2432), 2560]
QKV = [0, 1, 2, 4, 5, 3]
GLA = [12, 0, 1, 2, 3, 4, 5, 6, 7, 8, 9, 10, 11]

CONST_W = {
    "ident": P, "ones": P, "tail": P, "tail_all": P, "before": P, "window": 3 * SP3, "upto": P,
    "rope_swap": P, "axial_swap": P, "axial_cos": S, "axial_sin": S, "head_mean": P,
    "head_pick": 2, "after": S, "twice": S, "scan_fwd": S, "scan_bwd": S, "inv_freq": 1, "eps": 1, "one": 1,
}
CONST_AT, CONST_COLS = {}, 0
for _name, _w in CONST_W.items():
    CONST_AT[_name] = (CONST_COLS, _w)
    CONST_COLS += _w

ROWS = [
    {"c": 8, "b_ada": 48, "g_mix": 8, "g_ffn": 8, "g_final": 8, "g_sgu": 2},
    {"norm_mix": 16, "norm_mlp": 16, "final_norm": 8, "b_gate": 8, "out_norm": 2, "q_norm": 1, "k_norm": 1},
    {"conv_w0": 22 * 2, "conv_w1": 22 * 2},
    {"conv_w2": 22 * 2, "conv_b": 22 * 2},
]
COL_AT, N_COLS = {}, 0
for _rows in ROWS:
    for _name, _n in _rows.items():
        COL_AT[_name] = N_COLS
        N_COLS += _n


def constants():
    f = np.float32
    r = np.arange(P)
    k, q = r[:, None], r[None, :]
    t = np.arange(S)
    out = {}
    out["ident"] = (k == q)
    out["ones"] = np.ones((P, P))
    out["tail"] = -(k >= q).astype(f)
    out["tail_all"] = -np.ones((P, P))
    out["before"] = (k < q)
    win = []
    for dil in (1, 4, 16):
        for qb, width in ((0, P), (1, S)):
            back = (qb * P + r)[:, None] - np.arange(width)[None, :]
            ok = (back >= 0) & (back % dil == 0) & (back <= 128 * dil)
            win.append(np.where(ok, 0.0, -1e30))
    out["window"] = np.concatenate(win, 1)
    out["upto"] = (k <= q)
    for name, w in (("rope_swap", 32), ("axial_swap", 16)):
        low = (q % (2 * w)) < w
        out[name] = np.where(low & (k == q + w), -1.0, 0.0) + np.where(~low & (k == q - w), 1.0, 0.0)
    inv = (f(10000.0) ** (-np.arange(0, 32, 2, dtype=f) / f(32))).astype(f)
    pos = np.where((r % 64 < 32)[:, None], (t // 64)[None, :], (t % 64)[None, :]).astype(f)
    ang = pos * inv[r % 16][:, None]
    out["axial_cos"], out["axial_sin"] = np.cos(ang), np.sin(ang)
    out["head_mean"] = (k // HD == q // HD) / HD
    out["head_pick"] = (r[:, None] // HD == np.arange(2)[None, :]) / HD
    out["after"], out["twice"] = np.tile(k > q, (1, TT)), np.tile(1.0 + (k == q), (1, TT))
    out["scan_fwd"] = np.broadcast_to(t % P != 0, (P, S))
    out["scan_bwd"] = np.broadcast_to(t % P != P - 1, (P, S))
    inv = (f(10000.0) ** (-np.arange(0, HD, 2, dtype=f) / f(HD))).astype(f)
    out["inv_freq"] = inv[r % 32][:, None]
    out["eps"] = np.full((P, 1), EPS)
    out["one"] = np.ones((P, 1))
    return np.ascontiguousarray(np.concatenate([np.asarray(out[n], f) for n in CONST_W], 1))


def weight_stream():
    ada = [("ada", p, q) for p in range(2, 6) for q in range(4)]
    s = [("ada", p, q) for p in range(2) for q in range(4)]
    for n in range(11):
        s.append(("in", n))
        if n >= 3:
            s.append(ada.pop(0))
    s += [("out", 0), ("out", 1)] + ada + [("out", 2), ("out", 3)]
    for i in range(FF_STEPS + 1):
        s += [("gate", i), ("val", i)] if i < FF_STEPS else []
        s += [("down", i - 1)] if i > 0 else []
    s += [("qkv", n) for n in range(6)]
    s += [("wo", n) for n in range(4)]
    for layer in range(2):
        if layer == 1:
            s += [("gla", n) for n in range(13)]
            s += [("gla_out", n) for n in range(4)]
        for i in range(MLP_STEPS + 1):
            s += [("mlp_in", layer, i)] if i < MLP_STEPS else []
            s += [("mlp_out", layer, i - 1)] if i > 0 else []
    return s


STREAM = weight_stream()
LOAD_OF = {key: n for n, key in enumerate(STREAM)}
SPLITS = [key for key in STREAM if key[0] != "ada"]
SPLIT_OF = {key: n for n, key in enumerate(SPLITS)}


def schedule():
    ada = [("ada", p, q) for p in range(2, 6) for q in range(4)]
    s = [("setup",)] + [("ada", p, q) for p in range(2) for q in range(4)] + [("gains", 0)]
    s += [("root", 0), ("scaled", 0)]
    extra = {1: [("rope", 0)], 2: [("rope", 1), ("rope", 2)], 3: [("rope", 3), ("rope", 4)],
             4: [("rope", 5), ("v_norm",)], 8: [("gate_mix",), ("stick_a", 0)], 9: [("win_a", 0), ("stick_a", 1)]}
    for n in range(11):
        s.append(("in", n))
        s += extra.get(n, [])
        if n >= 3:
            s.append(ada.pop(0))
    s += [("stick_b", 0), ("win_a", 1), ("stick_a", 2), ("stick_b", 1), ada.pop(0), ("win_a", 2), ("stick_c", 0),
          ("stick_a", 3), ("stick_b", 2), ada.pop(0), ("win_a", 3), ("stick_a", 4), ("stick_b", 3), ada.pop(0),
          ("stick_c", 1), ("win_a", 4), ("stick_a", 5), ("stick_b", 4), ada.pop(0), ("win_a", 5), ("stick_b", 5),
          ("win_b",), ada.pop(0), ("stick_c", 2)]
    for m in range(3):
        s += [("win_c", 2 * m), ("win_c", 2 * m + 1), ada.pop(0), ("win_d", m)]
    s += [("gains", 1)] + [("split", 1, k) for k in range(KT)]
    s += [("project", "out", n) for n in range(4)]
    s += [("root", 1), ("scaled", 1)]
    for i in range(FF_STEPS + 1):
        s += [("ff_up", i)] if i < FF_STEPS else []
        s += [("down", "down", i - 1)] if i > 0 else []
    s += [("add_down", "down"), ("unscaled", 3)] + [("squares", 2, n) for n in range(4)] + [("tree", 2)]
    s += [("qkv", 0), ("total", 2), ("rescale", 2)] + [("squares", 3, n) for n in range(4)] + [("tree", 3)]
    s += [("q_a", 0), ("q_a", 1), ("qkv", 1), ("q_b", 0), ("q_b", 1), ("q_a", 2), ("q_a", 3), ("total", 3),
          ("r_cols", 3), ("qkv", 2), ("q_b", 2), ("q_b", 3), ("q_a", 4), ("q_a", 5), ("qkv", 3), ("k_a", 0),
          ("k_a", 1), ("q_b", 4), ("q_b", 5), ("qkv", 4), ("k_b", 0), ("k_b", 1), ("qkv", 5), ("k_c", 0),
          ("k_c", 1), ("q_a", 6), ("q_a", 7), ("q_b", 6), ("q_b", 7), ("q_scale",)]
    s += [("att_a", 0), ("att_a", 1)]
    for h in range(16):
        s += [("att_a", h + 2)] if h < 14 else []
        s += [("att_b", h)] + ([("att_o", h - 1)] if h else [])
        s += [("att_c", h // 2 - 1), ("split", 4, h // 2 - 1)] if h >= 2 and h % 2 == 0 else []
    s += [("att_o", 15), ("att_c", 7), ("split", 4, 7)]
    for n in range(4):
        s += [("project", "wo", n)] + ([("squares", 4, n)] if n < 3 else [])
    for layer in range(2):
        i = 4 + 2 * layer
        if layer == 1:
            s += [("unscaled", 5)] + [("squares", 5, n) for n in range(4)] + [("tree", 5)]
            s += [("gla", 0), ("gla", 1), ("total", 5), ("r_cols", 5)]
            s += [("gla_in", 0), ("gla_in", 1), ("gla", 2), ("gla_in", 2), ("gate", 0), ("gla", 3), ("gla_in", 3),
                  ("gate", 1), ("gla", 4), ("gla_in", 4), ("gate", 2), ("gla", 5), ("gla_in", 5), ("gate", 3)]
            s += [("keys", 0), ("keys", 1), ("gla", 6), ("gla_in", 6), ("mix", 0), ("keys", 2), ("gla", 7),
                  ("gla_in", 7), ("mix", 1), ("keys", 3), ("gla", 8), ("gla_in", 8), ("gla", 9), ("gla_in", 9),
                  ("mixed", 0), ("mix", 2), ("gla", 10), ("gla_in", 10), ("head_sum", 0), ("mixed", 1), ("mix", 3),
                  ("gla", 11), ("head_sum", 1), ("head_norm", 0), ("head_norm", 1), ("mixed", 2), ("gla_in", 11),
                  ("mixed", 3), ("head_sum", 2), ("gla", 12), ("head_sum", 3), ("gla_in", 12),
                  ("head_norm", 2), ("head_norm", 3)]
            s += [("split", 7, k) for k in range(KT)]
            for n in range(4):
                s += [("project", "gla_out", n)] + ([("squares", 6, n)] if n < 3 else [])
        s += [("unscaled", i), ("squares", i, 3), ("tree", i), ("mlp_up", layer, 0), ("total", i)]
        for n in range(MLP_STEPS + 1):
            s += [("mlp_up", layer, n)] if 0 < n < MLP_STEPS else []
            s += [("mlp_act", layer, n)] if n < MLP_STEPS else []
            s += [("down", "mlp_out", layer, n - 1)] if n > 0 else []
        s += [("add_down", "mlp_out", layer)]
    s += [("root", 7), ("scaled", 7), ("finish",)]
    return s


NEXT_NORM = {"out": 1, "down": 2, "wo": 4, "gla_out": 6}
X_OF_NORM = {3: 2, 4: 4, 5: 5, 6: 6}
SET_OF_NORM = {0: 0, 1: 2, 3: 3, 4: 5, 5: 6, 6: 8}
Q_CHUNK = [0, 0, 1, 1, 2, 2, 5, 5]
LAST_USE = {0: ("in", 10), 1: ("out", 3), 2: ("val", FF_STEPS - 1), 3: ("qkv", 5), 4: ("wo", 3),
            5: ("mlp_in", 0, MLP_STEPS - 1), 6: ("gla", 12), 7: ("gla_out", 3), 8: ("mlp_in", 1, MLP_STEPS - 1)}
FIRST_USE = {("in", 0), ("out", 0), ("gate", 0), ("qkv", 0), ("wo", 0), ("mlp_in", 0, 0), ("gla_out", 0), ("mlp_in", 1, 0)}
USES = {"in": 0, "out": 1, "gate": 2, "val": 2, "qkv": 3, "wo": 4, "gla": 6, "gla_out": 7}


def build(nc, a, out, known):
    marks, banks, counts, sems = {}, {}, {}, {}
    ctx = ExitStack()
    with ctx:
        def sb(name, shape, dt=F32):
            return ctx.enter_context(nc.sbuf_tensor(name, shape, dt))

        def sem(name):
            if name not in sems:
                sems[name] = ctx.enter_context(nc.semaphore(name))
            return sems[name]

        def mark(name, *event, by=1):
            counts[name] = counts.get(name, 0) + by
            assert (name, *event) not in marks, (name, event)
            marks[(name, *event)] = (name, counts[name])
            return sem(name), by

        def same(event, as_event):
            assert event not in marks, event
            marks[event] = marks[as_event]

        def at(*event):
            name, value = (event[0], 1) if known is None else known[0][event]
            return sem(name), value

        raw = sb("raw", [P, RAW_SLOTS, CHUNK])
        w_hi = sb("w_hi", [P, SPLIT_SLOTS, CHUNK], F32R)
        w_lo = sb("w_lo", [P, SPLIT_SLOTS, CHUNK], F32R)
        const = sb("const", [P, CONST_COLS])
        rows = sb("rows", [P, len(ROWS), P])
        cols = sb("cols", [P, N_COLS])
        mod = sb("mod", [P, 48])
        gain = sb("gain", [P, 4, KT])
        c_act = sb("c_act", [P, KT])
        ada = sb("ada", [P, 2, D])
        x_t = sb("x_t", [P, KT, S])
        h_hi = sb("h_hi", [P, KT, S], F32R)
        h_lo = sb("h_lo", [P, KT, S], F32R)
        y_t = sb("y_t", [P, KT, S])
        rstd = sb("rstd", [P, S])
        a_hi = sb("a_hi", [P, 4, S], F32R)
        a_lo = sb("a_lo", [P, 4, S], F32R)
        work = sb("work", [P, 8, S])
        arena = sb("arena", [P, 48 * S])
        rstd_x = sb("rstd_x", [P, S])
        r_col = sb("r_col", [P, TT])
        q_mean = sb("q_mean", [P, TT, 16])
        gain_qkv = sb("gain_qkv", [P, KT])
        pos_i = sb("pos_i", [P, S], mybir.dt.int32)
        small = sb("small", [P, P])
        psum = [ctx.enter_context(nc.psum_tensor(f"psum{b}", [P, 512], F32)) for b in range(8)]

        def norm_gain(i):
            return {3: gain_qkv[:, :], 4: col("norm_mlp", 0, KT), 5: col("norm_mix", KT, KT),
                    6: col("norm_mlp", KT, KT)}[i]

        def cst(name):
            o, w = CONST_AT[name]
            return const[:, o:o + w]

        def col(name, i=0, n=1):
            return cols[:, COL_AT[name] + i:COL_AT[name] + i + n]

        def area(first, n):
            return arena[:, first * S:(first + n) * S].rearrange("p (n s) -> p n s", s=S)

        def blocks3(ap):
            return ap.rearrange("p (n c) -> p n c", c=P)

        ring = {"n": 0, "last": {}, "set": range(8)}

        def evacuated(*job):
            name = "act_read" if known is not None and ("act_read", *job) in known[0] else "dve_read"
            return at(name, *job)

        def take(pe, *job):
            b = ring["set"][ring["n"] % len(ring["set"])]
            ring["n"] += 1
            if b in ring["last"]:
                pe.wait_ge(*evacuated(*ring["last"][b]))
            ring["last"][b] = job
            banks[job] = b
            return psum[b]

        def bank(*job):
            return psum[0 if known is None else known[1][job]]

        u_t, v_tok, v_nrm = area(0, 2), area(2, 2), area(4, 2)
        bqz, bk_t = area(6, 6), area(12, 3)
        vals = arena[:, 15 * S:21 * S].rearrange("p (t c) -> p t c", t=TT)
        cqk, cqz, ck_t = area(21, 6), area(27, 6), area(33, 3)
        w_sp_r = arena[:, 21 * S:23 * S].rearrange("p (g s) -> p g s", g=4)
        w_sp_t = arena[:, 36 * S:38 * S].rearrange("p (g s) -> p g s", g=4)
        angle = area(38, 6)
        b_sp_b = arena[:, 45 * S:46 * S].rearrange("p (m s) -> p m s", m=2)

        def stick(h):
            return arena[:, 21 * S + (h % 4) * SP3:21 * S + (h % 4 + 1) * SP3]

        def win_p(h):
            return arena[:, 36 * S + h * SP3:36 * S + (h + 1) * SP3]

        def win_pt(h):
            o = h * SP3 if h < 4 else 27 * S + (h - 4) * SP3
            return arena[:, o:o + SP3]

        ff_g, ff_v, ff_s = area(0, 2), area(2, 2), area(4, 2)
        aqz, ak_dup, v2 = area(6, 16), area(22, 4), area(26, 2)
        att_p = area(28, 6).rearrange("p (b q) s -> p b q s", b=3)
        att_pt = area(34, 4).rearrange("p (b q) s -> p b q s", b=2)
        qx, q_sq, turned = area(38, 4), area(42, 2), area(44, 2)
        k_x, k_rms = area(46, 2), area(0, 2)
        gq, gk, gr, z_t = area(6, 4), area(10, 4), area(22, 8), area(30, 1)
        gv = arena[:, 14 * S:22 * S].rearrange("p (t c) -> p t c", t=TT)
        qe = area(31, 8).rearrange("p (h n) s -> p h n s", n=2)
        ke = area(39, 8).rearrange("p (h n) s -> p h n s", n=2)
        pair = area(0, 4).rearrange("p (b t) s -> p b t s", b=2)
        gla_sq, mid = work[:, 4:8, :], small[:, 0:4].rearrange("p (n t) -> p n t", n=2)
        w_gate = ada[96:128, 0, :].rearrange("p (n e) -> p n e", n=2)
        x_rows = work[:, :, :].rearrange("p n s -> p (n s)").rearrange("p (t c) -> p t c", t=TT)
        y_rows = raw[:, 0:2, 0:D]

        def wview(buf, slot, kt):
            return buf[:, slot, :].rearrange("p (k c) -> p k c", k=kt)

        def halved(buf, slot, key):
            return wview(buf, slot, KT)[:, :, 0:P] if key == ("gla", 0) else buf[:, slot, :]

        def landed(n):
            return at(f"raw_landed{n % RAW_SLOTS}", n)

        block = ctx.enter_context(nc.Block())

        @block.sync
        def _(sp):
            def column_chunk(w, c0, n=S):
                return w[:, c0:c0 + n].rearrange("(k p) c -> p k c", p=P)

            def row_chunk(w, r0):
                return w[r0:r0 + S, :].rearrange("(k p) c -> p k c", p=P)

            def sources(key):
                kind, n = key[0], key[-1]
                if kind == "ada":
                    return [(0, row_chunk(a["w_ada"][0][:, key[1] * D:(key[1] + 1) * D], n * S))], 2
                if kind == "in":
                    c0 = IN_COLS[n]
                    if isinstance(c0, tuple):
                        return [(j * P, column_chunk(a["w_in"][0], c, P)) for j, c in enumerate(c0)], KT
                    return [(0, column_chunk(a["w_in"][0], c0))], KT
                if kind == "gla" and n == 0:
                    return [(0, column_chunk(a["gla_w_in_2"][0], GLA_IN - P, P))], KT
                if kind == "down":
                    return [(0, row_chunk(a["w_down"][0], n * S))], 2
                if kind == "mlp_out":
                    return [(0, row_chunk(a["mlp_w_out_2"][key[1]], n * S))], 2
                w, c0 = {
                    "out": lambda: (a["w_out"][0], n * S), "gate": lambda: (a["w_up"][0], n * S),
                    "val": lambda: (a["w_up"][0], D_FF + n * S), "qkv": lambda: (a["attn_w_qkv_2"][0], QKV[n] * S),
                    "wo": lambda: (a["attn_w_o_2"][0], n * S), "gla": lambda: (a["gla_w_in_2"][0], GLA[n] * S),
                    "gla_out": lambda: (a["gla_w_o_2"][0], n * S),
                    "mlp_in": lambda: (a["mlp_w_in_2"][key[1]], n * S),
                }[kind]()
                return [(0, column_chunk(w, c0))], KT

            for n, key in enumerate(STREAM):
                if n >= RAW_SLOTS:
                    old = STREAM[n - RAW_SLOTS]
                    if old[0] == "ada":
                        sp.wait_ge(*at("ada_added", *old[1:]))
                    else:
                        sp.wait_ge(*at("w_lo", SPLIT_OF[old]))
                parts, kt = sources(key)
                slot = n % RAW_SLOTS
                for j, (c0, src) in enumerate(parts):
                    dst = wview(raw, slot, kt)[:, :, c0:c0 + src.shape[2]]
                    event = (n,) if j == len(parts) - 1 else (n, "first part")
                    sp.dma_start(dst, src).then_inc(*mark(f"raw_landed{slot}", *event, by=16))
            for t in range(TT):
                sp.wait_ge(*at("y_rows", 2 * t))
                sp.wait_ge(*at("y_half", 2 * t + 1))
                sp.dma_start(out[0, t * P:(t + 1) * P, :], y_rows[:, t, :]).then_inc(*mark("out_landed", t, by=16))
            sp.wait_ge(*at("out_landed", TT - 1))

        @block.gpsimd
        def _(pool):
            pool.memset(bqz, 0.0).then_inc(*mark("zeroed", 0))
            pool.memset(cqz, 0.0).then_inc(*mark("zeroed", 1))
            for n, key in enumerate(SPLITS):
                r = LOAD_OF[key]
                pool.wait_ge(*landed(r))
                pool.wait_ge(*at("w_hi", n))
                pool.tensor_tensor(halved(w_lo, n % SPLIT_SLOTS, key), halved(raw, r % RAW_SLOTS, key),
                                   halved(w_hi, n % SPLIT_SLOTS, key).bitcast(F32), ALU.subtract)\
                    .then_inc(*mark("w_lo", n))

        @block.scalar
        def _(act):
            done = {"hi": 0}

            def weights_upto(n):
                while done["hi"] <= min(n, len(SPLITS) - 1):
                    m = done["hi"]
                    r = LOAD_OF[SPLITS[m]]
                    act.wait_ge(*landed(r))
                    if m >= SPLIT_SLOTS:
                        act.wait_ge(*at("chunk_used", m - SPLIT_SLOTS))
                    act.activation(halved(w_hi, m % SPLIT_SLOTS, SPLITS[m]), halved(raw, r % RAW_SLOTS, SPLITS[m]),
                                   ACT.Copy).then_inc(*mark("w_hi", m))
                    done["hi"] += 1

            def ahead(key):
                weights_upto(SPLIT_OF[key] + SPLIT_SLOTS - 1)

            def high(idx, k, src, func=ACT.Copy, **kw):
                if k == 0 and idx > 0:
                    act.wait_ge(*at("chunk_used", SPLIT_OF[LAST_USE[idx - 1]]))
                act.activation(h_hi[:, k, :], src, func, **kw).then_inc(*mark("high", idx, k))

            def split(idx, k):
                act.wait_ge(*at("full", idx, k))
                high(idx, k, y_t[:, k, :])

            def unscaled(i):
                for k in range(KT):
                    act.wait_ge(*at("x_new", X_OF_NORM[i], k))
                    high(SET_OF_NORM[i], k, x_t[:, k, :], ACT.Identity, scale=norm_gain(i)[:, k:k + 1])

            def squares(i, n):
                for k in (2 * n, 2 * n + 1):
                    act.wait_ge(*at("x_new", i, k))
                    act.activation(work[:, k, :], x_t[:, k, :], ACT.Square).then_inc(*mark("square", i, k))

            def total(i):
                act.wait_ge(*at("job", "sum", i))
                dst = rstd_x if i == 3 else rstd
                act.activation(dst[:, :], bank("sum", i)[:, 0:S], ACT.Sqrt, scale=1.0 / D, bias=cst("eps"))\
                    .then_inc(*mark("act_read", "sum", i))

            def copy(job, dst, func=ACT.Copy, **kw):
                act.wait_ge(*at("job", *job))
                act.activation(dst, bank(*job)[:, 0:S], func, **kw).then_inc(*mark("act_read", *job))

            def setup():
                act.dma_start(const[:, :], a["const"]).then_inc(*mark("const_landed", 0, by=16))
                at_row = 0
                src = {"c": a["c"].rearrange("o (n p) -> (o n) p", p=P),
                       "b_ada": a["b_ada"].rearrange("o (n p) -> (o n) p", p=P),
                       "g_mix": a["g_mix"].rearrange("o (n p) -> (o n) p", p=P),
                       "g_ffn": a["g_ffn"].rearrange("o (n p) -> (o n) p", p=P),
                       "g_final": a["g_final"].rearrange("(n p) -> n p", p=P),
                       "g_sgu": a["g_sgu"].rearrange("o (n p) -> (o n) p", p=P),
                       "norm_mix": a["norm_mix_2"].rearrange("o (n p) -> (o n) p", p=P),
                       "norm_mlp": a["norm_mlp_2"].rearrange("o (n p) -> (o n) p", p=P),
                       "final_norm": a["final_norm_2"].rearrange("(n p) -> n p", p=P),
                       "b_gate": a["gla_b_gate_2"][0].rearrange("o (n p) -> (o n) p", p=P),
                       "out_norm": a["gla_out_norm_2"].rearrange("o (n p) -> (o n) p", p=P),
                       "conv_w0": a["conv_w"][0, 0:1].rearrange("o (n p) -> (o n) p", p=P),
                       "conv_w1": a["conv_w"][0, 1:2].rearrange("o (n p) -> (o n) p", p=P),
                       "conv_w2": a["conv_w"][0, 2:3].rearrange("o (n p) -> (o n) p", p=P),
                       "conv_b": a["conv_b"].rearrange("o (n p) -> (o n) p", p=P)}
                for j, names in enumerate(ROWS):
                    at_row = 0
                    for name, n in names.items():
                        if name in ("q_norm", "k_norm"):
                            g = a[f"attn_{name}_2"]
                            act.dma_start(rows[at_row:at_row + 1, j, 0:HD], g).then_inc(*mark("rows_landed", name, 0, by=16))
                            act.dma_start(rows[at_row:at_row + 1, j, HD:P], g).then_inc(*mark("rows_landed", name, 1, by=16))
                        else:
                            act.dma_start(rows[at_row:at_row + n, j, :], src[name])\
                                .then_inc(*mark("rows_landed", name, by=16))
                        at_row += n
                    if j == 0:
                        act.dma_start(x_rows, a["x"][0].rearrange("(t p) c -> p t c", p=P))\
                            .then_inc(*mark("x_landed", 0, by=16))
                act.dma_start(w_sp_r, a["w_sp"][0].rearrange("g t s -> t g s")).then_inc(*mark("w_sp_landed", 0, by=16))
                act.dma_start(pos_i[:, :], a["positions"].broadcast_to([P, S])).then_inc(*mark("pos_landed", 0, by=16))
                for g in range(4):
                    act.dma_start(b_sp_b[64 * (g % 2):64 * (g % 2) + 64, g // 2, :],
                                  a["b_sp"][0, g:g + 1, :].broadcast_to([64, P])).then_inc(*mark("b_sp_landed", g, by=16))
                act.wait_ge(*at("cols", 0))
                act.activation(c_act[:, :], col("c", 0, KT), ACT.Silu).then_inc(*mark("c_act", 0))
                for j in range(2):
                    act.wait_ge(*at("angle", j))
                    act.activation(angle[:, j, :], angle[:, 2 + j, :], ACT.Sin).then_inc(*mark("sine", j))
                act.wait_ge(*at("x_new", 0, KT - 1))
                weights_upto(2)

            def root(i):
                for k in range(KT):
                    act.wait_ge(*at("x_new", i, k))
                    act.activation(work[:, k, :], x_t[:, k, :], ACT.Square).then_inc(*mark("square", i, k))
                copy(("sum", i), rstd[:, :], ACT.Sqrt, scale=1.0 / D, bias=cst("eps"))

            def scaled(i):
                if i in SET_OF_NORM:
                    for k in range(KT):
                        act.wait_ge(*at("normed", i, k))
                        high(SET_OF_NORM[i], k, y_t[:, k, :], ACT.Identity, bias=mod[:, 24 * i + k:24 * i + k + 1])

            def take_in(n):
                ahead(("in", n))
                for m in range(2):
                    job = ("in", n, m)
                    t = 2 * n + m
                    if n < 3:
                        copy(job, cqk[:, t, :], scale=0.125 if t < 3 else 1.0)
                    elif n == 3:
                        copy(job, u_t[:, m, :], ACT.Gelu_apprx_tanh)
                    elif n == 4:
                        copy(job, v_tok[:, m, :], ACT.Gelu_apprx_tanh)
                    elif n < 8 and t - 10 < 3:
                        act.wait_ge(*at("job", *job))
                        act.wait_ge(*at("zeroed", 0))
                        act.activation(bqz[0:64, 2 * (t - 10), :], bank(*job)[0:64, 0:S], ACT.Copy, scale=0.125)\
                            .then_inc(*mark("b_q", t - 10))
                        act.activation(bqz[64:128, 2 * (t - 10) + 1, :], bank(*job)[64:128, 0:S], ACT.Copy,
                                       scale=0.125).then_inc(*mark("act_read", *job))
                    elif n < 8:
                        copy(job, bk_t[:, t - 13, :])
                    else:
                        copy(job, vals[:, m, (n - 8) * S:(n - 7) * S])

            def v_norm():
                act.wait_ge(*at("v_sum", 0))
                act.activation(small[:, 8:16], small[:, 0:8], ACT.Sqrt, scale=1.0 / HD, bias=cst("eps"))\
                    .then_inc(*mark("v_root", 0))

            def stick_a(h):
                act.wait_ge(*at("job", "stick", h))
                if h >= 4:
                    act.wait_ge(*at("job", "stick_o", (h - 4) // 2))
                act.activation(stick(h), bank("stick", h)[:, 0:SP3], ACT.Abs).then_inc(*mark("stick_act", h, 0))
                act.wait_ge(*at("stick_act", h, 0))
                act.activation(stick(h), stick(h), ACT.Exp, scale=-1.0).then_inc(*mark("stick_act", h, 1))
                act.wait_ge(*at("stick_act", h, 1))
                act.activation(stick(h), stick(h), ACT.Ln, bias=cst("one")).then_inc(*mark("stick_act", h, 2))

            def stick_b(h):
                act.wait_ge(*at("stick_tail", h))
                act.activation(stick(h), bank("stick", h)[:, 0:SP3], ACT.Exp).then_inc(*mark("act_read", "stick", h))

            def win_a(h):
                act.wait_ge(*at("win_max", h))
                for q in range(TT):
                    pr = win_p(h)[:, 0:P] if q == 0 else win_p(h)[:, P:SP3]
                    act.activation(pr, pr, ACT.Exp, bias=small[:, 32 + 2 * h + q:33 + 2 * h + q],
                                   accum_out=small[:, 48 + 2 * h + q:49 + 2 * h + q]).then_inc(*mark("win_exp", h, q))

            def win_b():
                act.wait_ge(*at("win_rel", 0))
                act.activation(small[:, 64:76], small[:, 64:76], ACT.Exp).then_inc(*mark("win_factor", 0))

            def win_c(h):
                act.wait_ge(*at("job", "win_t", h))
                act.activation(win_pt(h), bank("win_t", h)[:, 0:SP3], ACT.Copy).then_inc(*mark("act_read", "win_t", h))

            def project(kind, n):
                ahead((kind, n))

            def ff_up(i):
                ahead(("gate", i))
                for f in range(2):
                    act.wait_ge(*at("job", "gate", i, f))
                    if i > 0:
                        act.wait_ge(*at("ff_product", i - 1, f))
                    act.activation(ff_g[:, f, :], bank("gate", i, f)[:, 0:S], ACT.Identity,
                                   scale=col("conv_w2", 2 * i + f), bias=col("conv_b", 2 * i + f))\
                        .then_inc(*mark("ff_newest", "gate", i, f))
                ahead(("val", i))
                for f in range(2):
                    act.wait_ge(*at("job", "val", i, f))
                    if i > 0:
                        act.wait_ge(*at("hidden_lo", "down", i - 1, f))
                    act.activation(ff_v[:, f, :], bank("val", i, f)[:, 0:S], ACT.Identity,
                                   scale=col("conv_w2", 22 + 2 * i + f), bias=col("conv_b", 22 + 2 * i + f))\
                        .then_inc(*mark("ff_newest", "val", i, f))
                    act.wait_ge(*at("dve_read", "gate", i, f))
                    act.activation(ff_s[:, f, :], ff_g[:, f, :], ACT.Silu).then_inc(*mark("ff_silu", i, f))
                for f in range(2):
                    act.wait_ge(*at("ff_product", i, f))
                    if i >= 2 and f == 0:
                        act.wait_ge(*at("chunk_used", SPLIT_OF[("down", i - 2)]))
                    act.activation(a_hi[:, 2 * (i % 2) + f, :], ff_v[:, f, :], ACT.Copy)\
                        .then_inc(*mark("hidden_hi", "down", i, f))

            def down(*key):
                ahead(key)

            def qkv(n):
                ahead(("qkv", n))

            def q_a(t):
                job = ("qkv", Q_CHUNK[t], t % 2)
                act.wait_ge(*at("job", *job))
                act.wait_ge(*at("gain_qkv", 1))
                if t >= 4:
                    act.wait_ge(*at("turn", t - 4, 2))
                act.activation(qx[:, t % 4, :], bank(*job)[:, 0:S], ACT.Identity, scale=small[:, 120:121])\
                    .then_inc(*mark("q_gained", t))
                if t >= 2:
                    act.wait_ge(*at("job", "axial", t - 2))
                act.activation(q_sq[:, t % 2, :], bank(*job)[:, 0:S], ACT.Square).then_inc(*mark("act_read", *job))

            def k_a(t):
                act.wait_ge(*at("k_scaled", t))
                act.wait_ge(*at("job", "axial", 4 + t))
                act.activation(q_sq[:, t, :], k_x[:, t, :], ACT.Square).then_inc(*mark("k_square", t))

            def k_b(t):
                act.wait_ge(*at("job", "k_mean", t))
                act.activation(k_rms[:, t, :], bank("k_mean", t)[:, 0:S], ACT.Sqrt, bias=cst("eps"))\
                    .then_inc(*mark("act_read", "k_mean", t))
                if t == 1:
                    for m in range(TT):
                        act.wait_ge(*at("dve_read", "r_cols", 3))
                        copy(("qkv", 4, m), v2[:, m, :], ACT.Identity, scale=r_col[:, m:m + 1])

            def k_c(t):
                for n in range(2):
                    act.wait_ge(*at("k_turned", t, n))
                    act.dma_start(ak_dup[64 * (1 - n):64 * (1 - n) + 64, 2 * t + n, :],
                                  ak_dup[64 * n:64 * n + 64, 2 * t + n, :])\
                        .then_inc(*mark(f"k_doubled{2 * t + n}", 0, by=16))

            def q_scale():
                act.wait_ge(*at("q_means", 0))
                act.activation(q_mean[:, :, :], q_mean[:, :, :], ACT.Sqrt, bias=cst("eps")).then_inc(*mark("q_rms", 0))

            def att_a(h):
                act.wait_ge(*at("att_max", h))
                if h >= 3:
                    act.wait_ge(*at("job", "att_t", h - 3))
                for q in range(TT):
                    c = 8 * (h % 3) + q
                    act.activation(att_p[:, h % 3, q, :], bank("att", h)[:, q * S:(q + 1) * S], ACT.Exp,
                                   scale=q_mean[:, q, h:h + 1], bias=small[:, c + 2:c + 3],
                                   accum_out=small[:, c + 4:c + 5])\
                        .then_inc(*(mark("act_read", "att", h) if q else mark("att_exp", h)))

            def att_b(h):
                act.wait_ge(*at("job", "att_t", h))
                if h >= 2:
                    act.wait_ge(*at("att_pv", h - 2))
                act.activation(att_pt[:, h % 2, :, :], bank("att_t", h)[:, :].rearrange("p (k s) -> p k s", k=TT),
                               ACT.Copy).then_inc(*mark("act_read", "att_t", h))

            def mlp_up(layer, i):
                ahead(("mlp_in", layer, i))

            def mlp_act(layer, i):
                for f in range(2):
                    act.wait_ge(*at("dve_read", "mlp_in", layer, i, f))
                    if i >= 2 and f == 0:
                        act.wait_ge(*at("chunk_used", SPLIT_OF[("mlp_out", layer, i - 2)]))
                    act.activation(a_hi[:, 2 * (i % 2) + f, :], ff_g[:, f, :], ACT.Square)\
                        .then_inc(*mark("hidden_hi", "mlp_out", layer, i, f))

            def gla(n):
                if n == 0:
                    act.wait_ge(*at("w_gate_zero", 0))
                    for j in range(2):
                        act.dma_start(w_gate[16 * j:16 * j + 16, j, :], a["gla_w_gate_up_2"][0, j])\
                            .then_inc(*mark("w_gate_landed", j, by=16))
                ahead(("gla", n))

            def gla_in(n):
                for m in range(2):
                    if 5 <= n < 9:
                        act.wait_ge(*at("dve_read", "r_cols", 5))
                        copy(("gla", n, m), gv[:, m, (n - 5) * S:(n - 4) * S], ACT.Identity, scale=r_col[:, m:m + 1])
                    elif n >= 9:
                        act.wait_ge(*at("dve_read", "gla", n, m))
                        j = 2 * (n - 9) + m
                        act.activation(gr[:, j, :], gr[:, j, :], ACT.Silu).then_inc(*mark("gla_gate", j))

            def gate(h):
                act.wait_ge(*at("job", "logit", h))
                if h > 0:
                    act.wait_ge(*at("dve_read", "logit", h - 1))
                for n in range(2):
                    act.activation(work[:, n, :], bank("logit", h)[:, n * S:(n + 1) * S], ACT.Abs,
                                   bias=col("b_gate", 4 * n + h)).then_inc(*mark("gate_abs", h, n))
                act.wait_ge(*at("gate_abs", h, 1))
                act.preload_act_table_set("natural_log_exp_and_others")
                act.activation(work[:, 0:2, :], work[:, 0:2, :], ACT.Exp, scale=-1.0).then_inc(*mark("gate_exp", h))
                act.wait_ge(*at("gate_exp", h))
                act.activation(work[:, 0:2, :], work[:, 0:2, :], ACT.Ln, bias=cst("one")).then_inc(*mark("gate_ln", h))
                act.wait_ge(*at("gate_sum", h, 1))
                act.activation(mid[:, :, :] if h == 0 else small[:, 4 * h:4 * h + 4].rearrange("p (n t) -> p n t", n=2),
                               work[:, 4:6, HD - 1::P], ACT.Exp, scale=1.0 / 16).then_inc(*mark("gate_mid", h))
                act.wait_ge(*at("gate_rel", h))
                act.activation(qe[:, h, :, :], work[:, 6:8, :], ACT.Exp, scale=1.0 / 16).then_inc(*mark("decay", h, 0))
                act.activation(ke[:, h, :, :], work[:, 6:8, :], ACT.Exp, scale=-1.0 / 16).then_inc(*mark("decay", h, 1))

            def mix(h):
                act.wait_ge(*at("job", "pair_fwd", h))
                if h >= 2:
                    act.wait_ge(*at("job", "gla_o", h - 2, 1))
                act.activation(pair[:, h % 2, :, :], bank("pair_fwd", h)[:, :].rearrange("p (t s) -> p t s", t=TT),
                               ACT.Copy).then_inc(*mark("act_read", "pair_fwd", h))

            def mixed(h):
                for m in range(2):
                    act.wait_ge(*at("job", "gla_o", h, m))
                    if h > 1:
                        act.wait_ge(*at("job", "gla_sum", h - 2))
                    act.activation(gla_sq[:, 2 * (h % 2) + m, :], bank("gla_o", h, m)[:, 0:S], ACT.Square)\
                        .then_inc(*mark("gla_square", h, m))

            def head_norm(h):
                act.wait_ge(*at("job", "gla_sum", h))
                act.activation(work[:, h, :], bank("gla_sum", h)[:, 0:S], ACT.Sqrt, scale=1.0 / S, bias=cst("eps"))\
                    .then_inc(*mark("act_read", "gla_sum", h))

            def finish():
                act.wait_ge(*at("w_lo", len(SPLITS) - 1))
                for j in (1, 3):
                    act.wait_ge(*at("job", "turned", j))
                    act.activation(y_rows[:, j // 2, 512:1024], bank("turned", j)[:, :], ACT.Copy)\
                        .then_inc(*mark("y_half", j))

            steps = {"setup": setup, "root": root, "scaled": scaled, "split": split, "unscaled": unscaled,
                     "squares": squares, "total": total, "in": take_in, "v_norm": v_norm,
                     "stick_a": stick_a, "stick_b": stick_b, "win_a": win_a, "win_b": win_b, "win_c": win_c,
                     "project": project, "ff_up": ff_up, "down": down, "qkv": qkv, "q_a": q_a,
                     "k_a": k_a, "k_b": k_b, "k_c": k_c, "q_scale": q_scale, "att_a": att_a, "att_b": att_b,
                     "mlp_up": mlp_up, "mlp_act": mlp_act, "gla": gla, "gla_in": gla_in, "gate": gate, "mix": mix,
                     "mixed": mixed, "head_norm": head_norm, "finish": finish}
            for step in schedule():
                if step[0] in steps:
                    steps[step[0]](*step[1:])

        @block.vector
        def _(dve):
            def split(idx, k):
                dve.wait_ge(*at("high", idx, k))
                dve.tensor_tensor(h_lo[:, k, :], y_t[:, k, :], h_hi[:, k, :].bitcast(F32), ALU.subtract)\
                    .then_inc(*mark("low", idx, k))

            def unscaled(i):
                for k in range(KT):
                    dve.wait_ge(*at("high", SET_OF_NORM[i], k))
                    dve.scalar_tensor_tensor(out=h_lo[:, k, :], in0=x_t[:, k, :], scalar=norm_gain(i)[:, k:k + 1],
                                             in1=h_hi[:, k, :].bitcast(F32), op0=ALU.mult, op1=ALU.subtract)\
                        .then_inc(*mark("low", SET_OF_NORM[i], k))

            def tree(i):
                for j, n in enumerate((4, 2, 1)):
                    dve.wait_ge(*(at("square", i, KT - 1) if j == 0 else at("tree", i, j - 1)))
                    dve.tensor_tensor(work[:, 0:n, :], work[:, 0:n, :], work[:, n:2 * n, :], ALU.add)\
                        .then_inc(*mark("tree", i, j))

            def total(i):
                dve.wait_ge(*at("act_read", "sum", i))
                dst = rstd_x if i == 3 else rstd
                dve.reciprocal(dst[:, :], dst[:, :]).then_inc(*mark("rstd", i))
                if i == 3:
                    dve.wait_ge(*at("rstd", i))
                    dve.tensor_tensor(rstd_x[:, :], rstd_x[:, :], rstd[:, :], ALU.mult).then_inc(*mark("rstd_both", 3))

            def rescale(i):
                dve.wait_ge(*at("rstd", i))
                dve.wait_ge(*at("low", SET_OF_NORM[3], KT - 1))
                for k in range(KT):
                    dve.scalar_tensor_tensor(out=x_t[:, k, :], in0=x_t[:, k, :], scalar=col("g_final", k),
                                             in1=rstd[:, :], op0=ALU.mult, op1=ALU.mult).then_inc(*mark("x_new", 3, k))

            def r_cols(i):
                dve.wait_ge(*at("job", "r_cols", i))
                dve.tensor_copy(r_col[:, :], bank("r_cols", i)[:, 0:TT]).then_inc(*mark("dve_read", "r_cols", i))

            def setup():
                for j in range(len(ROWS)):
                    dve.wait_ge(*at("job", "rows", j))
                    o = COL_AT[next(iter(ROWS[j]))]
                    n = sum(ROWS[j].values())
                    dve.tensor_copy(cols[:, o:o + n], bank("rows", j)[:, 0:n]).then_inc(*mark("dve_read", "rows", j))
                    same(("cols", j), ("dve_read", "rows", j))
                for j in range(4):
                    dve.wait_ge(*at("job", "x", j))
                    dve.tensor_copy(x_t[:, 2 * j:2 * j + 2, :], bank("x", j)[:, :].rearrange("p (k s) -> p k s", k=2))\
                        .then_inc(*mark("dve_read", "x", j))
                    for k in (2 * j, 2 * j + 1):
                        same(("x_new", 0, k), ("dve_read", "x", j))
                dve.wait_ge(*at("pos_landed", 0))
                dve.wait_ge(*at("const_landed", 0))
                dve.tensor_copy(angle[:, 0, :], pos_i[:, :]).then_inc(*mark("reduce", 0))
                dve.wait_ge(*at("reduce", 0))
                dve.tensor_scalar(angle[:, 4, :], angle[:, 0, :], cst("inv_freq"), None, ALU.mult)\
                    .then_inc(*mark("reduce", 1))
                dve.wait_ge(*at("reduce", 1))
                dve.tensor_scalar(angle[:, 5, :], angle[:, 4, :], float(1 / (2 * np.pi)), MAGIC, ALU.mult, ALU.add)\
                    .then_inc(*mark("reduce", 2))
                dve.wait_ge(*at("reduce", 2))
                dve.tensor_scalar(angle[:, 5, :], angle[:, 5, :], -MAGIC, None, ALU.add).then_inc(*mark("reduce", 3))
                for j, part in enumerate(TWO_PI):
                    dve.wait_ge(*at("reduce", 3 + j))
                    dve.scalar_tensor_tensor(out=angle[:, 4, :], in0=angle[:, 5, :], scalar=-part,
                                             in1=angle[:, 4, :], op0=ALU.mult, op1=ALU.add)\
                        .then_inc(*mark("reduce", 4 + j))
                dve.wait_ge(*at("reduce", 6))
                dve.tensor_scalar(angle[:, 2, :], angle[:, 4, :], PI_BELOW, -PI_BELOW, ALU.min, ALU.max)\
                    .then_inc(*mark("angle", 0))
                dve.scalar_tensor_tensor(out=angle[:, 3, :], in0=angle[:, 4, :], scalar=-1.0, in1=angle[:, 4, :],
                                         op0=ALU.mult, op1=ALU.max).then_inc(*mark("reduce", 7))
                dve.wait_ge(*at("reduce", 7))
                dve.tensor_scalar(angle[:, 3, :], angle[:, 3, :], -1.0, float(np.pi / 2), ALU.mult, ALU.add)\
                    .then_inc(*mark("angle", 1))
                for g in range(4):
                    dve.wait_ge(*at("job", "w_sp", 0))
                    dve.tensor_tensor(w_sp_t[:, g, :], bank("w_sp", 0)[:, g * P:(g + 1) * P], cst("upto"), ALU.mult)\
                        .then_inc(*(mark("dve_read", "w_sp", 0) if g == 3 else mark("w_sp_masked", g)))

            def ada_step(p, q):
                r = LOAD_OF[("ada", p, q)]
                dve.wait_ge(*landed(r))
                if q == 0:
                    dve.wait_ge(*at("c_act", 0))
                    if p >= 2:
                        dve.wait_ge(*at("job", "mod", p - 2))
                for kk in range(2):
                    k = 2 * q + kk
                    src = wview(raw, r % RAW_SLOTS, 2)[:, kk, :]
                    if k == 0:
                        ins = dve.tensor_scalar(ada[:, p % 2, :], src, c_act[:, 0:1], None, ALU.mult)
                    else:
                        dve.wait_ge(*(at("ada_added", p, q - 1) if kk == 0 else at("ada_half", p, q)))
                        ins = dve.scalar_tensor_tensor(out=ada[:, p % 2, :], in0=src, scalar=c_act[:, k:k + 1],
                                                       in1=ada[:, p % 2, :], op0=ALU.mult, op1=ALU.add)
                    ins.then_inc(*(mark("ada_added", p, q) if kk else mark("ada_half", p, q)))
                if q == 3:
                    dve.wait_ge(*at("job", "mod", p))
                    dve.tensor_tensor(mod[:, KT * p:KT * p + KT], bank("mod", p)[:, 0:KT], col("b_ada", KT * p, KT),
                                      ALU.add).then_inc(*mark("dve_read", "mod", p))

            def gains(n):
                if n == 0:
                    dve.wait_ge(*at("dve_read", "mod", 1))
                    dve.scalar_tensor_tensor(out=gain[:, 0, :], in0=mod[:, 8:16], scalar=1.0, in1=col("g_mix", 0, KT),
                                             op0=ALU.add, op1=ALU.mult).then_inc(*mark("gains", 0))
                else:
                    dve.wait_ge(*at("dve_read", "mod", 5))
                    dve.scalar_tensor_tensor(out=gain[:, 1, :], in0=mod[:, 32:40], scalar=1.0,
                                             in1=col("g_ffn", 0, KT), op0=ALU.add, op1=ALU.mult)\
                        .then_inc(*mark("gains", 1))
                    dve.tensor_scalar(gain[:, 2, :], mod[:, 16:24], 1.0, None, ALU.add).then_inc(*mark("gains", 2))
                    dve.tensor_scalar(gain[:, 3, :], mod[:, 40:48], 1.0, None, ALU.add).then_inc(*mark("gains", 3))

            def root(i):
                dve.wait_ge(*at("act_read", "sum", i))
                dve.reciprocal(rstd[:, :], rstd[:, :]).then_inc(*mark("rstd", i))

            def scaled(i):
                dve.wait_ge(*at("rstd", i))
                g = {0: gain[:, 0, :], 1: gain[:, 1, :], 7: col("final_norm", 0, KT)}[i]
                if i in (0, 1):
                    dve.wait_ge(*at("gains", i))
                for k in range(KT + 1):
                    if k < KT:
                        dve.scalar_tensor_tensor(out=y_t[:, k, :], in0=x_t[:, k, :], scalar=g[:, k:k + 1],
                                                 in1=rstd[:, :], op0=ALU.mult, op1=ALU.mult)\
                            .then_inc(*(mark("y_normed", k) if i == 7 else mark("normed", i, k)))
                    if k > 0 and i in SET_OF_NORM:
                        m = 24 * i + k - 1
                        dve.wait_ge(*at("high", SET_OF_NORM[i], k - 1))
                        dve.scalar_tensor_tensor(out=h_lo[:, k - 1, :], in0=y_t[:, k - 1, :], scalar=mod[:, m:m + 1],
                                                 in1=h_hi[:, k - 1, :].bitcast(F32), op0=ALU.add, op1=ALU.subtract)\
                            .then_inc(*mark("low", SET_OF_NORM[i], k - 1))

            def rope(t):
                dve.wait_ge(*at("job", "rope", t))
                dve.wait_ge(*at("sine", 1))
                if t == 0:
                    dve.wait_ge(*at("square", 0, KT - 1))
                    dve.wait_ge(*at("job", "sum", 0))
                else:
                    dve.wait_ge(*at("roped", t - 1, 2))
                dve.tensor_tensor(work[:, 0, :], cqk[:, t, :], angle[:, 1, :], ALU.mult).then_inc(*mark("roped", t, 0))
                dve.tensor_tensor(work[:, 1, :], bank("rope", t)[:, 0:S], angle[:, 0, :], ALU.mult)\
                    .then_inc(*mark("dve_read", "rope", t))
                dve.wait_ge(*at("dve_read", "rope", t))
                if t < 3:
                    dve.wait_ge(*at("zeroed", 1))
                    dve.tensor_tensor(cqz[0:64, 2 * t, :], work[0:64, 0, :], work[0:64, 1, :], ALU.add)\
                        .then_inc(*mark("roped", t, 1))
                    dve.tensor_tensor(cqz[64:128, 2 * t + 1, :], work[64:128, 0, :], work[64:128, 1, :], ALU.add)\
                        .then_inc(*mark("roped", t, 2))
                else:
                    dve.tensor_tensor(ck_t[:, t - 3, :], work[:, 0, :], work[:, 1, :], ALU.add)\
                        .then_inc(*mark("roped", t, 2))

            def v_norm():
                dve.wait_ge(*at("act_read", "in", 4, 1))
                sq = work[:, 2:4, :]
                dve.tensor_tensor(sq, v_tok, v_tok, ALU.mult).then_inc(*mark("v_square", 0))
                dve.wait_ge(*at("v_square", 0))
                dve.tensor_reduce(small[:, 0:8], sq.rearrange("p t (g c) -> p (t g) c", c=HD), AX.X, ALU.add)\
                    .then_inc(*mark("v_sum", 0))
                dve.wait_ge(*at("v_root", 0))
                dve.reciprocal(small[:, 8:16], small[:, 8:16]).then_inc(*mark("v_rstd", 0))
                dve.wait_ge(*at("v_rstd", 0))
                dve.tensor_tensor(v_nrm.rearrange("p t (g c) -> p (t g) c", c=HD),
                                  v_tok.rearrange("p t (g c) -> p (t g) c", c=HD),
                                  small[:, 8:16].rearrange("p (n o) -> p n o", o=1).broadcast_to([P, 8, HD]), ALU.mult)\
                    .then_inc(*mark("v_normed", 0))

            def gate_mix():
                dve.wait_ge(*at("b_sp_landed", 3))
                for m in range(2):
                    dve.wait_ge(*at("job", "gated", m))
                    if m == 0:
                        dve.wait_ge(*at("low", 0, KT - 1))
                        dve.wait_ge(*at("act_read", "in", 3, 1))
                    dve.scalar_tensor_tensor(out=blocks3(work[:, 4 + m, :]), in0=blocks3(bank("gated", m)[:, 0:S]),
                                             scalar=col("g_sgu", m),
                                             in1=b_sp_b[:, m:m + 1, :].broadcast_to([P, TT, P]),
                                             op0=ALU.mult, op1=ALU.add).then_inc(*mark("dve_read", "gated", m))
                    dve.wait_ge(*at("dve_read", "gated", m))
                    dve.tensor_tensor(y_t[:, m, :], work[:, 4 + m, :], u_t[:, m, :], ALU.mult)\
                        .then_inc(*mark("full", 1, m))

            def diag(ap):
                return blocks3(ap)[:, 0:3:2, :]

            def before():
                return cst("before").rearrange("p (o c) -> p o c", o=1).broadcast_to([P, 2, P])

            def stick_a(h):
                dve.wait_ge(*at("stick_act", h, 2))
                dve.scalar_tensor_tensor(out=stick(h), in0=bank("stick", h)[:, 0:SP3], scalar=0.0, in1=stick(h),
                                         op0=ALU.max, op1=ALU.add).then_inc(*mark("stick_soft", h))
                dve.wait_ge(*at("stick_soft", h))
                dve.tensor_tensor(diag(stick(h)), diag(stick(h)), before(), ALU.mult).then_inc(*mark("stick_masked", h))

            def stick_b(h):
                dve.wait_ge(*at("act_read", "stick", h))
                dve.scalar_tensor_tensor(out=diag(stick(h)), in0=diag(stick(h)), scalar=1.0, in1=before(),
                                         op0=ALU.min, op1=ALU.mult).then_inc(*mark("stick_weight", h))

            def stick_c(m):
                dve.wait_ge(*at("job", "stick_o", m))
                dve.tensor_copy(y_t[:, 2 + m, :], bank("stick_o", m)[:, 0:S]).then_inc(*mark("dve_read", "stick_o", m))
                same(("full", 1, 2 + m), ("dve_read", "stick_o", m))

            def win_a(h):
                dve.wait_ge(*at("job", "win", h))
                o = CONST_AT["window"][0] + (h // 2) * SP3
                dve.tensor_tensor(win_p(h), bank("win", h)[:, 0:SP3], const[:, o:o + SP3], ALU.add)\
                    .then_inc(*mark("dve_read", "win", h))
                dve.wait_ge(*at("dve_read", "win", h))
                dve.tensor_reduce(small[:, 16 + 2 * h:17 + 2 * h], win_p(h)[:, 0:P], AX.X, ALU.max)\
                    .then_inc(*mark("win_red", h, 0))
                dve.tensor_reduce(small[:, 17 + 2 * h:18 + 2 * h], win_p(h)[:, P:SP3], AX.X, ALU.max)\
                    .then_inc(*mark("win_red", h, 1))
                dve.wait_ge(*at("win_red", h, 1))
                dve.tensor_scalar(small[:, 32 + 2 * h:34 + 2 * h], small[:, 16 + 2 * h:18 + 2 * h], -1.0, None,
                                  ALU.mult).then_inc(*mark("win_max", h))

            def win_b():
                mx, den, rel, top, tmp, tot, fac = (small[:, 16:28], small[:, 48:60], small[:, 64:76],
                                                    small[:, 80:84], small[:, 88:100], small[:, 84:88],
                                                    small[:, 100:112])
                groups = lambda ap: ap.rearrange("p (g x) -> p g x", g=3)
                spread = lambda ap: ap.rearrange("p (o x) -> p o x", o=1).broadcast_to([P, 3, 4])
                dve.tensor_reduce(top, mx.rearrange("p (g x) -> p x g", g=3), AX.X, ALU.max)\
                    .then_inc(*mark("win_mix", 0))
                dve.wait_ge(*at("win_mix", 0))
                dve.tensor_tensor(groups(rel), groups(mx), spread(top), ALU.subtract).then_inc(*mark("win_rel", 0))
                dve.wait_ge(*at("win_factor", 0))
                dve.tensor_tensor(tmp, rel, den, ALU.mult).then_inc(*mark("win_mix", 1))
                dve.wait_ge(*at("win_mix", 1))
                dve.tensor_reduce(tot, tmp.rearrange("p (g x) -> p x g", g=3), AX.X, ALU.add)\
                    .then_inc(*mark("win_mix", 2))
                dve.wait_ge(*at("win_mix", 2))
                dve.reciprocal(tot, tot).then_inc(*mark("win_mix", 3))
                dve.wait_ge(*at("win_mix", 3))
                dve.tensor_tensor(groups(fac), groups(rel), spread(tot), ALU.mult).then_inc(*mark("win_mix", 4))
                dve.wait_ge(*at("win_mix", 4))
                for h in range(6):
                    for q in range(TT):
                        pr = win_p(h)[:, 0:P] if q == 0 else win_p(h)[:, P:SP3]
                        dve.tensor_scalar(pr, pr, small[:, 100 + 2 * h + q:101 + 2 * h + q], None, ALU.mult)\
                            .then_inc(*mark("win_scaled", h, q))

            def win_d(m):
                dve.wait_ge(*at("job", "win_o", m))
                dve.tensor_copy(y_t[:, 5 + m, :], bank("win_o", m)[:, 0:S]).then_inc(*mark("dve_read", "win_o", m))
                same(("full", 1, 5 + m), ("dve_read", "win_o", m))

            def project(kind, n):
                i = NEXT_NORM[kind]
                for m in range(2):
                    k = 2 * n + m
                    dve.wait_ge(*at("job", kind, n, m))
                    if kind == "out":
                        if k == 0:
                            dve.wait_ge(*at("gains", 2))
                        ins = dve.scalar_tensor_tensor(out=x_t[:, k, :], in0=bank(kind, n, m)[:, 0:S],
                                                       scalar=gain[:, 2, k:k + 1], in1=x_t[:, k, :],
                                                       op0=ALU.mult, op1=ALU.add)
                    else:
                        ins = dve.tensor_tensor(x_t[:, k, :], bank(kind, n, m)[:, 0:S], x_t[:, k, :], ALU.add)
                    ins.then_inc(*mark("dve_read", kind, n, m))
                    same(("x_new", i, k), ("dve_read", kind, n, m))

            def ff_up(i):
                if i == 1:
                    dve.memset(aqz, 0.0).then_inc(*mark("gain_qkv", 0))
                    dve.tensor_scalar(small[:, 120:121], col("q_norm"), 0.125, None, ALU.mult)\
                        .then_inc(*mark("gain_qkv", 1))
                    dve.tensor_tensor(gain_qkv[:, :], col("g_final", 0, KT), col("norm_mix", 0, KT), ALU.mult)\
                        .then_inc(*mark("gain_qkv", 2))
                for kind, buf, first in (("gate", ff_g, 0), ("val", ff_v, 22)):
                    for f in range(2):
                        c = bank(kind, i, f)
                        t = first + 2 * i + f
                        dve.wait_ge(*at("ff_newest", kind, i, f))
                        dve.scalar_tensor_tensor(out=buf[:, f, 1:S], in0=c[:, 0:S - 1], scalar=col("conv_w1", t),
                                                 in1=buf[:, f, 1:S], op0=ALU.mult, op1=ALU.add)\
                            .then_inc(*mark("ff_middle", kind, i, f))
                        dve.wait_ge(*at("ff_middle", kind, i, f))
                        dve.scalar_tensor_tensor(out=buf[:, f, 2:S], in0=c[:, 0:S - 2], scalar=col("conv_w0", t),
                                                 in1=buf[:, f, 2:S], op0=ALU.mult, op1=ALU.add)\
                            .then_inc(*mark("dve_read", kind, i, f))
                        if kind == "val":
                            dve.wait_ge(*at("dve_read", "val", i, f))
                            dve.wait_ge(*at("ff_silu", i, f))
                            dve.tensor_tensor(ff_v[:, f, :], ff_v[:, f, :], ff_s[:, f, :], ALU.mult)\
                                .then_inc(*mark("ff_product", i, f))
                for f in range(2):
                    hidden_low(ff_v[:, f, :], i, f, "down", i)

            def hidden_low(full, i, f, *key):
                dve.wait_ge(*at("hidden_hi", *key, f))
                b = 2 * (i % 2) + f
                dve.tensor_tensor(a_lo[:, b, :], full, a_hi[:, b, :].bitcast(F32), ALU.subtract)\
                    .then_inc(*mark("hidden_lo", *key, f))

            def mlp_act(layer, i):
                for f in range(2):
                    dve.wait_ge(*at("job", "mlp_in", layer, i, f))
                    if i > 0:
                        dve.wait_ge(*at("hidden_lo", "mlp_out", layer, i - 1, f))
                    else:
                        dve.wait_ge(*at("rstd", 4 + 2 * layer))
                    dve.scalar_tensor_tensor(out=ff_g[:, f, :], in0=bank("mlp_in", layer, i, f)[:, 0:S], scalar=0.0,
                                             in1=rstd[:, :], op0=ALU.max, op1=ALU.mult)\
                        .then_inc(*mark("dve_read", "mlp_in", layer, i, f))
                for f in range(2):
                    dve.wait_ge(*at("dve_read", "mlp_in", layer, i, f))
                    dve.tensor_tensor(ff_s[:, f, :], ff_g[:, f, :], ff_g[:, f, :], ALU.mult)\
                        .then_inc(*mark("relu_squared", layer, i, f))
                for f in range(2):
                    dve.wait_ge(*at("relu_squared", layer, i, f))
                    hidden_low(ff_s[:, f, :], i, f, "mlp_out", layer, i)

            def add_down(*key):
                i = 2 if key[0] == "down" else 5 + 2 * key[1]
                for k in range(KT):
                    acc = psum[4 + k // 2][:, (k % 2) * S:(k % 2 + 1) * S]
                    dve.wait_ge(*at("summed", *key, k | 1))
                    if key[0] == "down":
                        ins = dve.scalar_tensor_tensor(out=x_t[:, k, :], in0=acc, scalar=gain[:, 3, k:k + 1],
                                                       in1=x_t[:, k, :], op0=ALU.mult, op1=ALU.add)
                    else:
                        ins = dve.tensor_tensor(x_t[:, k, :], acc, x_t[:, k, :], ALU.add)
                    ins.then_inc(*mark("x_new", i, k))
                    if k % 2:
                        same(("dve_read", "acc", *key, 4 + k // 2), ("x_new", i, k))

            def q_b(t):
                dve.wait_ge(*at("job", "axial", t))
                if t > 0:
                    dve.wait_ge(*at("turn", t - 1, 2))
                turn(qx[:, t % 4, :], ("axial", t), 0)
                for n in range(2):
                    r = slice(64 * n, 64 * n + 64)
                    dve.tensor_tensor(aqz[r, 2 * t + n, :], turned[r, 0, :], turned[r, 1, :], ALU.add)\
                        .then_inc(*mark("turn", t, 1 + n))

            def turn(src, job, b):
                dve.tensor_tensor(turned[:, b, :], src, cst("axial_cos"), ALU.mult).then_inc(*mark("turn_cos", *job))
                if job[0] == "axial":
                    t = job[1]
                    dve.tensor_copy(q_mean[:, :, 2 * t:2 * t + 2],
                                    bank(*job)[:, S:S + 4].rearrange("p (t n) -> p t n", t=TT))\
                        .then_inc(*mark("q_mean", t))
                dve.tensor_tensor(turned[:, b + 1, :], bank(*job)[:, 0:S], cst("axial_sin"), ALU.mult)\
                    .then_inc(*mark("dve_read", *job))
                dve.wait_ge(*at("dve_read", *job))

            def k_a(t):
                dve.wait_ge(*at("job", "qkv", 3, t))
                dve.wait_ge(*at("rstd_both", 3))
                dve.tensor_tensor(k_x[:, t, :], bank("qkv", 3, t)[:, 0:S], rstd_x[:, :], ALU.mult)\
                    .then_inc(*mark("dve_read", "qkv", 3, t))
                same(("k_scaled", t), ("dve_read", "qkv", 3, t))

            def k_b(t):
                dve.wait_ge(*at("act_read", "k_mean", t))
                dve.reciprocal(k_rms[:, t, :], k_rms[:, t, :]).then_inc(*mark("k_rstd", t))
                dve.wait_ge(*at("k_rstd", t))
                dve.scalar_tensor_tensor(out=k_x[:, t, :], in0=k_x[:, t, :], scalar=col("k_norm"),
                                         in1=k_rms[:, t, :], op0=ALU.mult, op1=ALU.mult).then_inc(*mark("k_normed", t))

            def k_c(t):
                dve.wait_ge(*at("job", "k_axial", t))
                dve.wait_ge(*(at("turn", 5, 2) if t == 0 else at("k_turned", 0, 1)))
                turn(k_x[:, t, :], ("k_axial", t), 0)
                for n in range(2):
                    r = slice(64 * n, 64 * n + 64)
                    dve.tensor_tensor(ak_dup[r, 2 * t + n, :], turned[r, 0, :], turned[r, 1, :], ALU.add)\
                        .then_inc(*mark("k_turned", t, n))

            def q_scale():
                dve.wait_ge(*at("q_mean", 7))
                dve.wait_ge(*at("dve_read", "r_cols", 3))
                for t in range(TT):
                    dve.tensor_scalar(q_mean[:, t, :], q_mean[:, t, :], r_col[:, t:t + 1], r_col[:, t:t + 1],
                                      ALU.mult, ALU.mult).then_inc(*(mark("q_means", 0) if t else mark("q_mean_0", 0)))
                dve.wait_ge(*at("q_rms", 0))
                dve.reciprocal(q_mean[:, :, :], q_mean[:, :, :]).then_inc(*mark("q_rstd", 0))
                dve.wait_ge(*at("q_rstd", 0))
                for t in range(TT):
                    dve.tensor_scalar(q_mean[:, t, :], q_mean[:, t, :], r_col[:, t:t + 1], None, ALU.mult)\
                        .then_inc(*mark("q_factor", t))
                dve.wait_ge(*at("q_factor", 1))

            def att_a(h):
                o = 8 * (h % 3)
                dve.wait_ge(*at("job", "att", h))
                if h >= 3:
                    dve.wait_ge(*at("act_read", "att", h - 3))
                dve.tensor_reduce(small[:, o:o + 2], bank("att", h)[:, :].rearrange("p (q s) -> p q s", q=TT),
                                  AX.X, ALU.max).then_inc(*mark("att_red", h))
                dve.wait_ge(*at("att_red", h))
                dve.scalar_tensor_tensor(out=small[:, o + 2:o + 4], in0=small[:, o:o + 2], scalar=-1.0,
                                         in1=q_mean[:, :, h], op0=ALU.mult, op1=ALU.mult).then_inc(*mark("att_max", h))

            def att_b(h):
                o = 8 * (h % 3)
                dve.wait_ge(*at("act_read", "att", h))
                dve.reciprocal(small[:, o + 6:o + 8], small[:, o + 4:o + 6]).then_inc(*mark("att_rden", h))
                dve.wait_ge(*at("att_rden", h))
                for q in range(TT):
                    pr = att_p[:, h % 3, q, :]
                    dve.tensor_scalar(pr, pr, small[:, o + 6 + q:o + 7 + q], None, ALU.mult)\
                        .then_inc(*mark("att_scaled", h, q))

            def att_c(m):
                dve.wait_ge(*at("job", "att_o", m))
                dve.tensor_copy(y_t[:, m, :], bank("att_o", m)[:, 0:S]).then_inc(*mark("dve_read", "att_o", m))
                same(("full", 4, m), ("dve_read", "att_o", m))

            def gla(n):
                if n == 0:
                    dve.memset(ada[96:128, 0, :], 0.0).then_inc(*mark("w_gate_zero", 0))

            def gla_in(n):
                for m in range(1 if n == 0 else 2):
                    if 5 <= n < 9:
                        continue
                    job = ("gla", n, m)
                    dve.wait_ge(*at("job", *job))
                    if n == 0:
                        dve.wait_ge(*at("rstd", 5))
                        ins = dve.tensor_tensor(z_t[96:128, 0, :], bank(*job)[96:128, 0:S], rstd[96:128, :], ALU.mult)
                    elif n < 3:
                        ins = dve.scalar_tensor_tensor(out=gq[:, 2 * (n - 1) + m, :], in0=bank(*job)[:, 0:S],
                                                       scalar=float(P) ** -0.5, in1=rstd[:, :],
                                                       op0=ALU.mult, op1=ALU.mult)
                    else:
                        dst = gk[:, 2 * (n - 3) + m, :] if n < 5 else gr[:, 2 * (n - 9) + m, :]
                        ins = dve.tensor_tensor(dst, bank(*job)[:, 0:S], rstd[:, :], ALU.mult)
                    ins.then_inc(*mark("dve_read", *job))

            def gate(h):
                dve.wait_ge(*at("gate_abs", h, 1))
                for n in range(2):
                    dve.tensor_scalar(work[:, 2 + n, :], bank("logit", h)[:, n * S:(n + 1) * S],
                                      col("b_gate", 4 * n + h), 0.0, ALU.add, ALU.min)\
                        .then_inc(*mark("gate_min", h, n))
                dve.wait_ge(*at("gate_min", h, 1))
                dve.wait_ge(*at("gate_ln", h))
                dve.tensor_tensor(work[:, 2:4, :], work[:, 2:4, :], work[:, 0:2, :], ALU.subtract)\
                    .then_inc(*mark("dve_read", "logit", h))
                dve.wait_ge(*at("dve_read", "logit", h))
                if h > 0:
                    dve.wait_ge(*at("gate_mid", h - 1))
                dve.tensor_tensor_scan(work[:, 4, :], cst("scan_fwd"), work[:, 2, :], 0.0, ALU.mult, ALU.add)\
                    .then_inc(*mark("gate_sum", h, 0))
                dve.tensor_tensor_scan(work[:, 5, ::-1], cst("scan_bwd")[:, ::-1], work[:, 3, ::-1], 0.0,
                                       ALU.mult, ALU.add).then_inc(*mark("gate_sum", h, 1))
                dve.wait_ge(*at("gate_sum", h, 1))
                if h > 0:
                    dve.wait_ge(*at("decay", h - 1, 1))
                sums = work[:, 4:6, :].rearrange("p n (t c) -> p (n t) c", c=P)
                dve.tensor_tensor(work[:, 6:8, :].rearrange("p n (t c) -> p (n t) c", c=P), sums,
                                  sums[:, :, HD - 1:HD].broadcast_to([P, 2 * TT, P]), ALU.subtract)\
                    .then_inc(*mark("gate_rel", h))

            def keys(h):
                dve.wait_ge(*at("decay", h, 1))
                dve.wait_ge(*at("dve_read", "gla", 4, 1))
                dve.tensor_copy(small[:, 32 + 2 * h:33 + 2 * h], qe[:, h, 0, P - 1:P]).then_inc(*mark("border", h, 0))
                dve.tensor_copy(small[:, 33 + 2 * h:34 + 2 * h], qe[:, h, 1, P:P + 1]).then_inc(*mark("border", h, 1))
                dve.wait_ge(*at("border", h, 1))
                for n in range(2):
                    dve.tensor_tensor(qe[:, h, n, :], qe[:, h, n, :], gq[:, h, :], ALU.mult)\
                        .then_inc(*mark("decayed", h, 0, n))
                    dve.tensor_tensor(ke[:, h, n, :], ke[:, h, n, :], gk[:, h, :], ALU.mult)\
                        .then_inc(*mark("decayed", h, 1, n))
                dve.wait_ge(*at("decayed", h, 1, 1))
                for n in range(2):
                    qt, kt = (1, 0) if n == 0 else (0, 1)
                    c = 4 * h + 2 * n + qt
                    dve.tensor_scalar(gq[:, h, n * P:n * P + P], qe[:, h, n, qt * P:qt * P + P], small[:, c:c + 1],
                                      None, ALU.mult).then_inc(*mark("across", h, 0, n))
                    dve.tensor_scalar(gk[:, h, n * P:n * P + P], ke[:, h, n, kt * P:kt * P + P],
                                      small[:, 32 + 2 * h + n:33 + 2 * h + n], None, ALU.mult)\
                        .then_inc(*mark("across", h, 1, n))

            def mix(h):
                dst = pair[:, h % 2, :, :].rearrange("p t s -> p (t s)").rearrange("p (n c) -> p n c", c=P)[:, 0:4:3, :]
                dve.wait_ge(*at("act_read", "pair_fwd", h))
                dve.wait_ge(*at("job", "pair_bwd", h))
                dve.copy_predicated(dst, blocks3(cst("after").bitcast(mybir.dt.uint32)),
                                    blocks3(bank("pair_bwd", h)[:, 0:S])).then_inc(*mark("dve_read", "pair_bwd", h))
                dve.wait_ge(*at("dve_read", "pair_bwd", h))
                dve.tensor_tensor(dst, dst, blocks3(cst("twice")), ALU.mult).then_inc(*mark("paired", h))

            def mixed(h):
                for m in range(2):
                    dve.wait_ge(*at("gla_square", h, m))
                    dve.tensor_scalar(y_t[:, 2 * h + m, :], bank("gla_o", h, m)[:, 0:S], col("out_norm", m), None,
                                      ALU.mult).then_inc(*mark("dve_read", "gla_o", h, m))

            def head_norm(h):
                dve.wait_ge(*at("act_read", "gla_sum", h))
                dve.reciprocal(work[:, h, :], work[:, h, :]).then_inc(*mark("gla_rstd", h))
                dve.wait_ge(*at("gla_rstd", h))
                for m in range(2):
                    j = 2 * h + m
                    dve.wait_ge(*at("gla_gate", j))
                    dve.tensor_tensor(gr[:, j, :], gr[:, j, :], work[:, h, :], ALU.mult).then_inc(*mark("gate_all", j))
                for m in range(2):
                    j = 2 * h + m
                    dve.wait_ge(*at("gate_all", j))
                    dve.tensor_tensor(y_t[:, j, :], y_t[:, j, :], gr[:, j, :], ALU.mult)\
                        .then_inc(*mark("full", 7, j))

            def finish():
                dve.wait_ge(*at("w_lo", len(SPLITS) - 1))
                for j in (0, 2):
                    dve.wait_ge(*at("job", "turned", j))
                    dve.tensor_copy(y_rows[:, j // 2, 0:512], bank("turned", j)[:, :]).then_inc(*mark("y_rows", j))

            steps = {"setup": setup, "ada": ada_step, "gains": gains, "root": root, "scaled": scaled, "rope": rope,
                     "v_norm": v_norm, "gate_mix": gate_mix, "stick_a": stick_a, "stick_b": stick_b,
                     "stick_c": stick_c, "win_a": win_a, "win_b": win_b, "win_d": win_d, "split": split,
                     "unscaled": unscaled, "tree": tree, "total": total, "rescale": rescale, "r_cols": r_cols,
                     "project": project, "ff_up": ff_up, "mlp_act": mlp_act, "add_down": add_down, "q_b": q_b,
                     "k_a": k_a, "k_b": k_b, "k_c": k_c, "q_scale": q_scale, "att_a": att_a, "att_b": att_b,
                     "att_c": att_c, "gla": gla, "gla_in": gla_in, "gate": gate, "keys": keys, "mix": mix,
                     "mixed": mixed, "head_norm": head_norm, "finish": finish}
            for step in schedule():
                if step[0] in steps:
                    steps[step[0]](*step[1:])

        @block.tensor
        def _(pe):
            seen = set()

            def operand(idx, k):
                if (idx, k) not in seen:
                    seen.add((idx, k))
                    pe.wait_ge(*at("low", idx, k))

            def weights(key):
                n = SPLIT_OF[key]
                pe.wait_ge(*at("w_lo", n))
                return n % SPLIT_SLOTS

            def used(key, event):
                same(("chunk_used", SPLIT_OF[key]), event)

            def three(dst, lhs, rhs, start, stop):
                pe.matmul(dst, lhs[0], rhs[0], start=start, stop=False, skip_group_check=True)
                pe.matmul(dst, lhs[0], rhs[1], start=False, stop=False, skip_group_check=True)
                return pe.matmul(dst, lhs[1], rhs[0], start=False, stop=stop, skip_group_check=True)

            def feature_tile(idx, key, m, width=S):
                slot = weights(key)
                dst = take(pe, *key, m)[:, 0:S]
                for k in range(KT):
                    operand(idx, k)
                    w = [wview(b, slot, KT)[:, k, m * P:m * P + P] for b in (w_hi, w_lo)]
                    ins = three(dst, w, (h_hi[:, k, :], h_lo[:, k, :]), k == 0, k == KT - 1)
                ins.then_inc(*mark("job", *key, m))

            def token_tile(idx, key, t):
                slot = weights(key)
                dst = take(pe, *key, t)[:, 0:S]
                for k in range(KT):
                    operand(idx, k)
                    h = [b[:, k, t * P:t * P + P] for b in (h_hi, h_lo)]
                    w = [wview(b, slot, KT)[:, k, :] for b in (w_hi, w_lo)]
                    ins = three(dst, h, w, k == 0, k == KT - 1)
                ins.then_inc(*mark("job", *key, t))

            def project_chunk(idx, key, tile=feature_tile, n=2):
                if key in FIRST_USE and tile is feature_tile and n == 2:
                    slot = weights(key)
                    dst = [take(pe, *key, m)[:, 0:S] for m in range(n)]
                    for k in range(KT):
                        operand(idx, k)
                        for m in range(n):
                            w = [wview(b, slot, KT)[:, k, m * P:m * P + P] for b in (w_hi, w_lo)]
                            ins = three(dst[m], w, (h_hi[:, k, :], h_lo[:, k, :]), k == 0, k == KT - 1)
                            if k == KT - 1:
                                ins.then_inc(*mark("job", *key, m))
                else:
                    for m in range(n):
                        tile(idx, key, m)
                used(key, ("job", *key, n - 1))

            def setup():
                pe.wait_ge(*at("const_landed", 0))
                ident = cst("ident")
                for j in range(len(ROWS)):
                    n = sum(ROWS[j].values())
                    if j == 0:
                        pe.wait_ge(*at("rows_landed", "conv_b"))
                    pe.transpose(take(pe, "rows", j)[:, 0:n], rows[0:n, j, :], ident[0:n, 0:n])\
                        .then_inc(*mark("job", "rows", j))
                pe.wait_ge(*at("x_landed", 0))
                for j in range(4):
                    dst = take(pe, "x", j)
                    for kk in range(2):
                        for t in range(TT):
                            k = 2 * j + kk
                            ins = pe.transpose(dst[:, kk * S + t * P:kk * S + t * P + P],
                                               x_rows[:, t, k * P:k * P + P], ident)
                    ins.then_inc(*mark("job", "x", j))
                pe.wait_ge(*at("w_sp_landed", 0))
                dst = take(pe, "w_sp", 0)
                for g in range(4):
                    ins = pe.transpose(dst[:, g * P:(g + 1) * P], w_sp_r[:, g, :], ident)
                ins.then_inc(*mark("job", "w_sp", 0))

            def ada_step(p, q):
                if q == 3:
                    pe.wait_ge(*at("ada_added", p, 3))
                    dst = take(pe, "mod", p)
                    for k in range(KT):
                        ins = pe.matmul(dst[:, k:k + 1], ada[:, p % 2, k * P:(k + 1) * P], cst("ones")[:, 0:1],
                                        start=True, stop=True)
                    ins.then_inc(*mark("job", "mod", p))

            def root(i):
                dst = take(pe, "sum", i)[:, 0:S]
                for k in range(KT):
                    pe.wait_ge(*at("square", i, k))
                    ins = pe.matmul(dst, cst("ones"), work[:, k, :], start=(k == 0), stop=(k == KT - 1))
                ins.then_inc(*mark("job", "sum", i))

            def take_in(n):
                project_chunk(0, ("in", n), token_tile if n == 4 or n >= 8 else feature_tile)

            def rope(t):
                pe.wait_ge(*at("act_read", "in", t // 2, t % 2))
                pe.matmul(take(pe, "rope", t)[:, 0:S], cst("rope_swap"), cqk[:, t, :], start=True, stop=True)\
                    .then_inc(*mark("job", "rope", t))

            def gate_mix():
                pe.wait_ge(*at("v_normed", 0))
                pe.wait_ge(*at("dve_read", "w_sp", 0))
                for m in range(2):
                    dst = take(pe, "gated", m)
                    for g in range(2):
                        for t in range(TT):
                            f = (2 * m + g) * HD
                            ins = pe.matmul(dst[64 * g:64 * g + 64, t * P:t * P + P], v_nrm[:, t, f:f + HD],
                                            w_sp_t[:, 2 * m + g, :], start=True, stop=True, skip_group_check=True)
                    ins.then_inc(*mark("job", "gated", m))

            def stick_a(h):
                pe.wait_ge(*at("act_read", "in", 7, 1))
                dst = take(pe, "stick", h)
                k = bk_t[:, h // 2, :]
                pe.matmul(dst[:, 0:S], k[:, 0:P], bqz[:, h, :], start=True, stop=False, skip_group_check=True)
                pe.matmul(dst[:, S:SP3], k[:, P:S], bqz[:, h, P:S], start=False, stop=False, skip_group_check=True)\
                    .then_inc(*mark("job", "stick", h))

            def stick_b(h):
                pe.wait_ge(*at("stick_masked", h))
                s, dst = stick(h), bank("stick", h)
                pe.matmul(dst[:, 0:S], cst("tail"), s[:, 0:S], start=False, stop=False, skip_group_check=True)
                pe.matmul(dst[:, P:S], cst("tail_all"), s[:, S:SP3], start=False, stop=False, skip_group_check=True)
                pe.matmul(dst[:, S:SP3], cst("tail"), s[:, S:SP3], start=False, stop=True, skip_group_check=True)\
                    .then_inc(*mark("stick_tail", h))

            def values_out(dst, h, column, prob):
                o = 64 * (h % 2)
                pe.matmul(dst[o:o + 64, 0:S], vals[:, 0, column:column + HD], prob[:, 0:S], start=True, stop=False,
                          skip_group_check=True)
                return pe.matmul(dst[o:o + 64, P:S], vals[:, 1, column:column + HD], prob[:, S:SP3], start=False,
                                 stop=True, skip_group_check=True)

            def stick_c(m):
                dst = take(pe, "stick_o", m)
                for h in (2 * m, 2 * m + 1):
                    pe.wait_ge(*at("stick_weight", h))
                    pe.wait_ge(*at("act_read", "in", 10, 1))
                    ins = values_out(dst, h, h * HD, stick(h))
                ins.then_inc(*mark("job", "stick_o", m))

            def win_a(h):
                if h == 0:
                    pe.wait_ge(*at("roped", 5, 2))
                dst = take(pe, "win", h)
                pe.matmul(dst[:, 0:P], cqz[:, h, 0:P], ck_t[:, h // 2, 0:P], start=True, stop=True,
                          skip_group_check=True)
                pe.matmul(dst[:, P:SP3], cqz[:, h, P:S], ck_t[:, h // 2, :], start=True, stop=True,
                          skip_group_check=True).then_inc(*mark("job", "win", h))

            def win_c(h):
                pe.wait_ge(*at("win_scaled", h, 1))
                dst = take(pe, "win_t", h)
                for n in range(3):
                    ins = pe.transpose(dst[:, n * P:(n + 1) * P], win_p(h)[:, n * P:(n + 1) * P], cst("ident"))
                ins.then_inc(*mark("job", "win_t", h))

            def win_d(m):
                dst = take(pe, "win_o", m)
                for h in (2 * m, 2 * m + 1):
                    pe.wait_ge(*at("act_read", "win_t", h))
                    ins = values_out(dst, h, 6 * HD + h * HD, win_pt(h))
                ins.then_inc(*mark("job", "win_o", m))

            def project(kind, n):
                project_chunk(USES[kind], (kind, n))

            def ff_up(i):
                if i == 0:
                    ring["set"] = range(4)
                project_chunk(2, ("gate", i))
                project_chunk(2, ("val", i))

            def mlp_up(layer, i):
                if i == 0:
                    ring["set"] = range(4)
                project_chunk(5 + 3 * layer, ("mlp_in", layer, i))

            def down(*key):
                i = key[-1]
                last = i == (FF_STEPS if key[0] == "down" else MLP_STEPS) - 1
                slot = weights(key)
                for f in range(2):
                    pe.wait_ge(*at("hidden_lo", *key, f))
                for k in range(KT):
                    b = 4 + k // 2
                    if i == 0 and k % 2 == 0 and b in ring["last"]:
                        pe.wait_ge(*evacuated(*ring["last"][b]))
                    dst = psum[b][:, (k % 2) * S:(k % 2 + 1) * S]
                    for f in range(2):
                        w = [wview(x, slot, 2)[:, f, k * P:k * P + P] for x in (w_hi, w_lo)]
                        n = 2 * (i % 2) + f
                        ins = three(dst, w, (a_hi[:, n, :], a_lo[:, n, :]), i == 0 and k % 2 == 0 and f == 0,
                                    last and f == 1)
                    if last:
                        ins.then_inc(*mark("summed", *key[:-1], k))
                    elif k == KT - 1:
                        ins.then_inc(*mark("added", *key))
                used(key, ("summed", *key[:-1], KT - 1) if last else ("added", *key))

            def add_down(*key):
                for b in range(4, 8):
                    ring["last"][b] = ("acc", *key, b)
                ring["set"] = range(8)

            def qkv(n):
                project_chunk(3, ("qkv", n), token_tile if n == 4 else feature_tile)

            def total(i):
                pe.wait_ge(*at("tree", i, 2))
                pe.matmul(take(pe, "sum", i)[:, 0:S], cst("ones"), work[:, 0, :], start=True, stop=True)\
                    .then_inc(*mark("job", "sum", i))

            def r_cols(i):
                pe.wait_ge(*(at("rstd_both", 3) if i == 3 else at("rstd", i)))
                dst, src = take(pe, "r_cols", i), (rstd_x if i == 3 else rstd)
                for t in range(TT):
                    ins = pe.matmul(dst[:, t:t + 1], src[0:1, t * P:t * P + P], cst("one")[0:1, 0:1], start=True,
                                    stop=True)
                ins.then_inc(*mark("job", "r_cols", i))

            def q_b(t):
                dst = take(pe, "axial", t)
                pe.wait_ge(*at("act_read", "qkv", Q_CHUNK[t], t % 2))
                pe.matmul(dst[:, 0:S], cst("axial_swap"), qx[:, t % 4, :], start=True, stop=True,
                          skip_group_check=True)
                for n in range(TT):
                    ins = pe.matmul(dst[:, S + 2 * n:S + 2 * n + 2], q_sq[:, t % 2, n * P:n * P + P],
                                    cst("head_pick"), start=True, stop=True, skip_group_check=True)
                ins.then_inc(*mark("job", "axial", t))

            def k_b(t):
                pe.wait_ge(*at("k_square", t))
                pe.matmul(take(pe, "k_mean", t)[:, 0:S], cst("head_mean"), q_sq[:, t, :], start=True, stop=True)\
                    .then_inc(*mark("job", "k_mean", t))

            def k_c(t):
                pe.wait_ge(*at("k_normed", t))
                pe.matmul(take(pe, "k_axial", t)[:, 0:S], cst("axial_swap"), k_x[:, t, :], start=True, stop=True)\
                    .then_inc(*mark("job", "k_axial", t))

            def att_a(h):
                if h == 0:
                    pe.wait_ge(*at("turn", 7, 2))
                    for g in range(4):
                        pe.wait_ge(*at(f"k_doubled{g}", 0))
                dst = take(pe, "att", h)
                for q in range(TT):
                    ins = pe.matmul(dst[:, q * S:(q + 1) * S], aqz[:, h, q * P:q * P + P], ak_dup[:, h // 4, :],
                                    start=True, stop=True, skip_group_check=True)
                ins.then_inc(*mark("job", "att", h))

            def att_b(h):
                pe.wait_ge(*at("att_scaled", h, 1))
                dst = take(pe, "att_t", h)
                for q in range(TT):
                    for k in range(TT):
                        ins = pe.transpose(dst[:, k * S + q * P:k * S + q * P + P],
                                           att_p[:, h % 3, q, k * P:k * P + P], cst("ident"))
                ins.then_inc(*mark("job", "att_t", h))

            def att_o(h):
                pe.wait_ge(*at("act_read", "att_t", h))
                m = h // 2
                dst = take(pe, "att_o", m) if h % 2 == 0 else psum[banks[("att_o", m)]]
                o = 64 * (h % 2)
                g = h // 4
                for k in range(TT):
                    ins = pe.matmul(dst[o:o + 64, 0:S], v2[:, k, g * HD:g * HD + HD], att_pt[:, h % 2, k, :],
                                    start=(k == 0), stop=(k == TT - 1), skip_group_check=True)
                if h % 2:
                    ins.then_inc(*mark("job", "att_o", m))
                    same(("att_pv", h), ("job", "att_o", m))
                else:
                    ins.then_inc(*mark("att_pv", h))

            def gla(n):
                if n == 0:
                    project_chunk(6, ("gla", 0), n=1)
                else:
                    project_chunk(6, ("gla", n), token_tile if 5 <= n < 9 else feature_tile)

            def gate(h):
                if h == 0:
                    pe.wait_ge(*at("w_gate_landed", 1))
                    pe.wait_ge(*at("dve_read", "gla", 0, 0))
                dst = take(pe, "logit", h)
                for n in range(2):
                    ins = pe.matmul(dst[:, n * S:(n + 1) * S], w_gate[:, n, h * P:h * P + P], z_t[96:128, 0, :],
                                    start=True, stop=True, skip_group_check=True)
                ins.then_inc(*mark("job", "logit", h))

            def mix(h):
                pe.wait_ge(*at("across", h, 1, 1))
                fwd = take(pe, "pair_fwd", h)
                for c, k, q in ((0, ke[:, h, 0, 0:P], qe[:, h, 0, 0:P]), (1, gk[:, h, 0:P], gq[:, h, 0:P]),
                                (2, gk[:, h, P:S], gq[:, h, P:S]), (3, ke[:, h, 0, P:S], qe[:, h, 0, P:S])):
                    ins = pe.matmul(fwd[:, c * P:c * P + P], k, q, start=True, stop=True, skip_group_check=True)
                ins.then_inc(*mark("job", "pair_fwd", h))
                bwd = take(pe, "pair_bwd", h)
                for t in range(TT):
                    ins = pe.matmul(bwd[:, t * P:t * P + P], ke[:, h, 1, t * P:t * P + P],
                                    qe[:, h, 1, t * P:t * P + P], start=True, stop=True, skip_group_check=True)
                ins.then_inc(*mark("job", "pair_bwd", h))

            def mixed(h):
                pe.wait_ge(*at("paired", h))
                pe.wait_ge(*at("act_read", "gla", 8, 1))
                for m in range(2):
                    dst = take(pe, "gla_o", h, m)
                    for t in range(TT):
                        ins = pe.matmul(dst[:, 0:S], gv[:, t, h * S + m * P:h * S + m * P + P],
                                        pair[:, h % 2, t, :], start=(t == 0), stop=(t == TT - 1))
                    ins.then_inc(*mark("job", "gla_o", h, m))

            def head_sum(h):
                dst = take(pe, "gla_sum", h)[:, 0:S]
                for m in range(2):
                    pe.wait_ge(*at("gla_square", h, m))
                    ins = pe.matmul(dst, cst("ones"), gla_sq[:, 2 * (h % 2) + m, :], start=(m == 0), stop=(m == 1))
                ins.then_inc(*mark("job", "gla_sum", h))

            def finish():
                for j in range(4):
                    dst = take(pe, "turned", j)
                    for n in range(4):
                        k = 4 * (j % 2) + n
                        pe.wait_ge(*at("y_normed", k))
                        ins = pe.transpose(dst[:, n * P:n * P + P], y_t[:, k, (j // 2) * P:(j // 2) * P + P],
                                           cst("ident"))
                    ins.then_inc(*mark("job", "turned", j))

            steps = {"setup": setup, "ada": ada_step, "root": root, "in": take_in, "rope": rope,
                     "gate_mix": gate_mix, "stick_a": stick_a, "stick_b": stick_b, "stick_c": stick_c,
                     "win_a": win_a, "win_c": win_c, "win_d": win_d, "project": project, "ff_up": ff_up,
                     "mlp_up": mlp_up, "down": down, "add_down": add_down, "qkv": qkv, "q_b": q_b, "k_b": k_b,
                     "k_c": k_c, "total": total, "r_cols": r_cols, "att_a": att_a, "att_b": att_b, "att_o": att_o,
                     "gla": gla, "gate": gate, "mix": mix, "mixed": mixed, "head_sum": head_sum,
                     "finish": finish}
            for step in schedule():
                if step[0] in steps:
                    steps[step[0]](*step[1:])
    return marks, banks


_INS = ['x', 'c', 'positions', 'w_ada', 'b_ada', 'g_mix', 'w_in', 'g_sgu', 'w_sp', 'b_sp', 'w_out', 'g_ffn', 'w_up',
        'conv_w', 'conv_b', 'w_down', 'g_final', 'norm_mix_2', 'norm_mlp_2', 'attn_w_qkv_2', 'attn_q_norm_2',
        'attn_k_norm_2', 'attn_w_o_2', 'gla_w_in_2', 'gla_w_gate_up_2', 'gla_b_gate_2', 'gla_out_norm_2',
        'gla_w_o_2', 'mlp_w_in_2', 'mlp_w_out_2', 'final_norm_2']


def kernel(**inputs):
    import concourse.bacc as _bacc
    from concourse.bass_utils import run_bass_kernel_spmd as _run

    arrays = {f"in_{name}_dram": np.ascontiguousarray(inputs[name]) for name in _INS}
    arrays["in_const_dram"] = constants()
    known = None
    for _ in range(2):
        nc = _bacc.Bacc("TRN2", target_bir_lowering=False, num_devices=1)
        a = {name[3:-5]: nc.dram_tensor(name, v.shape, mybir.dt.from_np(v.dtype), kind="ExternalInput").ap()
             for name, v in arrays.items()}
        out = nc.dram_tensor("out_0_dram", (1, S, D), F32, kind="ExternalOutput").ap()
        known = build(nc, a, out, known)
    r = _run(nc, [arrays], core_ids=[0])
    return r.results[0]["out_0_dram"]
```

```python
from contextlib import ExitStack

import numpy as np

import concourse.bass as bass
from concourse import mybir

ALU = mybir.AluOpType
ACT = mybir.ActivationFunctionType
AX = mybir.AxisListType
F32 = mybir.dt.float32
F32R = mybir.dt.float32r

P = 128
D = 1024
S = 256
KT = D // P
TT = S // P
HD = 64
EPS = 1e-6
D_FF = 2816
FF_STEPS = D_FF // S
MLP_STEPS = 4 * D // S
GLA_IN = 3104
CHUNK = KT * S
RAW_SLOTS = 4
SPLIT_SLOTS = 3
SP3 = 3 * P
MAGIC = 12582912.0
TWO_PI = (6.28125, 0.0019350051879882812, 3.0199159819e-07)
PI_BELOW = 3.1415925

IN_COLS = [1664, 1920, 2176, 512, 768, 1024, 0, 256, 1280, (1536, 2432), 2560]
IN_U, IN_V = 6, 7
QKV = [0, 1, 2, 4, 5, 3]
GLA = [12, 0, 1, 2, 3, 4, 5, 6, 7, 8, 9, 10, 11]

CONST_W = {
    "ident": P, "ones": P, "inv_freq": 1, "eps": 1, "one": 1, "tail": P, "tail_all": P, "before": P,
    "window": 3 * SP3, "upto": P,
    "rope_swap": P, "axial_swap": P, "axial_cos": S, "axial_sin": S, "head_mean": P,
    "head_pick": 2, "after": S, "twice": S, "scan_fwd": S, "scan_bwd": S,
}
CONST_AT, CONST_COLS = {}, 0
for _name, _w in CONST_W.items():
    CONST_AT[_name] = (CONST_COLS, _w)
    CONST_COLS += _w
FIRST_CONST = CONST_AT["tail"][0]

ROWS = [
    {"c": 8},
    {"b_ada": 48, "g_mix": 8, "g_ffn": 8, "g_final": 8, "g_sgu": 2},
    {"norm_mix": 16, "norm_mlp": 16, "b_gate": 8, "out_norm": 2, "q_norm": 1, "k_norm": 1},
    {"conv_w0": 22 * 2, "conv_w1": 22 * 2},
    {"conv_w2": 22 * 2, "conv_b": 22 * 2},
]
COL_AT, N_COLS = {}, 0
for _rows in ROWS:
    for _name, _n in _rows.items():
        COL_AT[_name] = N_COLS
        N_COLS += _n


def constants():
    f = np.float32
    r = np.arange(P)
    k, q = r[:, None], r[None, :]
    t = np.arange(S)
    out = {}
    out["ident"] = (k == q)
    out["ones"] = np.ones((P, P))
    out["tail"] = -(k >= q).astype(f)
    out["tail_all"] = -np.ones((P, P))
    out["before"] = (k < q)
    win = []
    for dil in (1, 4, 16):
        for qb, width in ((0, P), (1, S)):
            back = (qb * P + r)[:, None] - np.arange(width)[None, :]
            ok = (back >= 0) & (back % dil == 0) & (back <= 128 * dil)
            win.append(np.where(ok, 0.0, -1e30))
    out["window"] = np.concatenate(win, 1)
    out["upto"] = (k <= q)
    for name, w in (("rope_swap", 32), ("axial_swap", 16)):
        low = (q % (2 * w)) < w
        out[name] = np.where(low & (k == q + w), -1.0, 0.0) + np.where(~low & (k == q - w), 1.0, 0.0)
    inv = (f(10000.0) ** (-np.arange(0, 32, 2, dtype=f) / f(32))).astype(f)
    pos = np.where((r % 64 < 32)[:, None], (t // 64)[None, :], (t % 64)[None, :]).astype(f)
    ang = pos * inv[r % 16][:, None]
    out["axial_cos"], out["axial_sin"] = np.cos(ang), np.sin(ang)
    out["head_mean"] = (k // HD == q // HD) / HD
    out["head_pick"] = (r[:, None] // HD == np.arange(2)[None, :]) / HD
    out["after"], out["twice"] = np.tile(k > q, (1, TT)), np.tile(1.0 + (k == q), (1, TT))
    out["scan_fwd"] = np.broadcast_to(t % P != 0, (P, S))
    out["scan_bwd"] = np.broadcast_to(t % P != P - 1, (P, S))
    inv = (f(10000.0) ** (-np.arange(0, HD, 2, dtype=f) / f(HD))).astype(f)
    out["inv_freq"] = inv[r % 32][:, None]
    out["eps"] = np.full((P, 1), EPS)
    out["one"] = np.ones((P, 1))
    return np.ascontiguousarray(np.concatenate([np.asarray(out[n], f) for n in CONST_W], 1))


def weight_stream():
    ada = [("ada", p, q) for p in range(2, 5) for q in range(4)]
    s = [("ada", p, q) for p in (1, 0) for q in range(4)]
    for n in range(11):
        s.append(("in", n))
        s += [ada.pop(0)] if n > 0 else []
    s += [("out", 0), ("out", 1), ("ada", 4, 2), ("out", 2), ("ada", 4, 3), ("ada", 5, 0), ("out", 3),
          ("ada", 5, 1), ("gate", 0), ("ada", 5, 2), ("val", 0), ("ada", 5, 3)]
    for i in range(1, FF_STEPS + 1):
        s += [("gate", i), ("val", i)] if i < FF_STEPS else []
        s += [("down", i - 1)]
    s += [("qkv", n) for n in range(6)]
    s += [("wo", n) for n in range(4)]
    for layer in range(2):
        if layer == 1:
            s += [("gla", n) for n in range(13)]
            s += [("gla_out", n) for n in range(4)]
        for i in range(MLP_STEPS + 1):
            s += [("mlp_in", layer, i)] if i < MLP_STEPS else []
            s += [("mlp_out", layer, i - 1)] if i > 0 else []
    return s


STREAM = weight_stream()
LOAD_OF = {key: n for n, key in enumerate(STREAM)}
SPLITS = [key for key in STREAM if key[0] != "ada"]
SPLIT_OF = {key: n for n, key in enumerate(SPLITS)}


def schedule():
    ada = [("ada", p, q) for p in range(2, 5) for q in range(4)]
    s = [("setup",), ("ada", 1, 0), ("ada", 1, 1), ("turn_x",), ("rows", 1), ("ada", 1, 2), ("ada", 1, 3),
         ("ada", 0, 0), ("root", 0), ("mod", 1), ("ada", 0, 1), ("ada", 0, 2), ("ada", 0, 3), ("mod", 0),
         ("gains", 0), ("scaled", 0), ("angles",)]
    extra = {1: [("rope", 0), ("rope", 1)], 2: [("rope", 2), ("rope", 3)], 3: [("rope", 4), ("rope", 5), ("w_sp",)],
             4: [("win_a", 0), ("win_a", 1), ("rows", 2), ("rows", 3), ("rows", 4)],
             5: [("win_a", 2)],
             6: [("win_a", 3), ("stick_a", 0), ("stick_a", 1)],
             7: [("win_a", 4), ("v_norm",), ("stick_b", 0), ("stick_b", 1), ("stick_a", 2)],
             8: [("win_a", 5), ("stick_a", 3), ("stick_b", 2)],
             9: [("win_b",), ("stick_a", 4), ("gate_mix",), ("stick_b", 3), ("stick_a", 5)],
             10: [("win_c", 0), ("win_c", 1), ("split", 1, 0), ("split", 1, 1), ("stick_b", 4), ("stick_b", 5),
                  ("stick_c", 0), ("win_c", 2), ("win_c", 3), ("win_d", 0), ("stick_c", 1), ("split", 1, 2),
                  ("win_c", 4), ("win_c", 5), ("win_d", 1), ("split", 1, 3), ("stick_c", 2), ("mod", 3),
                  ("win_d", 2), ("split", 1, 4), ("split", 1, 5), ("split", 1, 6), ("split", 1, 7)]}
    extra[5].append(("mod", 2))
    for n in range(11):
        s.append(("in", n))
        s += [ada.pop(0)] if n > 0 else []
        s += extra.get(n, [])
    s += [("gains", 1), ("ada", 4, 2), ("project", "out", 0), ("ada", 4, 3), ("ada", 5, 0), ("project", "out", 1),
          ("ada", 5, 1), ("project", "out", 2), ("mod", 4), ("ada", 5, 2), ("project", "out", 3), ("gains", 2)]
    s += [("root", 1), ("scaled", 1), ("ada", 5, 3)]
    for i in range(FF_STEPS + 1):
        s += [("ff_up", i)] if i < FF_STEPS else []
        s += [("mod", 5), ("gains", 3)] if i == 1 else []
        s += [("down", "down", i - 1)] if i > 0 else []
    s += [("add_down", "down"), ("unscaled", 3)] + [("squares", 2, n) for n in range(4)] + [("tree", 2)]
    s += [("qkv", 0), ("total", 2), ("rescale", 2)] + [("squares", 3, n) for n in range(4)] + [("tree", 3)]
    s += [("q_a", 0), ("q_a", 1), ("qkv", 1), ("q_b", 0), ("q_b", 1), ("q_a", 2), ("q_a", 3), ("qkv", 2), ("total", 3),
          ("q_b", 2), ("q_b", 3), ("q_a", 4), ("q_a", 5), ("qkv", 3), ("r_cols", 3), ("k_a", 0),
          ("k_a", 1), ("q_b", 4), ("q_b", 5), ("qkv", 4), ("q_scale", 0, 12), ("k_b", 0), ("k_b", 1), ("qkv", 5), ("q_a", 6),
          ("q_a", 7), ("k_c", 0), ("k_c", 1), ("q_b", 6), ("q_b", 7), ("q_scale", 12, 16)]
    s += [("att_a", 0), ("att_a", 1)]
    for h in range(16):
        s += [("att_scale", h)] + ([("att_a", h + 2)] if h < 14 else [])
        s += [("att_b", h)] + ([("att_o", h - 1)] if h else [])
        s += [("att_c", h // 2 - 1)] if h >= 2 and h % 2 == 0 else []
        s += [("split_hi", 4, h // 2 - 1)] if h >= 3 and h % 2 == 1 else []
        s += [("split_lo", 4, h // 2 - 2)] if h >= 4 and h % 2 == 0 else []
    s += [("split_lo", 4, 6), ("att_o", 15), ("att_c", 7), ("split", 4, 7)]
    for n in range(4):
        s += [("project", "wo", n)] + ([("squares", 4, n)] if n < 3 else [])
    for layer in range(2):
        i = 4 + 2 * layer
        if layer == 1:
            s += [("unscaled", 5)] + [("squares", 5, n) for n in range(4)] + [("tree", 5)]
            s += [("gla", 0), ("gla", 1), ("total", 5)]
            s += [("gla_in", 0), ("gla_in", 1), ("gla", 2), ("gla_in", 2), ("logit", 0), ("gla", 3), ("gate", 0),
                  ("gla_in", 3), ("logit", 1), ("gla", 4), ("gate", 1), ("gla_in", 4), ("logit", 2), ("gla", 5),
                  ("keys", 0), ("r_cols", 5), ("gate", 2), ("gla_in", 5), ("logit", 3)]
            s += [("gla", 6), ("keys", 1), ("gate", 3), ("gla_in", 6), ("keys", 2), ("gla", 7), ("mix", 0),
                  ("gla_in", 7), ("keys", 3), ("gla", 8), ("mix", 1), ("gla_in", 8), ("gla", 9), ("mixed", 0),
                  ("mix", 2), ("mixed", 1), ("gla_in", 9), ("gla", 10), ("head_sum", 0), ("head_sum", 1),
                  ("head_root", 0), ("head_root", 1), ("mixed", 2), ("mix", 3), ("gla_in", 10),
                  ("head_norm", 0), ("head_norm", 1), ("gla", 11), ("mixed", 3), ("head_sum", 2), ("head_sum", 3), ("head_root", 2),
                  ("head_root", 3), ("gla_in", 11), ("head_norm", 2), ("head_norm", 3)]
            s += [("head_gate", j) for j in range(6)]
            s += [("gla", 12)] + [("split_hi", 7, k) for k in range(6)] + [("gla_in", 12)]
            s += [("split_lo", 7, k) for k in range(6)]
            s += [("head_gate", 6), ("head_gate", 7), ("split", 7, 6), ("split", 7, 7)]
            for n in range(4):
                s += [("project", "gla_out", n)] + ([("squares", 6, n)] if n < 3 else [])
        s += [("unscaled", i), ("squares", i, 3), ("tree", i), ("mlp_up", layer, 0), ("total", i)]
        for n in range(MLP_STEPS + 1):
            s += [("mlp_up", layer, n)] if 0 < n < MLP_STEPS else []
            s += [("mlp_act", layer, n)] if n < MLP_STEPS else []
            s += [("down", "mlp_out", layer, n - 1)] if n > 0 else []
        s += [("add_down", "mlp_out", layer)]
    s += [("finish",)]
    return s


NEXT_NORM = {"out": 1, "down": 2, "wo": 4, "gla_out": 6}
X_OF_NORM = {3: 2, 4: 4, 5: 5, 6: 6}
SET_OF_NORM = {0: 0, 1: 2, 3: 3, 4: 5, 5: 6, 6: 8}
Q_CHUNK = [0, 0, 1, 1, 2, 2, 5, 5]
LAST_USE = {0: ("in", 10), 1: ("out", 3), 2: ("val", FF_STEPS - 1), 3: ("qkv", 5), 4: ("wo", 3),
            5: ("mlp_in", 0, MLP_STEPS - 1), 6: ("gla", 12), 7: ("gla_out", 3), 8: ("mlp_in", 1, MLP_STEPS - 1)}
FIRST_USE = {("in", 0), ("out", 0), ("gate", 0), ("qkv", 0), ("wo", 0), ("mlp_in", 0, 0), ("gla_out", 0),
             ("mlp_in", 1, 0)}
USES = {"in": 0, "out": 1, "gate": 2, "val": 2, "qkv": 3, "wo": 4, "gla": 6, "gla_out": 7}


def build(nc, a, out, known):
    marks, banks, counts, sems = {}, {}, {}, {}
    ctx = ExitStack()
    with ctx:
        def sb(name, shape, dt=F32):
            return ctx.enter_context(nc.sbuf_tensor(name, shape, dt))

        def sem(name):
            if name not in sems:
                sems[name] = ctx.enter_context(nc.semaphore(name))
            return sems[name]

        def mark(name, *event, by=1):
            counts[name] = counts.get(name, 0) + by
            assert (name, *event) not in marks, (name, event)
            marks[(name, *event)] = (name, counts[name])
            return sem(name), by

        def same(event, as_event):
            assert event not in marks, event
            marks[event] = marks[as_event]

        def at(*event):
            name, value = (event[0], 1) if known is None else known[0][event]
            return sem(name), value

        raw = sb("raw", [P, RAW_SLOTS, CHUNK])
        w_hi = sb("w_hi", [P, SPLIT_SLOTS, CHUNK], F32R)
        w_lo = sb("w_lo", [P, SPLIT_SLOTS, CHUNK], F32R)
        const = sb("const", [P, CONST_COLS])
        rows = sb("rows", [P, len(ROWS), P])
        cols = sb("cols", [P, N_COLS])
        mod = sb("mod", [P, 48])
        gain = sb("gain", [P, 4, KT])
        c_act = sb("c_act", [P, KT])
        ada = sb("ada", [P, 2, D])
        x_t = sb("x_t", [P, KT, S])
        h_hi = sb("h_hi", [P, KT, S], F32R)
        h_lo = sb("h_lo", [P, KT, S], F32R)
        y_t = sb("y_t", [P, KT, S])
        rstd = sb("rstd", [P, S])
        a_hi = sb("a_hi", [P, 4, S], F32R)
        a_lo = sb("a_lo", [P, 4, S], F32R)
        work = sb("work", [P, 8, S])
        arena = sb("arena", [P, 48 * S])
        rstd_x = sb("rstd_x", [P, S])
        r_col = sb("r_col", [P, TT])
        q_mean = sb("q_mean", [P, TT, 16])
        gain_qkv = sb("gain_qkv", [P, KT])
        pos_i = sb("pos_i", [P, S], mybir.dt.int32)
        small = sb("small", [P, P])
        psum = [ctx.enter_context(nc.psum_tensor(f"psum{b}", [P, 512], F32)) for b in range(8)]

        def norm_gain(i):
            return {3: gain_qkv[:, :], 4: col("norm_mlp", 0, KT), 5: col("norm_mix", KT, KT),
                    6: col("norm_mlp", KT, KT)}[i]

        def cst(name):
            o, w = CONST_AT[name]
            return const[:, o:o + w]

        def col(name, i=0, n=1):
            return cols[:, COL_AT[name] + i:COL_AT[name] + i + n]

        def area(first, n):
            return arena[:, first * S:(first + n) * S].rearrange("p (n s) -> p n s", s=S)

        def blocks3(ap):
            return ap.rearrange("p (n c) -> p n c", c=P)

        ring = {"n": 0, "last": {}, "set": range(8)}

        def evacuated(*job):
            name = "act_read" if known is not None and ("act_read", *job) in known[0] else "dve_read"
            return at(name, *job)

        def take(pe, *job):
            b = ring["set"][ring["n"] % len(ring["set"])]
            ring["n"] += 1
            if b in ring["last"]:
                pe.wait_ge(*evacuated(*ring["last"][b]))
            ring["last"][b] = job
            banks[job] = b
            return psum[b]

        def bank(*job):
            return psum[0 if known is None else known[1][job]]

        u_t, v_tok, v_nrm = area(0, 2), area(2, 2), area(4, 2)
        bqz, bk_t = area(6, 6), area(12, 3)
        vals = arena[:, 15 * S:21 * S].rearrange("p (t c) -> p t c", t=TT)
        cqk, cqz, ck_t = area(21, 6), area(27, 6), area(33, 3)
        w_sp_r = arena[:, 0:2 * S].rearrange("p (g s) -> p g s", g=4)
        w_sp_t = arena[:, 46 * S:48 * S].rearrange("p (g s) -> p g s", g=4)
        angle = area(38, 6)
        b_sp_b = arena[:, 45 * S:46 * S].rearrange("p (m s) -> p m s", m=2)

        def stick(h):
            if h < 4:
                return arena[:, 21 * S + h * SP3:21 * S + (h + 1) * SP3]
            return work[:, 6 * (h - 4):6 * (h - 4) + 2, :].rearrange("p n s -> p (n s)")[:, 0:SP3]

        def win_p(h):
            return arena[:, 36 * S + h * SP3:36 * S + (h + 1) * SP3]

        def win_pt(h):
            return arena[:, 27 * S + h * SP3:27 * S + (h + 1) * SP3]

        ff_g, ff_v, ff_s = area(0, 2), area(2, 2), area(4, 2)
        aqz, ak_dup, v2 = area(6, 16), area(22, 4), area(26, 2)
        att_p = area(28, 6).rearrange("p (b q) s -> p b q s", b=3)
        att_pt = area(34, 4).rearrange("p (b q) s -> p b q s", b=2)
        qx, q_sq, turned = area(38, 4), area(42, 2), area(44, 2)
        k_x, k_rms = area(46, 2), area(0, 2)
        gq, gk, gr, z_t = area(6, 4), area(10, 4), area(22, 8), area(30, 1)
        gv = arena[:, 14 * S:22 * S].rearrange("p (t c) -> p t c", t=TT)
        qe = area(31, 8).rearrange("p (h n) s -> p h n s", n=2)
        ke = area(39, 8).rearrange("p (h n) s -> p h n s", n=2)
        pair = area(0, 4).rearrange("p (b t) s -> p b t s", b=2)
        gla_sq = work[:, 4:8, :]
        g_last = ada[:, 1, :]
        w_gate = ada[96:128, 0, :].rearrange("p (n e) -> p n e", n=2)
        x_rows = work[:, :, :].rearrange("p n s -> p (n s)").rearrange("p (t c) -> p t c", t=TT)
        y_rows = raw[:, 0:2, 0:D]

        def wview(buf, slot, kt):
            return buf[:, slot, :].rearrange("p (k c) -> p k c", k=kt)

        def filled(buf, slot, key):
            return wview(buf, slot, KT)[:, :, 0:P] if key == ("gla", 0) else buf[:, slot, :]

        def landed(n):
            return at(f"raw_landed{n % RAW_SLOTS}", n)

        block = ctx.enter_context(nc.Block())

        @block.sync
        def _(sp):
            def column_chunk(w, c0, n=S):
                return w[:, c0:c0 + n].rearrange("(k p) c -> p k c", p=P)

            def row_chunk(w, r0):
                return w[r0:r0 + S, :].rearrange("(k p) c -> p k c", p=P)

            def sources(key):
                kind, n = key[0], key[-1]
                if kind == "ada":
                    return [(0, row_chunk(a["w_ada"][0][:, key[1] * D:(key[1] + 1) * D], n * S))], 2
                if kind == "in":
                    c0 = IN_COLS[n]
                    if isinstance(c0, tuple):
                        return [(j * P, column_chunk(a["w_in"][0], c, P)) for j, c in enumerate(c0)], KT
                    return [(0, column_chunk(a["w_in"][0], c0))], KT
                if kind == "gla" and n == 0:
                    return [(0, column_chunk(a["gla_w_in_2"][0], GLA_IN - P, P))], KT
                if kind == "down":
                    return [(0, row_chunk(a["w_down"][0], n * S))], 2
                if kind == "mlp_out":
                    return [(0, row_chunk(a["mlp_w_out_2"][key[1]], n * S))], 2
                w, c0 = {
                    "out": lambda: (a["w_out"][0], n * S), "gate": lambda: (a["w_up"][0], n * S),
                    "val": lambda: (a["w_up"][0], D_FF + n * S), "qkv": lambda: (a["attn_w_qkv_2"][0], QKV[n] * S),
                    "wo": lambda: (a["attn_w_o_2"][0], n * S), "gla": lambda: (a["gla_w_in_2"][0], GLA[n] * S),
                    "gla_out": lambda: (a["gla_w_o_2"][0], n * S),
                    "mlp_in": lambda: (a["mlp_w_in_2"][key[1]], n * S),
                }[kind]()
                return [(0, column_chunk(w, c0))], KT

            def load_rows(j):
                at_row = 0
                for name, n in ROWS[j].items():
                    if name in ("q_norm", "k_norm"):
                        g = a[f"attn_{name}_2"]
                        for e in range(2):
                            sp.dma_start(rows[at_row:at_row + 1, j, e * HD:(e + 1) * HD], g)\
                                .then_inc(*mark(f"rows{j}_landed", name, e, by=16))
                    else:
                        if name == "b_gate":
                            v = a["gla_b_gate_2"][0]
                        elif name.startswith("conv_w"):
                            v = a["conv_w"][0, int(name[-1]):int(name[-1]) + 1]
                        else:
                            v = a[{"norm_mix": "norm_mix_2", "norm_mlp": "norm_mlp_2",
                                   "out_norm": "gla_out_norm_2"}.get(name, name)]
                        v = v.rearrange("(n p) -> n p", p=P) if len(v.shape) == 1 else \
                            v.rearrange("o (n p) -> (o n) p", p=P)
                        sp.dma_start(rows[at_row:at_row + n, j, :], v)\
                            .then_inc(*mark(f"rows{j}_landed", name, by=16))
                    at_row += n

            def load_rest():
                sp.dma_start(const[:, FIRST_CONST:], a["const"][:, FIRST_CONST:])\
                    .then_inc(*mark("more_const_landed", 0, by=16))
                sp.dma_start(w_sp_r, a["w_sp"][0].rearrange("g t s -> t g s")).then_inc(*mark("w_sp_landed", 0, by=16))

            def load_b_sp():
                for g in range(4):
                    sp.dma_start(b_sp_b[64 * (g % 2):64 * (g % 2) + 64, g // 2, :],
                                 a["b_sp"][0, g:g + 1, :].broadcast_to([64, P])).then_inc(*mark("b_sp_landed", g, by=16))

            between = {3: lambda: load_rows(1), 10: load_rest, 12: lambda: load_rows(2), 13: lambda: load_rows(3),
                       14: lambda: load_rows(4), 15: load_b_sp}
            load_rows(0)
            sp.dma_start(const[:, 0:FIRST_CONST], a["const"][:, 0:FIRST_CONST])\
                .then_inc(*mark("const_landed", 0, by=16))
            for n, key in enumerate(STREAM):
                if n in between:
                    between[n]()
                if n >= RAW_SLOTS:
                    old = STREAM[n - RAW_SLOTS]
                    if old[0] == "ada":
                        sp.wait_ge(*at("ada_added", *old[1:]))
                    else:
                        sp.wait_ge(*at("w_lo", SPLIT_OF[old]))
                parts, kt = sources(key)
                slot = n % RAW_SLOTS
                for j, (c0, src) in enumerate(parts):
                    dst = wview(raw, slot, kt)[:, :, c0:c0 + src.shape[2]]
                    event = (n,) if j == len(parts) - 1 else (n, "first part")
                    sp.dma_start(dst, src).then_inc(*mark(f"raw_landed{slot}", *event, by=16))
            for t in range(TT):
                for half in range(2):
                    r = slice(512 * half, 512 * half + 512)
                    sp.wait_ge(*at("y_rows", t, half))
                    sp.dma_start(out[0, t * P:(t + 1) * P, r], y_rows[:, t, r])\
                        .then_inc(*mark("out_landed", t, half, by=16))
            sp.wait_ge(*at("out_landed", TT - 1, 1))

        @block.gpsimd
        def _(pool):
            pool.memset(bqz, 0.0).then_inc(*mark("zeroed", 0))
            pool.memset(cqz, 0.0).then_inc(*mark("zeroed", 1))
            for n, key in enumerate(SPLITS):
                r = LOAD_OF[key]
                pool.wait_ge(*landed(r))
                pool.wait_ge(*at("w_hi", n))
                pool.tensor_tensor(filled(w_lo, n % SPLIT_SLOTS, key), filled(raw, r % RAW_SLOTS, key),
                                   filled(w_hi, n % SPLIT_SLOTS, key).bitcast(F32), ALU.subtract)\
                    .then_inc(*mark("w_lo", n))

        @block.scalar
        def _(act):
            done = {"hi": 0}

            def weights_upto(n):
                while done["hi"] <= min(n, len(SPLITS) - 1):
                    m = done["hi"]
                    r = LOAD_OF[SPLITS[m]]
                    act.wait_ge(*landed(r))
                    if m >= SPLIT_SLOTS:
                        act.wait_ge(*at("chunk_used", m - SPLIT_SLOTS))
                    act.activation(filled(w_hi, m % SPLIT_SLOTS, SPLITS[m]), filled(raw, r % RAW_SLOTS, SPLITS[m]),
                                   ACT.Copy).then_inc(*mark("w_hi", m))
                    done["hi"] += 1

            def ahead(key):
                weights_upto(SPLIT_OF[key] + SPLIT_SLOTS - 1)

            def high(idx, k, src, func=ACT.Copy, **kw):
                if k == 0 and idx > 0:
                    act.wait_ge(*at("chunk_used", SPLIT_OF[LAST_USE[idx - 1]]))
                act.activation(h_hi[:, k, :], src, func, **kw).then_inc(*mark("high", idx, k))

            def split(idx, k):
                act.wait_ge(*at("full", idx, k))
                high(idx, k, y_t[:, k, :])

            def unscaled(i):
                for k in range(KT):
                    act.wait_ge(*at("x_new", X_OF_NORM[i], k))
                    high(SET_OF_NORM[i], k, x_t[:, k, :], ACT.Identity, scale=norm_gain(i)[:, k:k + 1])

            def squares(i, n):
                for k in (2 * n, 2 * n + 1):
                    act.wait_ge(*at("x_new", i, k))
                    act.activation(work[:, k, :], x_t[:, k, :], ACT.Square).then_inc(*mark("square", i, k))

            def total(i):
                act.wait_ge(*at("job", "sum", i))
                dst = rstd_x if i == 3 else rstd
                act.activation(dst[:, :], bank("sum", i)[:, 0:S], ACT.Sqrt, scale=1.0 / D, bias=cst("eps"))\
                    .then_inc(*mark("act_read", "sum", i))

            def copy(job, dst, func=ACT.Copy, **kw):
                act.wait_ge(*at("job", *job))
                act.activation(dst, bank(*job)[:, 0:S], func, **kw).then_inc(*mark("act_read", *job))

            def setup():
                act.dma_start(x_rows, a["x"][0].rearrange("(t p) c -> p t c", p=P)).then_inc(*mark("x_landed", 0, by=16))
                act.dma_start(pos_i[:, :], a["positions"].broadcast_to([P, S])).then_inc(*mark("pos_landed", 0, by=16))
                act.wait_ge(*at("cols", 0))
                act.activation(c_act[:, :], col("c", 0, KT), ACT.Silu).then_inc(*mark("c_act", 0))
                act.preload_act_table_set("sqrt_and_others")

            def turn_x():
                for j in range(4):
                    act.wait_ge(*at("job", "x", j))
                    act.activation(x_t[:, 2 * j:2 * j + 2, :], bank("x", j)[:, :].rearrange("p (k s) -> p k s", k=2),
                                   ACT.Copy).then_inc(*mark("act_read", "x", j))
                    for k in (2 * j, 2 * j + 1):
                        same(("x_new", 0, k), ("act_read", "x", j))

            def angles():
                for j in range(2):
                    act.wait_ge(*at("angle", j))
                    act.activation(angle[:, j, :], angle[:, 2 + j, :], ACT.Sin).then_inc(*mark("sine", j))

            def root(i):
                if i == 0:
                    act.wait_ge(*at("x_new", 0, KT - 1))
                for k in range(KT):
                    act.wait_ge(*at("x_new", i, k))
                    act.activation(work[:, k, :], x_t[:, k, :], ACT.Square).then_inc(*mark("square", i, k))
                copy(("sum", i), rstd[:, :], ACT.Sqrt, scale=1.0 / D, bias=cst("eps"))

            def scaled(i):
                if i == 0:
                    weights_upto(1)
                for k in range(KT):
                    act.wait_ge(*at("normed", i, k))
                    high(SET_OF_NORM[i], k, y_t[:, k, :], ACT.Identity, bias=mod[:, 24 * i + k:24 * i + k + 1])

            def take_in(n):
                ahead(("in", n))
                for m in range(2):
                    job = ("in", n, m)
                    t = 2 * n + m
                    if n < 3:
                        copy(job, cqk[:, t, :], scale=0.125 if t < 3 else 1.0)
                    elif n == IN_U:
                        act.wait_ge(*at("job", "w_sp", 0))
                        copy(job, u_t[:, m, :], ACT.Gelu_apprx_tanh)
                    elif n == IN_V:
                        copy(job, v_tok[:, m, :], ACT.Gelu_apprx_tanh)
                    elif n < 6 and t - 6 < 3:
                        act.wait_ge(*at("job", *job))
                        act.wait_ge(*at("zeroed", 0))
                        act.activation(bqz[0:64, 2 * (t - 6), :], bank(*job)[0:64, 0:S], ACT.Copy, scale=0.125)\
                            .then_inc(*mark("b_q", t - 6))
                        act.activation(bqz[64:128, 2 * (t - 6) + 1, :], bank(*job)[64:128, 0:S], ACT.Copy,
                                       scale=0.125).then_inc(*mark("act_read", *job))
                    elif n < 6:
                        copy(job, bk_t[:, t - 9, :])
                    else:
                        copy(job, vals[:, m, (n - 8) * S:(n - 7) * S])

            def v_norm():
                act.wait_ge(*at("v_sum", 0))
                act.activation(small[:, 8:16], small[:, 0:8], ACT.Sqrt, scale=1.0 / HD, bias=cst("eps"))\
                    .then_inc(*mark("v_root", 0))

            def stick_a(h):
                act.wait_ge(*at("job", "stick", h))
                if h in (0, 2):
                    act.preload_act_table_set("natural_log_exp_and_others")
                act.activation(stick(h), bank("stick", h)[:, 0:SP3], ACT.Abs).then_inc(*mark("stick_act", h, 0))
                act.wait_ge(*at("stick_act", h, 0))
                act.activation(stick(h), stick(h), ACT.Exp, scale=-1.0).then_inc(*mark("stick_act", h, 1))
                act.wait_ge(*at("stick_act", h, 1))
                act.activation(stick(h), stick(h), ACT.Ln, bias=cst("one")).then_inc(*mark("stick_act", h, 2))

            def stick_b(h):
                act.wait_ge(*at("stick_tail", h))
                act.activation(stick(h), bank("stick", h)[:, 0:SP3], ACT.Exp).then_inc(*mark("act_read", "stick", h))

            def win_a(h):
                act.wait_ge(*at("win_max", h))
                for q in range(TT):
                    pr = win_p(h)[:, 0:P] if q == 0 else win_p(h)[:, P:SP3]
                    act.activation(pr, pr, ACT.Exp, bias=small[:, 32 + 2 * h + q:33 + 2 * h + q],
                                   accum_out=small[:, 48 + 2 * h + q:49 + 2 * h + q]).then_inc(*mark("win_exp", h, q))

            def win_b():
                act.wait_ge(*at("win_rel", 0))
                act.activation(small[:, 64:76], small[:, 64:76], ACT.Exp).then_inc(*mark("win_factor", 0))

            def win_c(h):
                act.wait_ge(*at("job", "win_t", h))
                act.activation(win_pt(h), bank("win_t", h)[:, 0:SP3], ACT.Copy).then_inc(*mark("act_read", "win_t", h))

            def project(kind, n):
                ahead((kind, n))
                if n == 0:
                    act.preload_act_table_set("sqrt_and_others")

            def add_down(*key):
                act.preload_act_table_set("sqrt_and_others")

            def ff_up(i):
                ahead(("gate", i))
                for f in range(2):
                    act.wait_ge(*at("job", "gate", i, f))
                    if i > 0:
                        act.wait_ge(*at("ff_product", i - 1, f))
                    act.activation(ff_g[:, f, :], bank("gate", i, f)[:, 0:S], ACT.Identity,
                                   scale=col("conv_w2", 2 * i + f), bias=col("conv_b", 2 * i + f))\
                        .then_inc(*mark("ff_newest", "gate", i, f))
                ahead(("val", i))
                for f in range(2):
                    act.wait_ge(*at("job", "val", i, f))
                    if i > 0:
                        act.wait_ge(*at("hidden_lo", "down", i - 1, f))
                    act.activation(ff_v[:, f, :], bank("val", i, f)[:, 0:S], ACT.Identity,
                                   scale=col("conv_w2", 22 + 2 * i + f), bias=col("conv_b", 22 + 2 * i + f))\
                        .then_inc(*mark("ff_newest", "val", i, f))
                    act.wait_ge(*at("dve_read", "gate", i, f))
                    act.activation(ff_s[:, f, :], ff_g[:, f, :], ACT.Silu).then_inc(*mark("ff_silu", i, f))
                for f in range(2):
                    act.wait_ge(*at("ff_product", i, f))
                    if i >= 2 and f == 0:
                        act.wait_ge(*at("chunk_used", SPLIT_OF[("down", i - 2)]))
                    act.activation(a_hi[:, 2 * (i % 2) + f, :], ff_v[:, f, :], ACT.Copy)\
                        .then_inc(*mark("hidden_hi", "down", i, f))

            def down(*key):
                ahead(key)

            def qkv(n):
                ahead(("qkv", n))

            def q_a(t):
                job = ("qkv", Q_CHUNK[t], t % 2)
                act.wait_ge(*at("job", *job))
                act.wait_ge(*at("gain_qkv", 1))
                if t >= 4:
                    act.wait_ge(*at("turn", t - 4, 2))
                act.activation(qx[:, t % 4, :], bank(*job)[:, 0:S], ACT.Identity, scale=small[:, 120:121])\
                    .then_inc(*mark("q_gained", t))
                if t >= 2:
                    act.wait_ge(*at("job", "axial", t - 2))
                act.activation(q_sq[:, t % 2, :], bank(*job)[:, 0:S], ACT.Square).then_inc(*mark("act_read", *job))

            def k_a(t):
                act.wait_ge(*at("k_scaled", t))
                act.wait_ge(*at("job", "axial", 4 + t))
                act.activation(q_sq[:, t, :], k_x[:, t, :], ACT.Square).then_inc(*mark("k_square", t))

            def k_b(t):
                act.wait_ge(*at("job", "k_mean", t))
                act.activation(k_rms[:, t, :], bank("k_mean", t)[:, 0:S], ACT.Sqrt, bias=cst("eps"))\
                    .then_inc(*mark("act_read", "k_mean", t))
                if t == 1:
                    for m in range(TT):
                        act.wait_ge(*at("dve_read", "r_cols", 3))
                        copy(("qkv", 4, m), v2[:, m, :], ACT.Identity, scale=r_col[:, m:m + 1])

            def k_c(t):
                for n in range(2):
                    act.wait_ge(*at("k_turned", t, n))
                    act.dma_start(ak_dup[64 * (1 - n):64 * (1 - n) + 64, 2 * t + n, :],
                                  ak_dup[64 * n:64 * n + 64, 2 * t + n, :])\
                        .then_inc(*mark(f"k_doubled{2 * t + n}", 0, by=16))

            def q_scale(a, b):
                act.wait_ge(*at("q_means", a))
                act.activation(q_mean[:, :, a:b], q_mean[:, :, a:b], ACT.Sqrt, bias=cst("eps"))\
                    .then_inc(*mark("q_rms", a))

            def att_a(h):
                act.wait_ge(*at("att_max", h))
                if h >= 3:
                    act.wait_ge(*at("job", "att_t", h - 3))
                for q in range(TT):
                    c = 8 * (h % 3) + q
                    act.activation(att_p[:, h % 3, q, :], bank("att", h)[:, q * S:(q + 1) * S], ACT.Exp,
                                   scale=q_mean[:, q, h:h + 1], bias=small[:, c + 2:c + 3],
                                   accum_out=small[:, c + 4:c + 5])\
                        .then_inc(*(mark("act_read", "att", h) if q else mark("att_exp", h)))

            def att_b(h):
                act.wait_ge(*at("job", "att_t", h))
                if h >= 2:
                    act.wait_ge(*at("att_pv", h - 2))
                act.activation(att_pt[:, h % 2, :, :], bank("att_t", h)[:, :].rearrange("p (k s) -> p k s", k=TT),
                               ACT.Copy).then_inc(*mark("act_read", "att_t", h))

            def mlp_up(layer, i):
                ahead(("mlp_in", layer, i))
                if (layer, i) == (0, 2):
                    act.wait_ge(*at("w_gate_zero", 0))
                    for j in range(2):
                        act.dma_start(w_gate[16 * j:16 * j + 16, j, :], a["gla_w_gate_up_2"][0, j])\
                            .then_inc(*mark("w_gate_landed", j, by=16))
                    act.dma_start(g_last, a["final_norm_2"].rearrange("(o n) -> o n", o=1).broadcast_to([P, D]))\
                        .then_inc(*mark("g_last_landed", 0, by=16))

            def mlp_act(layer, i):
                for f in range(2):
                    act.wait_ge(*at("dve_read", "mlp_in", layer, i, f))
                    if i >= 2 and f == 0:
                        act.wait_ge(*at("chunk_used", SPLIT_OF[("mlp_out", layer, i - 2)]))
                    act.activation(a_hi[:, 2 * (i % 2) + f, :], ff_g[:, f, :], ACT.Square)\
                        .then_inc(*mark("hidden_hi", "mlp_out", layer, i, f))

            def gla(n):
                ahead(("gla", n))

            def gla_in(n):
                for m in range(2):
                    if 5 <= n < 9:
                        act.wait_ge(*at("dve_read", "r_cols", 5))
                        copy(("gla", n, m), gv[:, m, (n - 5) * S:(n - 4) * S], ACT.Identity, scale=r_col[:, m:m + 1])
                    elif n >= 9:
                        act.wait_ge(*at("dve_read", "gla", n, m))
                        j = 2 * (n - 9) + m
                        act.activation(gr[:, j, :], gr[:, j, :], ACT.Silu).then_inc(*mark("gla_gate", j))

            def gate(h):
                act.wait_ge(*at("job", "logit", h))
                if h > 0:
                    act.wait_ge(*at("dve_read", "logit", h - 1))
                for n in range(2):
                    act.activation(work[:, n, :], bank("logit", h)[:, n * S:(n + 1) * S], ACT.Abs,
                                   bias=col("b_gate", 4 * n + h)).then_inc(*mark("gate_abs", h, n))
                act.wait_ge(*at("gate_abs", h, 1))
                if h == 0:
                    act.preload_act_table_set("natural_log_exp_and_others")
                act.activation(work[:, 0:2, :], work[:, 0:2, :], ACT.Exp, scale=-1.0).then_inc(*mark("gate_exp", h))
                act.wait_ge(*at("gate_exp", h))
                act.activation(work[:, 0:2, :], work[:, 0:2, :], ACT.Ln, bias=cst("one")).then_inc(*mark("gate_ln", h))
                act.wait_ge(*at("gate_sum", h, 1))
                act.activation(small[:, 4 * h:4 * h + 4].rearrange("p (n t) -> p n t", n=2), work[:, 4:6, HD - 1::P],
                               ACT.Exp, scale=1.0 / 16).then_inc(*mark("gate_mid", h))
                act.wait_ge(*at("gate_rel", h))
                act.activation(qe[:, h, :, :], work[:, 6:8, :], ACT.Exp, scale=1.0 / 16).then_inc(*mark("decay", h, 0))
                act.activation(ke[:, h, :, :], work[:, 6:8, :], ACT.Exp, scale=-1.0 / 16).then_inc(*mark("decay", h, 1))

            def mix(h):
                act.wait_ge(*at("job", "pair_fwd", h))
                if h >= 2:
                    act.wait_ge(*at("job", "gla_o", h - 2, 1))
                act.activation(pair[:, h % 2, :, :], bank("pair_fwd", h)[:, :].rearrange("p (t s) -> p t s", t=TT),
                               ACT.Copy).then_inc(*mark("act_read", "pair_fwd", h))

            def mixed(h):
                for m in range(2):
                    act.wait_ge(*at("job", "gla_o", h, m))
                    if h > 1:
                        act.wait_ge(*at("job", "gla_sum", h - 2))
                    act.activation(gla_sq[:, 2 * (h % 2) + m, :], bank("gla_o", h, m)[:, 0:S], ACT.Square)\
                        .then_inc(*mark("gla_square", h, m))

            def head_root(h):
                act.wait_ge(*at("job", "gla_sum", h))
                act.activation(work[:, h, :], bank("gla_sum", h)[:, 0:S], ACT.Sqrt, scale=1.0 / S, bias=cst("eps"))\
                    .then_inc(*mark("act_read", "gla_sum", h))

            def finish():
                for half in range(2):
                    for t in range(TT):
                        act.wait_ge(*at("job", "turned", t, half))
                        act.activation(work[:, 4 * t + 2 * half:4 * t + 2 * half + 2, :],
                                       bank("turned", t, half)[:, :].rearrange("p (n s) -> p n s", n=2), ACT.Square,
                                       accum_out=small[:, 64 + 2 * half + t:65 + 2 * half + t])\
                            .then_inc(*mark("last_square", t, half))
                act.wait_ge(*at("last_sum", 0))
                act.activation(small[:, 70:72], small[:, 68:70], ACT.Sqrt, scale=1.0 / D, bias=cst("eps"))\
                    .then_inc(*mark("last_root", 0))

            steps = {"setup": setup, "turn_x": turn_x, "angles": angles, "add_down": add_down, "root": root,
                     "scaled": scaled,
                     "split": split, "split_hi": split, "unscaled": unscaled,
                     "squares": squares, "total": total, "in": take_in, "v_norm": v_norm,
                     "stick_a": stick_a, "stick_b": stick_b, "win_a": win_a, "win_b": win_b, "win_c": win_c,
                     "project": project, "ff_up": ff_up, "down": down, "qkv": qkv, "q_a": q_a,
                     "k_a": k_a, "k_b": k_b, "k_c": k_c, "q_scale": q_scale, "att_a": att_a, "att_b": att_b,
                     "mlp_up": mlp_up, "mlp_act": mlp_act, "gla": gla, "gla_in": gla_in, "gate": gate, "mix": mix,
                     "mixed": mixed, "head_root": head_root, "finish": finish}
            for step in schedule():
                if step[0] in steps:
                    steps[step[0]](*step[1:])

        @block.vector
        def _(dve):
            def split(idx, k):
                dve.wait_ge(*at("high", idx, k))
                dve.tensor_tensor(h_lo[:, k, :], y_t[:, k, :], h_hi[:, k, :].bitcast(F32), ALU.subtract)\
                    .then_inc(*mark("low", idx, k))

            def unscaled(i):
                for k in range(KT):
                    dve.wait_ge(*at("high", SET_OF_NORM[i], k))
                    dve.scalar_tensor_tensor(out=h_lo[:, k, :], in0=x_t[:, k, :], scalar=norm_gain(i)[:, k:k + 1],
                                             in1=h_hi[:, k, :].bitcast(F32), op0=ALU.mult, op1=ALU.subtract)\
                        .then_inc(*mark("low", SET_OF_NORM[i], k))

            def tree(i):
                for j, n in enumerate((4, 2, 1)):
                    dve.wait_ge(*(at("square", i, KT - 1) if j == 0 else at("tree", i, j - 1)))
                    dve.tensor_tensor(work[:, 0:n, :], work[:, 0:n, :], work[:, n:2 * n, :], ALU.add)\
                        .then_inc(*mark("tree", i, j))

            def total(i):
                dve.wait_ge(*at("act_read", "sum", i))
                dst = rstd_x if i == 3 else rstd
                dve.reciprocal(dst[:, :], dst[:, :]).then_inc(*mark("rstd", i))
                if i == 3:
                    dve.wait_ge(*at("rstd", i))
                    dve.tensor_tensor(rstd_x[:, :], rstd_x[:, :], rstd[:, :], ALU.mult).then_inc(*mark("rstd_both", 3))

            def rescale(i):
                dve.wait_ge(*at("rstd", i))
                dve.wait_ge(*at("low", SET_OF_NORM[3], KT - 1))
                for k in range(KT):
                    dve.scalar_tensor_tensor(out=x_t[:, k, :], in0=x_t[:, k, :], scalar=col("g_final", k),
                                             in1=rstd[:, :], op0=ALU.mult, op1=ALU.mult).then_inc(*mark("x_new", 3, k))

            def r_cols(i):
                dve.wait_ge(*at("job", "r_cols", i))
                dve.tensor_copy(r_col[:, :], bank("r_cols", i)[:, 0:TT]).then_inc(*mark("dve_read", "r_cols", i))

            def columns(j):
                dve.wait_ge(*at("job", "rows", j))
                o = COL_AT[next(iter(ROWS[j]))]
                n = sum(ROWS[j].values())
                dve.tensor_copy(cols[:, o:o + n], bank("rows", j)[:, 0:n]).then_inc(*mark("dve_read", "rows", j))
                same(("cols", j), ("dve_read", "rows", j))

            def setup():
                columns(0)

            def angles():
                dve.wait_ge(*at("pos_landed", 0))
                dve.wait_ge(*at("const_landed", 0))
                dve.tensor_copy(angle[:, 0, :], pos_i[:, :]).then_inc(*mark("reduce", 0))
                dve.wait_ge(*at("reduce", 0))
                dve.tensor_scalar(angle[:, 4, :], angle[:, 0, :], cst("inv_freq"), None, ALU.mult)\
                    .then_inc(*mark("reduce", 1))
                dve.wait_ge(*at("reduce", 1))
                dve.tensor_scalar(angle[:, 5, :], angle[:, 4, :], float(1 / (2 * np.pi)), MAGIC, ALU.mult, ALU.add)\
                    .then_inc(*mark("reduce", 2))
                dve.wait_ge(*at("reduce", 2))
                dve.tensor_scalar(angle[:, 5, :], angle[:, 5, :], -MAGIC, None, ALU.add).then_inc(*mark("reduce", 3))
                for j, part in enumerate(TWO_PI):
                    dve.wait_ge(*at("reduce", 3 + j))
                    dve.scalar_tensor_tensor(out=angle[:, 4, :], in0=angle[:, 5, :], scalar=-part,
                                             in1=angle[:, 4, :], op0=ALU.mult, op1=ALU.add)\
                        .then_inc(*mark("reduce", 4 + j))
                dve.wait_ge(*at("reduce", 6))
                dve.tensor_scalar(angle[:, 2, :], angle[:, 4, :], PI_BELOW, -PI_BELOW, ALU.min, ALU.max)\
                    .then_inc(*mark("angle", 0))
                dve.scalar_tensor_tensor(out=angle[:, 3, :], in0=angle[:, 4, :], scalar=-1.0, in1=angle[:, 4, :],
                                         op0=ALU.mult, op1=ALU.max).then_inc(*mark("reduce", 7))
                dve.wait_ge(*at("reduce", 7))
                dve.tensor_scalar(angle[:, 3, :], angle[:, 3, :], -1.0, float(np.pi / 2), ALU.mult, ALU.add)\
                    .then_inc(*mark("angle", 1))

            def mask_w_sp():
                dve.wait_ge(*at("more_const_landed", 0))
                for g in range(4):
                    dve.wait_ge(*at("job", "w_sp", 0))
                    dve.tensor_tensor(w_sp_t[:, g, :], bank("w_sp", 0)[:, g * P:(g + 1) * P], cst("upto"), ALU.mult)\
                        .then_inc(*(mark("dve_read", "w_sp", 0) if g == 3 else mark("w_sp_masked", g)))

            def ada_step(p, q):
                r = LOAD_OF[("ada", p, q)]
                dve.wait_ge(*landed(r))
                if q == 0:
                    dve.wait_ge(*at("c_act", 0))
                    if p >= 2:
                        dve.wait_ge(*at("job", "mod", p - 2))
                for kk in range(2):
                    k = 2 * q + kk
                    src = wview(raw, r % RAW_SLOTS, 2)[:, kk, :]
                    if k == 0:
                        ins = dve.tensor_scalar(ada[:, p % 2, :], src, c_act[:, 0:1], None, ALU.mult)
                    else:
                        dve.wait_ge(*(at("ada_added", p, q - 1) if kk == 0 else at("ada_half", p, q)))
                        ins = dve.scalar_tensor_tensor(out=ada[:, p % 2, :], in0=src, scalar=c_act[:, k:k + 1],
                                                       in1=ada[:, p % 2, :], op0=ALU.mult, op1=ALU.add)
                    ins.then_inc(*(mark("ada_added", p, q) if kk else mark("ada_half", p, q)))

            def modulation(p):
                dve.wait_ge(*at("job", "mod", p))
                dve.tensor_tensor(mod[:, KT * p:KT * p + KT], bank("mod", p)[:, 0:KT], col("b_ada", KT * p, KT),
                                  ALU.add).then_inc(*mark("dve_read", "mod", p))

            def gains(n):
                if n == 0:
                    dve.wait_ge(*at("dve_read", "mod", 0))
                    dve.scalar_tensor_tensor(out=gain[:, 0, :], in0=mod[:, 8:16], scalar=1.0, in1=col("g_mix", 0, KT),
                                             op0=ALU.add, op1=ALU.mult).then_inc(*mark("gains", 0))
                elif n == 1:
                    dve.wait_ge(*at("dve_read", "mod", 2))
                    dve.tensor_scalar(gain[:, 2, :], mod[:, 16:24], 1.0, None, ALU.add).then_inc(*mark("gains", 1))
                elif n == 2:
                    dve.wait_ge(*at("dve_read", "mod", 4))
                    dve.scalar_tensor_tensor(out=gain[:, 1, :], in0=mod[:, 32:40], scalar=1.0,
                                             in1=col("g_ffn", 0, KT), op0=ALU.add, op1=ALU.mult)\
                        .then_inc(*mark("gains", 2))
                else:
                    dve.wait_ge(*at("dve_read", "mod", 5))
                    dve.tensor_scalar(gain[:, 3, :], mod[:, 40:48], 1.0, None, ALU.add).then_inc(*mark("gains", 3))
                    dve.wait_ge(*at("gains", 3))

            def root(i):
                dve.wait_ge(*at("act_read", "sum", i))
                dve.reciprocal(rstd[:, :], rstd[:, :]).then_inc(*mark("rstd", i))

            def scaled(i):
                dve.wait_ge(*at("rstd", i))
                dve.wait_ge(*at("gains", 2 * i))
                for k in range(KT + 1):
                    if k < KT:
                        dve.scalar_tensor_tensor(out=y_t[:, k, :], in0=x_t[:, k, :], scalar=gain[:, i, k:k + 1],
                                                 in1=rstd[:, :], op0=ALU.mult, op1=ALU.mult)\
                            .then_inc(*mark("normed", i, k))
                    if k > 0:
                        m = 24 * i + k - 1
                        dve.wait_ge(*at("high", SET_OF_NORM[i], k - 1))
                        dve.scalar_tensor_tensor(out=h_lo[:, k - 1, :], in0=y_t[:, k - 1, :], scalar=mod[:, m:m + 1],
                                                 in1=h_hi[:, k - 1, :].bitcast(F32), op0=ALU.add, op1=ALU.subtract)\
                            .then_inc(*mark("low", SET_OF_NORM[i], k - 1))

            def rope(t):
                dve.wait_ge(*at("job", "rope", t))
                dve.wait_ge(*at("sine", 1))
                if t == 0:
                    dve.wait_ge(*at("square", 0, KT - 1))
                    dve.wait_ge(*at("job", "sum", 0))
                else:
                    dve.wait_ge(*at("roped", t - 1, 2))
                dve.tensor_tensor(work[:, 0, :], cqk[:, t, :], angle[:, 1, :], ALU.mult).then_inc(*mark("roped", t, 0))
                dve.tensor_tensor(work[:, 1, :], bank("rope", t)[:, 0:S], angle[:, 0, :], ALU.mult)\
                    .then_inc(*mark("dve_read", "rope", t))
                dve.wait_ge(*at("dve_read", "rope", t))
                if t < 3:
                    dve.wait_ge(*at("zeroed", 1))
                    dve.tensor_tensor(cqz[0:64, 2 * t, :], work[0:64, 0, :], work[0:64, 1, :], ALU.add)\
                        .then_inc(*mark("roped", t, 1))
                    dve.tensor_tensor(cqz[64:128, 2 * t + 1, :], work[64:128, 0, :], work[64:128, 1, :], ALU.add)\
                        .then_inc(*mark("roped", t, 2))
                else:
                    dve.tensor_tensor(ck_t[:, t - 3, :], work[:, 0, :], work[:, 1, :], ALU.add)\
                        .then_inc(*mark("roped", t, 2))

            def v_norm():
                dve.wait_ge(*at("act_read", "in", IN_V, 1))
                sq = work[:, 2:4, :]
                dve.tensor_tensor(sq, v_tok, v_tok, ALU.mult).then_inc(*mark("v_square", 0))
                dve.wait_ge(*at("v_square", 0))
                dve.tensor_reduce(small[:, 0:8], sq.rearrange("p t (g c) -> p (t g) c", c=HD), AX.X, ALU.add)\
                    .then_inc(*mark("v_sum", 0))
                dve.wait_ge(*at("v_root", 0))
                dve.reciprocal(small[:, 8:16], small[:, 8:16]).then_inc(*mark("v_rstd", 0))
                dve.wait_ge(*at("v_rstd", 0))
                dve.tensor_tensor(v_nrm.rearrange("p t (g c) -> p (t g) c", c=HD),
                                  v_tok.rearrange("p t (g c) -> p (t g) c", c=HD),
                                  small[:, 8:16].rearrange("p (n o) -> p n o", o=1).broadcast_to([P, 8, HD]), ALU.mult)\
                    .then_inc(*mark("v_normed", 0))

            def gate_mix():
                dve.wait_ge(*at("b_sp_landed", 3))
                for m in range(2):
                    dve.wait_ge(*at("job", "gated", m))
                    if m == 0:
                        dve.wait_ge(*at("low", 0, KT - 1))
                        dve.wait_ge(*at("act_read", "in", IN_U, 1))
                    dve.scalar_tensor_tensor(out=blocks3(work[:, 4 + m, :]), in0=blocks3(bank("gated", m)[:, 0:S]),
                                             scalar=col("g_sgu", m),
                                             in1=b_sp_b[:, m:m + 1, :].broadcast_to([P, TT, P]),
                                             op0=ALU.mult, op1=ALU.add).then_inc(*mark("dve_read", "gated", m))
                    dve.wait_ge(*at("dve_read", "gated", m))
                    dve.tensor_tensor(y_t[:, m, :], work[:, 4 + m, :], u_t[:, m, :], ALU.mult)\
                        .then_inc(*mark("full", 1, m))

            def diag(ap):
                return blocks3(ap)[:, 0:3:2, :]

            def before():
                return cst("before").rearrange("p (o c) -> p o c", o=1).broadcast_to([P, 2, P])

            def stick_a(h):
                dve.wait_ge(*at("stick_act", h, 2))
                dve.scalar_tensor_tensor(out=stick(h), in0=bank("stick", h)[:, 0:SP3], scalar=0.0, in1=stick(h),
                                         op0=ALU.max, op1=ALU.add).then_inc(*mark("stick_soft", h))
                dve.wait_ge(*at("stick_soft", h))
                dve.tensor_tensor(diag(stick(h)), diag(stick(h)), before(), ALU.mult).then_inc(*mark("stick_masked", h))

            def stick_b(h):
                dve.wait_ge(*at("act_read", "stick", h))
                dve.scalar_tensor_tensor(out=diag(stick(h)), in0=diag(stick(h)), scalar=1.0, in1=before(),
                                         op0=ALU.min, op1=ALU.mult).then_inc(*mark("stick_weight", h))

            def stick_c(m):
                dve.wait_ge(*at("job", "stick_o", m))
                dve.tensor_copy(y_t[:, 2 + m, :], bank("stick_o", m)[:, 0:S]).then_inc(*mark("dve_read", "stick_o", m))
                same(("full", 1, 2 + m), ("dve_read", "stick_o", m))

            def win_a(h):
                dve.wait_ge(*at("job", "win", h))
                o = CONST_AT["window"][0] + (h // 2) * SP3
                dve.tensor_tensor(win_p(h), bank("win", h)[:, 0:SP3], const[:, o:o + SP3], ALU.add)\
                    .then_inc(*mark("dve_read", "win", h))
                dve.wait_ge(*at("dve_read", "win", h))
                dve.tensor_reduce(small[:, 16 + 2 * h:17 + 2 * h], win_p(h)[:, 0:P], AX.X, ALU.max)\
                    .then_inc(*mark("win_red", h, 0))
                dve.tensor_reduce(small[:, 17 + 2 * h:18 + 2 * h], win_p(h)[:, P:SP3], AX.X, ALU.max)\
                    .then_inc(*mark("win_red", h, 1))
                dve.wait_ge(*at("win_red", h, 1))
                dve.tensor_scalar(small[:, 32 + 2 * h:34 + 2 * h], small[:, 16 + 2 * h:18 + 2 * h], -1.0, None,
                                  ALU.mult).then_inc(*mark("win_max", h))

            def win_b():
                mx, den, rel, top, tmp, tot, fac = (small[:, 16:28], small[:, 48:60], small[:, 64:76],
                                                    small[:, 80:84], small[:, 88:100], small[:, 84:88],
                                                    small[:, 100:112])
                groups = lambda ap: ap.rearrange("p (g x) -> p g x", g=3)
                spread = lambda ap: ap.rearrange("p (o x) -> p o x", o=1).broadcast_to([P, 3, 4])
                dve.tensor_reduce(top, mx.rearrange("p (g x) -> p x g", g=3), AX.X, ALU.max)\
                    .then_inc(*mark("win_mix", 0))
                dve.wait_ge(*at("win_mix", 0))
                dve.tensor_tensor(groups(rel), groups(mx), spread(top), ALU.subtract).then_inc(*mark("win_rel", 0))
                dve.wait_ge(*at("win_factor", 0))
                dve.tensor_tensor(tmp, rel, den, ALU.mult).then_inc(*mark("win_mix", 1))
                dve.wait_ge(*at("win_mix", 1))
                dve.tensor_reduce(tot, tmp.rearrange("p (g x) -> p x g", g=3), AX.X, ALU.add)\
                    .then_inc(*mark("win_mix", 2))
                dve.wait_ge(*at("win_mix", 2))
                dve.reciprocal(tot, tot).then_inc(*mark("win_mix", 3))
                dve.wait_ge(*at("win_mix", 3))
                dve.tensor_tensor(groups(fac), groups(rel), spread(tot), ALU.mult).then_inc(*mark("win_mix", 4))
                dve.wait_ge(*at("win_mix", 4))
                for h in range(6):
                    for q in range(TT):
                        pr = win_p(h)[:, 0:P] if q == 0 else win_p(h)[:, P:SP3]
                        dve.tensor_scalar(pr, pr, small[:, 100 + 2 * h + q:101 + 2 * h + q], None, ALU.mult)\
                            .then_inc(*mark("win_scaled", h, q))

            def win_d(m):
                dve.wait_ge(*at("job", "win_o", m))
                dve.tensor_copy(y_t[:, 5 + m, :], bank("win_o", m)[:, 0:S]).then_inc(*mark("dve_read", "win_o", m))
                same(("full", 1, 5 + m), ("dve_read", "win_o", m))

            def project(kind, n):
                i = NEXT_NORM[kind]
                for m in range(2):
                    k = 2 * n + m
                    dve.wait_ge(*at("job", kind, n, m))
                    if kind == "out":
                        if k == 0:
                            dve.wait_ge(*at("gains", 1))
                        ins = dve.scalar_tensor_tensor(out=x_t[:, k, :], in0=bank(kind, n, m)[:, 0:S],
                                                       scalar=gain[:, 2, k:k + 1], in1=x_t[:, k, :],
                                                       op0=ALU.mult, op1=ALU.add)
                    else:
                        ins = dve.tensor_tensor(x_t[:, k, :], bank(kind, n, m)[:, 0:S], x_t[:, k, :], ALU.add)
                    ins.then_inc(*mark("dve_read", kind, n, m))
                    same(("x_new", i, k), ("dve_read", kind, n, m))

            def ff_up(i):
                if i == 1:
                    dve.memset(aqz, 0.0).then_inc(*mark("gain_qkv", 0))
                    dve.tensor_scalar(small[:, 120:121], col("q_norm"), 0.125, None, ALU.mult)\
                        .then_inc(*mark("gain_qkv", 1))
                    dve.tensor_tensor(gain_qkv[:, :], col("g_final", 0, KT), col("norm_mix", 0, KT), ALU.mult)\
                        .then_inc(*mark("gain_qkv", 2))
                for kind, buf, first in (("gate", ff_g, 0), ("val", ff_v, 22)):
                    for f in range(2):
                        c = bank(kind, i, f)
                        t = first + 2 * i + f
                        dve.wait_ge(*at("ff_newest", kind, i, f))
                        dve.scalar_tensor_tensor(out=buf[:, f, 1:S], in0=c[:, 0:S - 1], scalar=col("conv_w1", t),
                                                 in1=buf[:, f, 1:S], op0=ALU.mult, op1=ALU.add)\
                            .then_inc(*mark("ff_middle", kind, i, f))
                        dve.wait_ge(*at("ff_middle", kind, i, f))
                        dve.scalar_tensor_tensor(out=buf[:, f, 2:S], in0=c[:, 0:S - 2], scalar=col("conv_w0", t),
                                                 in1=buf[:, f, 2:S], op0=ALU.mult, op1=ALU.add)\
                            .then_inc(*mark("dve_read", kind, i, f))
                        if kind == "val":
                            dve.wait_ge(*at("dve_read", "val", i, f))
                            dve.wait_ge(*at("ff_silu", i, f))
                            dve.tensor_tensor(ff_v[:, f, :], ff_v[:, f, :], ff_s[:, f, :], ALU.mult)\
                                .then_inc(*mark("ff_product", i, f))
                for f in range(2):
                    hidden_low(ff_v[:, f, :], i, f, "down", i)

            def hidden_low(full, i, f, *key):
                dve.wait_ge(*at("hidden_hi", *key, f))
                b = 2 * (i % 2) + f
                dve.tensor_tensor(a_lo[:, b, :], full, a_hi[:, b, :].bitcast(F32), ALU.subtract)\
                    .then_inc(*mark("hidden_lo", *key, f))

            def mlp_act(layer, i):
                if (layer, i) == (0, 1):
                    dve.memset(ada[96:128, 0, :], 0.0).then_inc(*mark("w_gate_zero", 0))
                for f in range(2):
                    dve.wait_ge(*at("job", "mlp_in", layer, i, f))
                    if i > 0:
                        dve.wait_ge(*at("hidden_lo", "mlp_out", layer, i - 1, f))
                    else:
                        dve.wait_ge(*at("rstd", 4 + 2 * layer))
                    dve.scalar_tensor_tensor(out=ff_g[:, f, :], in0=bank("mlp_in", layer, i, f)[:, 0:S], scalar=0.0,
                                             in1=rstd[:, :], op0=ALU.max, op1=ALU.mult)\
                        .then_inc(*mark("dve_read", "mlp_in", layer, i, f))
                for f in range(2):
                    dve.wait_ge(*at("dve_read", "mlp_in", layer, i, f))
                    dve.tensor_tensor(ff_s[:, f, :], ff_g[:, f, :], ff_g[:, f, :], ALU.mult)\
                        .then_inc(*mark("relu_squared", layer, i, f))
                for f in range(2):
                    dve.wait_ge(*at("relu_squared", layer, i, f))
                    hidden_low(ff_s[:, f, :], i, f, "mlp_out", layer, i)

            def add_down(*key):
                i = 2 if key[0] == "down" else 5 + 2 * key[1]
                for k in range(KT):
                    acc = psum[4 + k // 2][:, (k % 2) * S:(k % 2 + 1) * S]
                    dve.wait_ge(*at("summed", *key, k | 1))
                    if key[0] == "down":
                        ins = dve.scalar_tensor_tensor(out=x_t[:, k, :], in0=acc, scalar=gain[:, 3, k:k + 1],
                                                       in1=x_t[:, k, :], op0=ALU.mult, op1=ALU.add)
                    else:
                        ins = dve.tensor_tensor(x_t[:, k, :], acc, x_t[:, k, :], ALU.add)
                    ins.then_inc(*mark("x_new", i, k))
                    if k % 2:
                        same(("dve_read", "acc", *key, 4 + k // 2), ("x_new", i, k))

            def q_b(t):
                dve.wait_ge(*at("job", "axial", t))
                if t > 0:
                    dve.wait_ge(*(at("turn", t - 1, 2) if t != 6 else at("k_turned", 1, 1)))
                turn(qx[:, t % 4, :], ("axial", t), 0)
                for n in range(2):
                    r = slice(64 * n, 64 * n + 64)
                    dve.tensor_tensor(aqz[r, 2 * t + n, :], turned[r, 0, :], turned[r, 1, :], ALU.add)\
                        .then_inc(*mark("turn", t, 1 + n))

            def turn(src, job, b):
                dve.tensor_tensor(turned[:, b, :], src, cst("axial_cos"), ALU.mult).then_inc(*mark("turn_cos", *job))
                if job[0] == "axial":
                    t = job[1]
                    dve.tensor_copy(q_mean[:, :, 2 * t:2 * t + 2],
                                    bank(*job)[:, S:S + 4].rearrange("p (t n) -> p t n", t=TT))\
                        .then_inc(*mark("q_mean", t))
                dve.tensor_tensor(turned[:, b + 1, :], bank(*job)[:, 0:S], cst("axial_sin"), ALU.mult)\
                    .then_inc(*mark("dve_read", *job))
                dve.wait_ge(*at("dve_read", *job))

            def k_a(t):
                dve.wait_ge(*at("job", "qkv", 3, t))
                dve.wait_ge(*at("rstd_both", 3))
                dve.tensor_tensor(k_x[:, t, :], bank("qkv", 3, t)[:, 0:S], rstd_x[:, :], ALU.mult)\
                    .then_inc(*mark("dve_read", "qkv", 3, t))
                same(("k_scaled", t), ("dve_read", "qkv", 3, t))

            def k_b(t):
                dve.wait_ge(*at("act_read", "k_mean", t))
                dve.reciprocal(k_rms[:, t, :], k_rms[:, t, :]).then_inc(*mark("k_rstd", t))
                dve.wait_ge(*at("k_rstd", t))
                dve.scalar_tensor_tensor(out=k_x[:, t, :], in0=k_x[:, t, :], scalar=col("k_norm"),
                                         in1=k_rms[:, t, :], op0=ALU.mult, op1=ALU.mult).then_inc(*mark("k_normed", t))

            def k_c(t):
                dve.wait_ge(*at("job", "k_axial", t))
                dve.wait_ge(*(at("turn", 5, 2) if t == 0 else at("k_turned", 0, 1)))
                turn(k_x[:, t, :], ("k_axial", t), 0)
                for n in range(2):
                    r = slice(64 * n, 64 * n + 64)
                    dve.tensor_tensor(ak_dup[r, 2 * t + n, :], turned[r, 0, :], turned[r, 1, :], ALU.add)\
                        .then_inc(*mark("k_turned", t, n))

            def q_scale(a, b):
                dve.wait_ge(*at("q_mean", b // 2 - 1))
                dve.wait_ge(*at("dve_read", "r_cols", 3))
                for t in range(TT):
                    dve.tensor_scalar(q_mean[:, t, a:b], q_mean[:, t, a:b], r_col[:, t:t + 1], r_col[:, t:t + 1],
                                      ALU.mult, ALU.mult).then_inc(*(mark("q_means", a) if t else mark("q_mean_0", a)))
                dve.wait_ge(*at("q_rms", a))
                dve.reciprocal(q_mean[:, :, a:b], q_mean[:, :, a:b]).then_inc(*mark("q_rstd", a))
                dve.wait_ge(*at("q_rstd", a))
                for t in range(TT):
                    dve.tensor_scalar(q_mean[:, t, a:b], q_mean[:, t, a:b], r_col[:, t:t + 1], None, ALU.mult)\
                        .then_inc(*mark("q_factor", a, t))
                dve.wait_ge(*at("q_factor", a, 1))

            def att_a(h):
                o = 8 * (h % 3)
                dve.wait_ge(*at("job", "att", h))
                if h >= 3:
                    dve.wait_ge(*at("act_read", "att", h - 3))
                dve.tensor_reduce(small[:, o:o + 2], bank("att", h)[:, :].rearrange("p (q s) -> p q s", q=TT),
                                  AX.X, ALU.max).then_inc(*mark("att_red", h))
                dve.wait_ge(*at("att_red", h))
                dve.scalar_tensor_tensor(out=small[:, o + 2:o + 4], in0=small[:, o:o + 2], scalar=-1.0,
                                         in1=q_mean[:, :, h], op0=ALU.mult, op1=ALU.mult).then_inc(*mark("att_max", h))

            def att_scale(h):
                o = 8 * (h % 3)
                dve.wait_ge(*at("act_read", "att", h))
                dve.reciprocal(small[:, o + 6:o + 8], small[:, o + 4:o + 6]).then_inc(*mark("att_rden", h))
                dve.wait_ge(*at("att_rden", h))
                for q in range(TT):
                    pr = att_p[:, h % 3, q, :]
                    dve.tensor_scalar(pr, pr, small[:, o + 6 + q:o + 7 + q], None, ALU.mult)\
                        .then_inc(*mark("att_scaled", h, q))

            def att_c(m):
                dve.wait_ge(*at("job", "att_o", m))
                dve.tensor_copy(y_t[:, m, :], bank("att_o", m)[:, 0:S]).then_inc(*mark("dve_read", "att_o", m))
                same(("full", 4, m), ("dve_read", "att_o", m))

            def gla_in(n):
                for m in range(1 if n == 0 else 2):
                    if 5 <= n < 9:
                        continue
                    job = ("gla", n, m)
                    dve.wait_ge(*at("job", *job))
                    if n == 0:
                        dve.wait_ge(*at("rstd", 5))
                        ins = dve.tensor_tensor(z_t[96:128, 0, :], bank(*job)[96:128, 0:S], rstd[96:128, :], ALU.mult)
                    elif n < 3:
                        ins = dve.scalar_tensor_tensor(out=gq[:, 2 * (n - 1) + m, :], in0=bank(*job)[:, 0:S],
                                                       scalar=float(P) ** -0.5, in1=rstd[:, :],
                                                       op0=ALU.mult, op1=ALU.mult)
                    else:
                        dst = gk[:, 2 * (n - 3) + m, :] if n < 5 else gr[:, 2 * (n - 9) + m, :]
                        ins = dve.tensor_tensor(dst, bank(*job)[:, 0:S], rstd[:, :], ALU.mult)
                    ins.then_inc(*mark("dve_read", *job))

            def gate(h):
                dve.wait_ge(*at("gate_abs", h, 1))
                for n in range(2):
                    dve.tensor_scalar(work[:, 2 + n, :], bank("logit", h)[:, n * S:(n + 1) * S],
                                      col("b_gate", 4 * n + h), 0.0, ALU.add, ALU.min)\
                        .then_inc(*mark("gate_min", h, n))
                dve.wait_ge(*at("gate_min", h, 1))
                dve.wait_ge(*at("gate_ln", h))
                dve.tensor_tensor(work[:, 2:4, :], work[:, 2:4, :], work[:, 0:2, :], ALU.subtract)\
                    .then_inc(*mark("dve_read", "logit", h))
                dve.wait_ge(*at("dve_read", "logit", h))
                if h > 0:
                    dve.wait_ge(*at("gate_mid", h - 1))
                dve.tensor_tensor_scan(work[:, 4, :], cst("scan_fwd"), work[:, 2, :], 0.0, ALU.mult, ALU.add)\
                    .then_inc(*mark("gate_sum", h, 0))
                dve.tensor_tensor_scan(work[:, 5, ::-1], cst("scan_bwd")[:, ::-1], work[:, 3, ::-1], 0.0,
                                       ALU.mult, ALU.add).then_inc(*mark("gate_sum", h, 1))
                dve.wait_ge(*at("gate_sum", h, 1))
                if h > 0:
                    dve.wait_ge(*at("decay", h - 1, 1))
                sums = work[:, 4:6, :].rearrange("p n (t c) -> p (n t) c", c=P)
                dve.tensor_tensor(work[:, 6:8, :].rearrange("p n (t c) -> p (n t) c", c=P), sums,
                                  sums[:, :, HD - 1:HD].broadcast_to([P, 2 * TT, P]), ALU.subtract)\
                    .then_inc(*mark("gate_rel", h))

            def keys(h):
                dve.wait_ge(*at("decay", h, 1))
                dve.wait_ge(*at("dve_read", "gla", 4, 1))
                dve.tensor_copy(small[:, 32 + 2 * h:33 + 2 * h], qe[:, h, 0, P - 1:P]).then_inc(*mark("border", h, 0))
                dve.tensor_copy(small[:, 33 + 2 * h:34 + 2 * h], qe[:, h, 1, P:P + 1]).then_inc(*mark("border", h, 1))
                dve.wait_ge(*at("border", h, 1))
                for n in range(2):
                    dve.tensor_tensor(qe[:, h, n, :], qe[:, h, n, :], gq[:, h, :], ALU.mult)\
                        .then_inc(*mark("decayed", h, 0, n))
                    dve.tensor_tensor(ke[:, h, n, :], ke[:, h, n, :], gk[:, h, :], ALU.mult)\
                        .then_inc(*mark("decayed", h, 1, n))
                dve.wait_ge(*at("decayed", h, 1, 1))
                for n in range(2):
                    qt, kt = (1, 0) if n == 0 else (0, 1)
                    c = 4 * h + 2 * n + qt
                    dve.tensor_scalar(gq[:, h, n * P:n * P + P], qe[:, h, n, qt * P:qt * P + P], small[:, c:c + 1],
                                      None, ALU.mult).then_inc(*mark("across", h, 0, n))
                    dve.tensor_scalar(gk[:, h, n * P:n * P + P], ke[:, h, n, kt * P:kt * P + P],
                                      small[:, 32 + 2 * h + n:33 + 2 * h + n], None, ALU.mult)\
                        .then_inc(*mark("across", h, 1, n))

            def mix(h):
                dst = pair[:, h % 2, :, :].rearrange("p t s -> p (t s)").rearrange("p (n c) -> p n c", c=P)[:, 0:4:3, :]
                dve.wait_ge(*at("act_read", "pair_fwd", h))
                dve.wait_ge(*at("job", "pair_bwd", h))
                dve.copy_predicated(dst, blocks3(cst("after").bitcast(mybir.dt.uint32)),
                                    blocks3(bank("pair_bwd", h)[:, 0:S])).then_inc(*mark("dve_read", "pair_bwd", h))
                dve.wait_ge(*at("dve_read", "pair_bwd", h))
                dve.tensor_tensor(dst, dst, blocks3(cst("twice")), ALU.mult).then_inc(*mark("paired", h))

            def mixed(h):
                for m in range(2):
                    dve.wait_ge(*at("gla_square", h, m))
                    dve.tensor_scalar(y_t[:, 2 * h + m, :], bank("gla_o", h, m)[:, 0:S], col("out_norm", m), None,
                                      ALU.mult).then_inc(*mark("dve_read", "gla_o", h, m))

            def head_norm(h):
                dve.wait_ge(*at("act_read", "gla_sum", h))
                dve.reciprocal(work[:, h, :], work[:, h, :]).then_inc(*mark("gla_rstd", h))
                dve.wait_ge(*at("gla_rstd", h))
                for j in (2 * h, 2 * h + 1):
                    dve.wait_ge(*at("dve_read", "gla_o", h, 1))
                    dve.tensor_tensor(y_t[:, j, :], y_t[:, j, :], work[:, h, :], ALU.mult)\
                        .then_inc(*mark("head_normed", j))

            def head_gate(j):
                dve.wait_ge(*at("gla_gate", j))
                dve.wait_ge(*at("head_normed", j))
                dve.tensor_tensor(y_t[:, j, :], y_t[:, j, :], gr[:, j, :], ALU.mult).then_inc(*mark("full", 7, j))

            def finish():
                dve.wait_ge(*at("last_square", TT - 1, 1))
                dve.tensor_tensor(small[:, 68:70], small[:, 64:66], small[:, 66:68], ALU.add)\
                    .then_inc(*mark("last_sum", 0))
                dve.wait_ge(*at("last_root", 0))
                dve.reciprocal(small[:, 72:74], small[:, 70:72]).then_inc(*mark("last_rstd", 0))
                dve.wait_ge(*at("last_rstd", 0))
                dve.wait_ge(*at("g_last_landed", 0))
                dve.wait_ge(*at("w_lo", len(SPLITS) - 1))
                for t in range(TT):
                    for half in range(2):
                        r = slice(512 * half, 512 * half + 512)
                        dve.scalar_tensor_tensor(out=y_rows[:, t, r], in0=bank("turned", t, half)[:, :],
                                                 scalar=small[:, 72 + t:73 + t], in1=g_last[:, r],
                                                 op0=ALU.mult, op1=ALU.mult).then_inc(*mark("y_rows", t, half))

            steps = {"setup": setup, "rows": columns, "angles": angles, "w_sp": mask_w_sp, "ada": ada_step,
                     "mod": modulation, "gains": gains, "root": root, "scaled": scaled, "rope": rope,
                     "v_norm": v_norm, "gate_mix": gate_mix, "stick_a": stick_a, "stick_b": stick_b,
                     "stick_c": stick_c, "win_a": win_a, "win_b": win_b, "win_d": win_d,
                     "split": split, "split_lo": split,
                     "unscaled": unscaled, "tree": tree, "total": total, "rescale": rescale, "r_cols": r_cols,
                     "project": project, "ff_up": ff_up, "mlp_act": mlp_act, "add_down": add_down, "q_b": q_b,
                     "k_a": k_a, "k_b": k_b, "k_c": k_c, "q_scale": q_scale, "att_a": att_a, "att_scale": att_scale,
                     "att_c": att_c, "gla_in": gla_in, "gate": gate, "keys": keys, "mix": mix,
                     "mixed": mixed, "head_norm": head_norm, "head_gate": head_gate, "finish": finish}
            for step in schedule():
                if step[0] in steps:
                    steps[step[0]](*step[1:])

        @block.tensor
        def _(pe):
            seen = set()

            def operand(idx, k):
                if (idx, k) not in seen:
                    seen.add((idx, k))
                    pe.wait_ge(*at("low", idx, k))

            def weights(key):
                n = SPLIT_OF[key]
                pe.wait_ge(*at("w_lo", n))
                return n % SPLIT_SLOTS

            def used(key, event):
                same(("chunk_used", SPLIT_OF[key]), event)

            def three(dst, lhs, rhs, start, stop):
                pe.matmul(dst, lhs[0], rhs[0], start=start, stop=False, skip_group_check=True)
                pe.matmul(dst, lhs[0], rhs[1], start=False, stop=False, skip_group_check=True)
                return pe.matmul(dst, lhs[1], rhs[0], start=False, stop=stop, skip_group_check=True)

            def feature_tile(idx, key, m):
                slot = weights(key)
                dst = take(pe, *key, m)[:, 0:S]
                for k in range(KT):
                    operand(idx, k)
                    w = [wview(b, slot, KT)[:, k, m * P:m * P + P] for b in (w_hi, w_lo)]
                    ins = three(dst, w, (h_hi[:, k, :], h_lo[:, k, :]), k == 0, k == KT - 1)
                ins.then_inc(*mark("job", *key, m))

            def token_tile(idx, key, t):
                slot = weights(key)
                dst = take(pe, *key, t)[:, 0:S]
                for k in range(KT):
                    operand(idx, k)
                    h = [b[:, k, t * P:t * P + P] for b in (h_hi, h_lo)]
                    w = [wview(b, slot, KT)[:, k, :] for b in (w_hi, w_lo)]
                    ins = three(dst, h, w, k == 0, k == KT - 1)
                ins.then_inc(*mark("job", *key, t))

            def project_chunk(idx, key, tile=feature_tile, n=2):
                if key in FIRST_USE and tile is feature_tile and n == 2:
                    slot = weights(key)
                    dst = [take(pe, *key, m)[:, 0:S] for m in range(n)]
                    for k in range(KT):
                        operand(idx, k)
                        for m in range(n):
                            w = [wview(b, slot, KT)[:, k, m * P:m * P + P] for b in (w_hi, w_lo)]
                            ins = three(dst[m], w, (h_hi[:, k, :], h_lo[:, k, :]), k == 0, k == KT - 1)
                            if k == KT - 1:
                                ins.then_inc(*mark("job", *key, m))
                else:
                    for m in range(n):
                        tile(idx, key, m)
                used(key, ("job", *key, n - 1))

            def turn_rows(j):
                n = sum(ROWS[j].values())
                last = list(ROWS[j])[-1]
                pe.wait_ge(*(at(f"rows{j}_landed", last, 1) if last == "k_norm" else at(f"rows{j}_landed", last)))
                pe.transpose(take(pe, "rows", j)[:, 0:n], rows[0:n, j, :], cst("ident")[0:n, 0:n])\
                    .then_inc(*mark("job", "rows", j))

            def setup():
                pe.wait_ge(*at("const_landed", 0))
                turn_rows(0)

            def turn_x():
                pe.wait_ge(*at("x_landed", 0))
                for j in range(4):
                    dst = take(pe, "x", j)
                    for kk in range(2):
                        for t in range(TT):
                            k = 2 * j + kk
                            ins = pe.transpose(dst[:, kk * S + t * P:kk * S + t * P + P],
                                               x_rows[:, t, k * P:k * P + P], cst("ident"))
                    ins.then_inc(*mark("job", "x", j))

            def turn_w_sp():
                pe.wait_ge(*at("w_sp_landed", 0))
                dst = take(pe, "w_sp", 0)
                for g in range(4):
                    ins = pe.transpose(dst[:, g * P:(g + 1) * P], w_sp_r[:, g, :], cst("ident"))
                ins.then_inc(*mark("job", "w_sp", 0))

            def modulation(p):
                pe.wait_ge(*at("ada_added", p, 3))
                dst = take(pe, "mod", p)
                for k in range(KT):
                    ins = pe.matmul(dst[:, k:k + 1], ada[:, p % 2, k * P:(k + 1) * P], cst("ones")[:, 0:1],
                                    start=True, stop=True)
                ins.then_inc(*mark("job", "mod", p))

            def root(i):
                dst = take(pe, "sum", i)[:, 0:S]
                for k in range(KT):
                    pe.wait_ge(*at("square", i, k))
                    ins = pe.matmul(dst, cst("ones"), work[:, k, :], start=(k == 0), stop=(k == KT - 1))
                ins.then_inc(*mark("job", "sum", i))

            def take_in(n):
                project_chunk(0, ("in", n), token_tile if n >= IN_V else feature_tile)

            def rope(t):
                pe.wait_ge(*at("act_read", "in", t // 2, t % 2))
                pe.matmul(take(pe, "rope", t)[:, 0:S], cst("rope_swap"), cqk[:, t, :], start=True, stop=True)\
                    .then_inc(*mark("job", "rope", t))

            def gate_mix():
                pe.wait_ge(*at("v_normed", 0))
                pe.wait_ge(*at("dve_read", "w_sp", 0))
                for m in range(2):
                    dst = take(pe, "gated", m)
                    for g in range(2):
                        for t in range(TT):
                            f = (2 * m + g) * HD
                            ins = pe.matmul(dst[64 * g:64 * g + 64, t * P:t * P + P], v_nrm[:, t, f:f + HD],
                                            w_sp_t[:, 2 * m + g, :], start=True, stop=True, skip_group_check=True)
                    ins.then_inc(*mark("job", "gated", m))

            def stick_a(h):
                pe.wait_ge(*at("act_read", "in", 5, 1))
                dst = take(pe, "stick", h)
                k = bk_t[:, h // 2, :]
                pe.matmul(dst[:, 0:S], k[:, 0:P], bqz[:, h, :], start=True, stop=False, skip_group_check=True)
                pe.matmul(dst[:, S:SP3], k[:, P:S], bqz[:, h, P:S], start=False, stop=False, skip_group_check=True)\
                    .then_inc(*mark("job", "stick", h))

            def stick_b(h):
                pe.wait_ge(*at("stick_masked", h))
                s, dst = stick(h), bank("stick", h)
                pe.matmul(dst[:, 0:S], cst("tail"), s[:, 0:S], start=False, stop=False, skip_group_check=True)
                pe.matmul(dst[:, P:S], cst("tail_all"), s[:, S:SP3], start=False, stop=False, skip_group_check=True)
                pe.matmul(dst[:, S:SP3], cst("tail"), s[:, S:SP3], start=False, stop=True, skip_group_check=True)\
                    .then_inc(*mark("stick_tail", h))

            def values_out(dst, h, column, prob):
                o = 64 * (h % 2)
                pe.matmul(dst[o:o + 64, 0:S], vals[:, 0, column:column + HD], prob[:, 0:S], start=True, stop=False,
                          skip_group_check=True)
                return pe.matmul(dst[o:o + 64, P:S], vals[:, 1, column:column + HD], prob[:, S:SP3], start=False,
                                 stop=True, skip_group_check=True)

            def stick_c(m):
                dst = take(pe, "stick_o", m)
                for h in (2 * m, 2 * m + 1):
                    pe.wait_ge(*at("stick_weight", h))
                    pe.wait_ge(*at("act_read", "in", 10, 1))
                    ins = values_out(dst, h, h * HD, stick(h))
                ins.then_inc(*mark("job", "stick_o", m))

            def win_a(h):
                if h == 0:
                    pe.wait_ge(*at("roped", 5, 2))
                dst = take(pe, "win", h)
                pe.matmul(dst[:, 0:P], cqz[:, h, 0:P], ck_t[:, h // 2, 0:P], start=True, stop=True,
                          skip_group_check=True)
                pe.matmul(dst[:, P:SP3], cqz[:, h, P:S], ck_t[:, h // 2, :], start=True, stop=True,
                          skip_group_check=True).then_inc(*mark("job", "win", h))

            def win_c(h):
                pe.wait_ge(*at("win_scaled", h, 1))
                dst = take(pe, "win_t", h)
                for n in range(3):
                    ins = pe.transpose(dst[:, n * P:(n + 1) * P], win_p(h)[:, n * P:(n + 1) * P], cst("ident"))
                ins.then_inc(*mark("job", "win_t", h))

            def win_d(m):
                dst = take(pe, "win_o", m)
                for h in (2 * m, 2 * m + 1):
                    pe.wait_ge(*at("act_read", "win_t", h))
                    ins = values_out(dst, h, 6 * HD + h * HD, win_pt(h))
                ins.then_inc(*mark("job", "win_o", m))

            def project(kind, n):
                project_chunk(USES[kind], (kind, n))

            def ff_up(i):
                if i == 0:
                    ring["set"] = range(4)
                project_chunk(2, ("gate", i))
                project_chunk(2, ("val", i))

            def mlp_up(layer, i):
                if i == 0:
                    ring["set"] = range(4)
                project_chunk(5 + 3 * layer, ("mlp_in", layer, i))

            def down(*key):
                i = key[-1]
                last = i == (FF_STEPS if key[0] == "down" else MLP_STEPS) - 1
                slot = weights(key)
                for f in range(2):
                    pe.wait_ge(*at("hidden_lo", *key, f))
                for k in range(KT):
                    b = 4 + k // 2
                    if i == 0 and k % 2 == 0 and b in ring["last"]:
                        pe.wait_ge(*evacuated(*ring["last"][b]))
                    dst = psum[b][:, (k % 2) * S:(k % 2 + 1) * S]
                    for f in range(2):
                        w = [wview(x, slot, 2)[:, f, k * P:k * P + P] for x in (w_hi, w_lo)]
                        n = 2 * (i % 2) + f
                        ins = three(dst, w, (a_hi[:, n, :], a_lo[:, n, :]), i == 0 and k % 2 == 0 and f == 0,
                                    last and f == 1)
                    if last:
                        ins.then_inc(*mark("summed", *key[:-1], k))
                    elif k == KT - 1:
                        ins.then_inc(*mark("added", *key))
                used(key, ("summed", *key[:-1], KT - 1) if last else ("added", *key))

            def add_down(*key):
                for b in range(4, 8):
                    ring["last"][b] = ("acc", *key, b)
                ring["set"] = range(8)

            def qkv(n):
                project_chunk(3, ("qkv", n), token_tile if n == 4 else feature_tile)

            def total(i):
                pe.wait_ge(*at("tree", i, 2))
                pe.matmul(take(pe, "sum", i)[:, 0:S], cst("ones"), work[:, 0, :], start=True, stop=True)\
                    .then_inc(*mark("job", "sum", i))

            def r_cols(i):
                pe.wait_ge(*(at("rstd_both", 3) if i == 3 else at("rstd", i)))
                dst, src = take(pe, "r_cols", i), (rstd_x if i == 3 else rstd)
                for t in range(TT):
                    ins = pe.matmul(dst[:, t:t + 1], src[0:1, t * P:t * P + P], cst("one")[0:1, 0:1], start=True,
                                    stop=True)
                ins.then_inc(*mark("job", "r_cols", i))

            def q_b(t):
                dst = take(pe, "axial", t)
                pe.wait_ge(*at("act_read", "qkv", Q_CHUNK[t], t % 2))
                pe.matmul(dst[:, 0:S], cst("axial_swap"), qx[:, t % 4, :], start=True, stop=True,
                          skip_group_check=True)
                for n in range(TT):
                    ins = pe.matmul(dst[:, S + 2 * n:S + 2 * n + 2], q_sq[:, t % 2, n * P:n * P + P],
                                    cst("head_pick"), start=True, stop=True, skip_group_check=True)
                ins.then_inc(*mark("job", "axial", t))

            def k_b(t):
                pe.wait_ge(*at("k_square", t))
                pe.matmul(take(pe, "k_mean", t)[:, 0:S], cst("head_mean"), q_sq[:, t, :], start=True, stop=True)\
                    .then_inc(*mark("job", "k_mean", t))

            def k_c(t):
                pe.wait_ge(*at("k_normed", t))
                pe.matmul(take(pe, "k_axial", t)[:, 0:S], cst("axial_swap"), k_x[:, t, :], start=True, stop=True)\
                    .then_inc(*mark("job", "k_axial", t))

            def att_a(h):
                pe.wait_ge(*at("turn", h // 2, 2))
                if h % 4 == 0:
                    pe.wait_ge(*at(f"k_doubled{h // 4}", 0))
                dst = take(pe, "att", h)
                for q in range(TT):
                    ins = pe.matmul(dst[:, q * S:(q + 1) * S], aqz[:, h, q * P:q * P + P], ak_dup[:, h // 4, :],
                                    start=True, stop=True, skip_group_check=True)
                ins.then_inc(*mark("job", "att", h))

            def att_b(h):
                pe.wait_ge(*at("att_scaled", h, 1))
                dst = take(pe, "att_t", h)
                for q in range(TT):
                    for k in range(TT):
                        ins = pe.transpose(dst[:, k * S + q * P:k * S + q * P + P],
                                           att_p[:, h % 3, q, k * P:k * P + P], cst("ident"))
                ins.then_inc(*mark("job", "att_t", h))

            def att_o(h):
                pe.wait_ge(*at("act_read", "att_t", h))
                m = h // 2
                dst = take(pe, "att_o", m) if h % 2 == 0 else psum[banks[("att_o", m)]]
                o = 64 * (h % 2)
                g = h // 4
                for k in range(TT):
                    ins = pe.matmul(dst[o:o + 64, 0:S], v2[:, k, g * HD:g * HD + HD], att_pt[:, h % 2, k, :],
                                    start=(k == 0), stop=(k == TT - 1), skip_group_check=True)
                if h % 2:
                    ins.then_inc(*mark("job", "att_o", m))
                    same(("att_pv", h), ("job", "att_o", m))
                else:
                    ins.then_inc(*mark("att_pv", h))

            def gla(n):
                if n == 0:
                    project_chunk(6, ("gla", 0), n=1)
                else:
                    project_chunk(6, ("gla", n), token_tile if 5 <= n < 9 else feature_tile)

            def logit(h):
                if h == 0:
                    pe.wait_ge(*at("w_gate_landed", 1))
                    pe.wait_ge(*at("dve_read", "gla", 0, 0))
                dst = take(pe, "logit", h)
                for n in range(2):
                    ins = pe.matmul(dst[:, n * S:(n + 1) * S], w_gate[:, n, h * P:h * P + P], z_t[96:128, 0, :],
                                    start=True, stop=True, skip_group_check=True)
                ins.then_inc(*mark("job", "logit", h))

            def mix(h):
                pe.wait_ge(*at("across", h, 1, 1))
                fwd = take(pe, "pair_fwd", h)
                for c, k, q in ((0, ke[:, h, 0, 0:P], qe[:, h, 0, 0:P]), (1, gk[:, h, 0:P], gq[:, h, 0:P]),
                                (2, gk[:, h, P:S], gq[:, h, P:S]), (3, ke[:, h, 0, P:S], qe[:, h, 0, P:S])):
                    ins = pe.matmul(fwd[:, c * P:c * P + P], k, q, start=True, stop=True, skip_group_check=True)
                ins.then_inc(*mark("job", "pair_fwd", h))
                bwd = take(pe, "pair_bwd", h)
                for t in range(TT):
                    ins = pe.matmul(bwd[:, t * P:t * P + P], ke[:, h, 1, t * P:t * P + P],
                                    qe[:, h, 1, t * P:t * P + P], start=True, stop=True, skip_group_check=True)
                ins.then_inc(*mark("job", "pair_bwd", h))

            def mixed(h):
                pe.wait_ge(*at("paired", h))
                pe.wait_ge(*at("act_read", "gla", 8, 1))
                for m in range(2):
                    dst = take(pe, "gla_o", h, m)
                    for t in range(TT):
                        ins = pe.matmul(dst[:, 0:S], gv[:, t, h * S + m * P:h * S + m * P + P],
                                        pair[:, h % 2, t, :], start=(t == 0), stop=(t == TT - 1))
                    ins.then_inc(*mark("job", "gla_o", h, m))

            def head_sum(h):
                dst = take(pe, "gla_sum", h)[:, 0:S]
                for m in range(2):
                    pe.wait_ge(*at("gla_square", h, m))
                    ins = pe.matmul(dst, cst("ones"), gla_sq[:, 2 * (h % 2) + m, :], start=(m == 0), stop=(m == 1))
                ins.then_inc(*mark("job", "gla_sum", h))

            def finish():
                for half in range(2):
                    for t in range(TT):
                        dst = take(pe, "turned", t, half)
                        for n in range(4):
                            k = 4 * half + n
                            pe.wait_ge(*at("x_new", 7, k))
                            ins = pe.transpose(dst[:, n * P:n * P + P], x_t[:, k, t * P:t * P + P], cst("ident"))
                        ins.then_inc(*mark("job", "turned", t, half))

            steps = {"setup": setup, "rows": turn_rows, "turn_x": turn_x, "w_sp": turn_w_sp, "mod": modulation,
                     "root": root, "in": take_in, "rope": rope,
                     "gate_mix": gate_mix, "stick_a": stick_a, "stick_b": stick_b, "stick_c": stick_c,
                     "win_a": win_a, "win_c": win_c, "win_d": win_d, "project": project, "ff_up": ff_up,
                     "mlp_up": mlp_up, "down": down, "add_down": add_down, "qkv": qkv, "q_b": q_b, "k_b": k_b,
                     "k_c": k_c, "total": total, "r_cols": r_cols, "att_a": att_a, "att_b": att_b, "att_o": att_o,
                     "gla": gla, "logit": logit, "mix": mix, "mixed": mixed, "head_sum": head_sum,
                     "finish": finish}
            for step in schedule():
                if step[0] in steps:
                    steps[step[0]](*step[1:])
    return marks, banks


_INS = ['x', 'c', 'positions', 'w_ada', 'b_ada', 'g_mix', 'w_in', 'g_sgu', 'w_sp', 'b_sp', 'w_out', 'g_ffn', 'w_up',
        'conv_w', 'conv_b', 'w_down', 'g_final', 'norm_mix_2', 'norm_mlp_2', 'attn_w_qkv_2', 'attn_q_norm_2',
        'attn_k_norm_2', 'attn_w_o_2', 'gla_w_in_2', 'gla_w_gate_up_2', 'gla_b_gate_2', 'gla_out_norm_2',
        'gla_w_o_2', 'mlp_w_in_2', 'mlp_w_out_2', 'final_norm_2']


def kernel(**inputs):
    import concourse.bacc as _bacc
    from concourse.bass_utils import run_bass_kernel_spmd as _run

    arrays = {f"in_{name}_dram": np.ascontiguousarray(inputs[name]) for name in _INS}
    arrays["in_const_dram"] = constants()
    known = None
    for _ in range(2):
        nc = _bacc.Bacc("TRN2", target_bir_lowering=False, num_devices=1)
        a = {name[3:-5]: nc.dram_tensor(name, v.shape, mybir.dt.from_np(v.dtype), kind="ExternalInput").ap()
             for name, v in arrays.items()}
        out = nc.dram_tensor("out_0_dram", (1, S, D), F32, kind="ExternalOutput").ap()
        known = build(nc, a, out, known)
    r = _run(nc, [arrays], core_ids=[0])
    return r.results[0]["out_0_dram"]
```
